# Optimizing a Trainium2 kernel written in Bass

```python
import math
import jax, jax.numpy as jnp
from jax import lax
import numpy as np

"""Hybrid decoder trunk, interleaved token mixers + PEER channel mixer.

Layer i uses token mixer (i mod 2): 0 = gated linear attention (GLA, chunked),
1 = differential softmax attention with partial rotary. Every layer is followed
by a product-key expert retrieval (PEER) channel mixer. Pre-RMSNorm before each
sub-layer, plain residual adds, one final RMSNorm.

Inputs : x (BATCH, SEQ, D_MODEL) float32, positions (BATCH, SEQ) int32, weights.
Output : (BATCH, SEQ, D_MODEL).
"""

D_MODEL = 1024
BATCH = 1
SEQ = 256
DEPTH = 2

N_MIXERS = 2
N_GLA_LAYERS = (DEPTH + 1) // 2
N_DIFF_LAYERS = DEPTH // 2
RMS_EPS = 1e-6

GLA_HEADS = 4
GLA_DK = D_MODEL // 2 // GLA_HEADS
GLA_DV = D_MODEL // GLA_HEADS
GLA_GATE_RANK = 16
GLA_TAU = 16.0
GLA_CHUNK = 64
GLA_QK = GLA_HEADS * GLA_DK
GLA_V = GLA_HEADS * GLA_DV
GLA_IN = 2 * GLA_QK + 2 * GLA_V + GLA_GATE_RANK

DIFF_HEADS = D_MODEL // 128
DIFF_DH = 64
DIFF_DV = 2 * DIFF_DH
DIFF_QK = 2 * DIFF_HEADS * DIFF_DH
DIFF_VW = DIFF_HEADS * DIFF_DV
DIFF_IN = 2 * DIFF_QK + DIFF_VW
ROPE_DIMS = DIFF_DH // 4
ROPE_THETA = 500000.0
Q_BLOCK = 128

PEER_HEADS = 8
PEER_NKEYS = 128
PEER_N_EXPERTS = PEER_NKEYS * PEER_NKEYS
PEER_DKEY = 128
PEER_TOPK = 16
PEER_TOKEN_BLOCK = 128

kernel_name = "hybrid_gla_diffattn_peer"

def rmsnorm(x, g):
    xf = x.astype(jnp.float32)
    y = xf * lax.rsqrt(jnp.mean(xf * xf, axis=-1, keepdims=True) + RMS_EPS)
    return (y * g.astype(jnp.float32)).astype(x.dtype)

def gla_mixer(h, w_in, w_gate_up, b_gate, g_norm, w_out):
    B, S, _ = h.shape
    nC = S // GLA_CHUNK
    proj = h @ w_in
    q, k, v, r, glr = jnp.split(
        proj, [GLA_QK, 2 * GLA_QK, 2 * GLA_QK + GLA_V, 2 * GLA_QK + 2 * GLA_V], axis=-1)
    glog = jax.nn.log_sigmoid((glr @ w_gate_up + b_gate).astype(jnp.float32)) / GLA_TAU

    def heads(t, d):
        return t.reshape(B, nC, GLA_CHUNK, GLA_HEADS, d).transpose(0, 3, 1, 2, 4)

    q = heads(q, GLA_DK) * (GLA_DK ** -0.5)
    k = heads(k, GLA_DK)
    v = heads(v, GLA_DV)
    cum = jnp.cumsum(heads(glog, GLA_DK), axis=3)
    last = cum[:, :, :, -1:, :]
    mid = cum[:, :, :, GLA_CHUNK // 2 - 1:GLA_CHUNK // 2, :]

    a = jnp.einsum('bhncd,bhnjd->bhncj', q * jnp.exp(cum - mid), k * jnp.exp(mid - cum))
    causal = jnp.tril(jnp.ones((GLA_CHUNK, GLA_CHUNK), dtype=bool))
    a = jnp.where(causal, a, 0.0)
    o_intra = jnp.einsum('bhncj,bhnjv->bhncv', a, v)

    kv = jnp.einsum('bhncd,bhncv->nbhdv', k * jnp.exp(last - cum), v)
    chunk_decay = jnp.exp(last[:, :, :, 0, :]).transpose(2, 0, 1, 3)

    def step(state, inp):
        dec, kv_c = inp
        return dec[..., None] * state + kv_c, state

    init = jnp.zeros((B, GLA_HEADS, GLA_DK, GLA_DV), kv.dtype)
    _, states = lax.scan(step, init, (chunk_decay, kv))
    o_inter = jnp.einsum('bhncd,nbhdv->bhncv', q * jnp.exp(cum), states)

    o = (o_intra + o_inter).transpose(0, 2, 3, 1, 4).reshape(B, S, GLA_HEADS, GLA_DV)
    o = rmsnorm(o, g_norm).reshape(B, S, GLA_V) * jax.nn.silu(r.astype(jnp.float32))
    return o.astype(h.dtype) @ w_out

def rope_partial(t, cos, sin):
    half = ROPE_DIMS // 2
    x1, x2, rest = t[..., :half], t[..., half:ROPE_DIMS], t[..., ROPE_DIMS:]
    return jnp.concatenate([x1 * cos - x2 * sin, x2 * cos + x1 * sin, rest], axis=-1).astype(t.dtype)

def diff_mixer(h, positions, w_in, lq1, lk1, lq2, lk2, g_norm, w_out, lambda_init):
    B, S, _ = h.shape
    nQ = S // Q_BLOCK
    proj = h @ w_in
    q, k, v = jnp.split(proj, [DIFF_QK, 2 * DIFF_QK], axis=-1)
    q = q.reshape(B, S, 2 * DIFF_HEADS, DIFF_DH)
    k = k.reshape(B, S, 2 * DIFF_HEADS, DIFF_DH)
    v = v.reshape(B, S, DIFF_HEADS, DIFF_DV)

    inv_freq = ROPE_THETA ** (-jnp.arange(0, ROPE_DIMS, 2, dtype=jnp.float32) / ROPE_DIMS)
    ang = positions.astype(jnp.float32)[..., None] * inv_freq
    cos, sin = jnp.cos(ang)[:, :, None, :], jnp.sin(ang)[:, :, None, :]
    q = rope_partial(q, cos, sin) * (DIFF_DH ** -0.5)
    k = rope_partial(k, cos, sin)
    q = q.reshape(B, S, DIFF_HEADS, 2, DIFF_DH)
    k = k.reshape(B, S, DIFF_HEADS, 2, DIFF_DH)

    lam = (jnp.exp(jnp.sum(lq1.astype(jnp.float32) * lk1.astype(jnp.float32)))
           - jnp.exp(jnp.sum(lq2.astype(jnp.float32) * lk2.astype(jnp.float32)))
           + lambda_init)

    qb = q.reshape(B, nQ, Q_BLOCK, DIFF_HEADS, 2, DIFF_DH).transpose(1, 0, 2, 3, 4, 5)
    key_idx = jnp.arange(S)

    def block(args):
        q_blk, i = args
        s = jnp.einsum('bqhmd,bkhmd->bhmqk', q_blk, k).astype(jnp.float32)
        q_idx = i * Q_BLOCK + jnp.arange(Q_BLOCK)
        mask = key_idx[None, :] <= q_idx[:, None]
        p = jax.nn.softmax(jnp.where(mask, s, -jnp.inf), axis=-1)
        attn = p[:, :, 0] - lam * p[:, :, 1]
        return jnp.einsum('bhqk,bkhv->bqhv', attn.astype(v.dtype), v)

    o = lax.map(block, (qb, jnp.arange(nQ)))
    o = o.transpose(1, 0, 2, 3, 4).reshape(B, S, DIFF_HEADS, DIFF_DV)
    o = rmsnorm(o, g_norm) * (1.0 - lambda_init)
    return o.reshape(B, S, DIFF_VW) @ w_out

def peer(h, w_query, sub_keys, expert_u, expert_v):
    B, S, D = h.shape
    tokens = h.reshape(-1, PEER_TOKEN_BLOCK, D)

    def block(x_blk):
        T = x_blk.shape[0]
        qry = (x_blk @ w_query).reshape(T, PEER_HEADS, 2, PEER_DKEY)
        scores = jnp.einsum('thpd,hpnd->thpn', qry, sub_keys).astype(jnp.float32)
        top_s, top_i = lax.top_k(scores, PEER_TOPK)
        cand_s = top_s[:, :, 0, :, None] + top_s[:, :, 1, None, :]
        cand_i = top_i[:, :, 0, :, None] * PEER_NKEYS + top_i[:, :, 1, None, :]
        cand_s = cand_s.reshape(T, PEER_HEADS, PEER_TOPK * PEER_TOPK)
        cand_i = cand_i.reshape(T, PEER_HEADS, PEER_TOPK * PEER_TOPK)
        best_s, best_pos = lax.top_k(cand_s, PEER_TOPK)
        idx = jnp.take_along_axis(cand_i, best_pos, axis=-1)
        gate = jax.nn.softmax(best_s, axis=-1)
        u = expert_u[idx]
        act = jax.nn.gelu(jnp.einsum('thkd,td->thk', u, x_blk), approximate=False)
        vsel = expert_v[idx]
        return jnp.einsum('thk,thkd->td', (gate * act).astype(vsel.dtype), vsel)

    return lax.map(block, tokens).reshape(B, S, D)

def setup_inputs(seed: int = 0) -> dict:
    key = jax.random.key(seed)
    ks = jax.random.split(key, 24)
    f32 = jnp.float32
    D = D_MODEL

    def nrm(k, shape, scale):
        return jax.random.normal(k, shape, f32) * scale

    x = jax.random.normal(ks[0], (BATCH, SEQ, D), f32)
    positions = jnp.broadcast_to(jnp.arange(SEQ, dtype=jnp.int32)[None, :], (BATCH, SEQ))
    return {
        "x": x,
        "positions": positions,
        "norm_mix": 1.0 + nrm(ks[1], (DEPTH, D), 0.02),
        "norm_ffn": 1.0 + nrm(ks[2], (DEPTH, D), 0.02),
        "norm_final": 1.0 + nrm(ks[3], (D,), 0.02),
        "gla_w_in": nrm(ks[4], (N_GLA_LAYERS, D, GLA_IN), D ** -0.5),
        "gla_w_gate_up": nrm(ks[5], (N_GLA_LAYERS, GLA_GATE_RANK, GLA_QK), GLA_GATE_RANK ** -0.5),
        "gla_b_gate": nrm(ks[6], (N_GLA_LAYERS, GLA_QK), 0.1),
        "gla_norm": 1.0 + nrm(ks[7], (N_GLA_LAYERS, GLA_HEADS, GLA_DV), 0.02),
        "gla_w_out": nrm(ks[8], (N_GLA_LAYERS, GLA_V, D), GLA_V ** -0.5),
        "diff_w_in": nrm(ks[9], (N_DIFF_LAYERS, D, DIFF_IN), D ** -0.5),
        "diff_lambda_q1": nrm(ks[10], (N_DIFF_LAYERS, DIFF_DH), 0.1),
        "diff_lambda_k1": nrm(ks[11], (N_DIFF_LAYERS, DIFF_DH), 0.1),
        "diff_lambda_q2": nrm(ks[12], (N_DIFF_LAYERS, DIFF_DH), 0.1),
        "diff_lambda_k2": nrm(ks[13], (N_DIFF_LAYERS, DIFF_DH), 0.1),
        "diff_norm": 1.0 + nrm(ks[14], (N_DIFF_LAYERS, DIFF_HEADS, DIFF_DV), 0.02),
        "diff_w_out": nrm(ks[15], (N_DIFF_LAYERS, DIFF_VW, D), DIFF_VW ** -0.5),
        "peer_w_query": nrm(ks[16], (DEPTH, D, PEER_HEADS * 2 * PEER_DKEY), D ** -0.5),
        "peer_sub_keys": nrm(ks[17], (DEPTH, PEER_HEADS, 2, PEER_NKEYS, PEER_DKEY), PEER_DKEY ** -0.5),
        "peer_u": nrm(ks[18], (DEPTH, PEER_N_EXPERTS, D), D ** -0.5),
        "peer_v": nrm(ks[19], (DEPTH, PEER_N_EXPERTS, D), PEER_HEADS ** -0.5),
    }

def reference(x, positions, norm_mix, norm_ffn, norm_final,
              gla_w_in, gla_w_gate_up, gla_b_gate, gla_norm, gla_w_out,
              diff_w_in, diff_lambda_q1, diff_lambda_k1, diff_lambda_q2, diff_lambda_k2,
              diff_norm, diff_w_out,
              peer_w_query, peer_sub_keys, peer_u, peer_v):
    h = x
    for i in range(DEPTH):
        hn = rmsnorm(h, norm_mix[i])
        j = i // N_MIXERS
        if i % N_MIXERS == 0:
            mix = gla_mixer(hn, gla_w_in[j], gla_w_gate_up[j], gla_b_gate[j],
                            gla_norm[j], gla_w_out[j])
        else:
            lambda_init = 0.8 - 0.6 * math.exp(-0.3 * i)
            mix = diff_mixer(hn, positions, diff_w_in[j], diff_lambda_q1[j], diff_lambda_k1[j],
                             diff_lambda_q2[j], diff_lambda_k2[j], diff_norm[j], diff_w_out[j],
                             lambda_init)
        h = h + mix.astype(h.dtype)
        ff = peer(rmsnorm(h, norm_ffn[i]), peer_w_query[i], peer_sub_keys[i], peer_u[i], peer_v[i])
        h = h + ff.astype(h.dtype)
    return rmsnorm(h, norm_final)


_drawn_inputs = setup_inputs


def setup_inputs(seed=0):
    import zlib

    import numpy as np

    out = dict(_drawn_inputs(seed))
    spreads = {}
    factors = {'norm_final': 3.006, 'diff_lambda_q1': 6.422, 'diff_norm': 3.406}
    for name, (base, spread) in spreads.items():
        noise = np.random.default_rng([zlib.crc32(name.encode()), seed]).standard_normal(out[name].shape)
        drawn = base * np.exp(spread * noise) if base else spread * noise
        out[name] = __import__('jax').numpy.asarray(drawn.astype(out[name].dtype))
    for name, factor in factors.items():
        out[name] = (out[name] * factor).astype(out[name].dtype)
    return out
```

```python
import math
from contextlib import ExitStack

import numpy as np
import concourse.bass as bass
from concourse import mybir

P = 128
D = 1024
KD = D // P
SEQ = 256
NT = SEQ // P
EPS = 1e-6
NEG = -3.0e38
BANK = 512

GH, GDK, GDV, GCH, GRANK, GTAU = 4, 128, 256, 64, 16, 16.0
NCH = SEQ // GCH
DH, DDH, DDV = 8, 64, 128
ROPE, THETA = 16, 500000.0
PH, NK, TOPK = 8, 128, 16
HP = 2 * PH
SLOTS = PH * TOPK
NCHUNK = 128
U4 = 4
TOK4 = 4
NGRP = SEQ // TOK4

WBLK = KD * 512
A_WGLR = 6 * WBLK
A_Q, A_K, A_V, A_R, A_GLR = 24832, 25856, 26880, 28928, 30976
A_HX = 32768 - NT * D
A_WOUT = 0
A_WQ = 8192
A_X, A_CUM, A_E1, A_E2, A_E3, A_E4, A_Z, A_T, A_ONES, A_KN, A_AT, A_ST = (
    8192, 9216, 10240, 11264, 12288, 13312, 14336, 15360, 16384, 17408, 18432, 19456)
A_DQ, A_DK, A_DV = 24832, 26880, 28928
A_RT, A_QT, A_KT, A_S, A_P, A_ATT, A_ATTT, A_O = 8192, 10240, 12288, 14336, 15360, 16384, 16896, 18432
A_QRY, A_CAND, A_EQ, A_KEYN, A_KEYT, A_SC = 0, 4096, 8192, 24576, 26624, 28672
A_TS, A_TI, A_TIF, A_BS, A_BP, A_PA, A_PAF, A_IJ, A_GG, A_SM = (
    12288, 12800, 13312, 13824, 14080, 14336, 14848, 15360, 15872, 16128)


def trunk_kernel(nc, x, positions, norm_mix, norm_ffn, norm_final,
                 gla_w_in, gla_w_gate_up, gla_b_gate, gla_norm, gla_w_out,
                 diff_w_in, lq1, lk1, lq2, lk2, diff_norm, diff_w_out,
                 peer_w_query, peer_sub_keys, peer_u, peer_v, out):
    f32, f32r = mybir.dt.float32, mybir.dt.float32r
    i32, u32 = mybir.dt.int32, mybir.dt.uint32
    ALU, ACT, AX = mybir.AluOpType, mybir.ActivationFunctionType, mybir.AxisListType
    ctx = ExitStack()
    with ctx:
        def sb(name, shape, dt=f32):
            return ctx.enter_context(nc.sbuf_tensor(name, shape, dt))

        sems = {}

        def S(name):
            if name not in sems:
                sems[name] = ctx.enter_context(nc.semaphore(name))
            return sems[name]

        arena = sb("arena", [P, 32768])
        h = sb("h", [P, NT, D])
        hnT = sb("hnT", [P, KD, SEQ])
        hnT_split = sb("hnT_split", [P, 2, KD, SEQ], f32r)
        raw = sb("raw", [P, U4, D])
        split = sb("split", [P, 2, 2, D], f32r)
        wsplit = sb("wsplit", [P, 2, 2, SEQ], f32r)
        ident = sb("ident", [P, P])
        iota = sb("iota", [P, P])
        causalT = sb("causalT", [P, P])
        causal_add = sb("causal_add", [P, P])
        slotT = sb("slotT", [P, 3, SEQ])
        gains = sb("gains", [P, 56])
        gain_rows = sb("gain_rows", [56, P])
        stat = sb("stat", [P, 64])
        gate_up = sb("gate_up", [GRANK, GH * GDK])
        pos_i = sb("pos_i", [P, NT], i32)
        bank_all = ctx.enter_context(nc.psum_tensor("banks", [P, 8 * BANK], f32))

        def bank(b, n=1):
            return bank_all[:, b * BANK:(b + n) * BANK]

        def ar(off, n):
            return arena[:, off:off + n]

        W = arena[:, :].rearrange("p (i t) -> p i t", t=SEQ)
        G_MIX, G_FFN, G_GLA, G_DIFF, G_BG = 0, 16, 32, 40, 48
        ST_SS, ST_V, ST_Y, ST_T, ST_DEC = 0, 8, 16, 24, 32

        def OH(r, k, which):
            return hnT[:, :, :].rearrange("p k t -> p (k t)")[:, ((r * TOK4 + k) * 2 + which) * P:
                                                               ((r * TOK4 + k) * 2 + which + 1) * P]

        block = ctx.enter_context(nc.Block())

        win_of = [gla_w_in[0], diff_w_in[0]]
        wout_of = [gla_w_out[0], diff_w_out[0]]

        def cols(w, a, b):
            return w.rearrange("(k p) n -> p k n", p=P)[:, :, a:b]

        @block.sync
        def _(sp):
            sp.dma_start(h[:], x[0].rearrange("(m p) d -> p m d", p=P)).then_inc(S("x_loaded"), 16)
            def load_u(L, c, u):
                sp.dma_start(raw[:, u, :], peer_u[L].rearrange("(c p) d -> p c d", p=P)[:, c, :]
                             ).then_inc(S(f"raw_loaded{u}"), 16)

            def load_v(L, c, u):
                sp.dma_start(raw[:, u, :], peer_v[L].rearrange("(c p) d -> p c d", p=P)[:, c, :]
                             ).then_inc(S(f"raw_loaded{u}"), 16)

            for L in range(2):
                b = L * NCHUNK
                for u in range(U4):
                    if L:
                        sp.wait_ge(S("v_hi"), b - U4 + u + 1)
                        sp.wait_ge(S("v_lo"), b - U4 + u + 1)
                    load_u(L, u, u)
                with sp.Fori(1, NCHUNK // U4) as g0:
                    c0 = g0 * U4
                    for u in range(U4):
                        sp.wait_ge(S("u_transposed"), c0 + (b + u - U4 + 1))
                        load_u(L, c0 + u, u)
                for u in range(U4):
                    sp.wait_ge(S("u_transposed"), b + NCHUNK - U4 + u + 1)
                    load_v(L, u, u)
                with sp.Fori(1, NCHUNK // U4) as g0:
                    c0 = g0 * U4
                    for u in range(U4):
                        sp.wait_ge(S("v_hi"), c0 + (b + u - U4 + 1))
                        sp.wait_ge(S("v_lo"), c0 + (b + u - U4 + 1))
                        load_v(L, c0 + u, u)
            sp.wait_ge(S("v_lo"), 2 * NCHUNK)
            sp.dma_start(raw[:, 0, :], norm_final.rearrange("(a n) -> a n", a=1).broadcast_to([P, D])
                         ).then_inc(S("gfinal_loaded"), 16)
            sp.wait_ge(S("out_ready"), 1)
            sp.dma_start(out[0].rearrange("(m p) d -> p m d", p=P),
                         ar(A_HX, NT * D).rearrange("p (m d) -> p m d", m=NT)).then_inc(S("out_stored"), 16)
            sp.wait_ge(S("out_stored"), 16)

        @block.gpsimd
        def _(pool):
            for L in range(2):
                if L == 0:
                    pool.dma_start(ar(A_WGLR, KD * GRANK).rearrange("p (k n) -> p k n", k=KD),
                                   cols(win_of[0], 3072, 3088)).then_inc(S("glr_loaded"), 16)
                for blk in range(6):
                    if L:
                        pool.wait_ge(S("w_lo"), 16 * (blk + 1))
                    pool.dma_start(ar(blk * WBLK, WBLK).rearrange("p (k n) -> p k n", k=KD),
                                   cols(win_of[L], 512 * blk, 512 * blk + 512)
                                   ).then_inc(S(f"win_loaded{blk}"), 16)
                if L == 0:
                    pool.memset(ident[:], 0.0).then_inc(S("const0"), 1)
                    pool.memset(causalT[:], 1.0).then_inc(S("const0"), 1)
                    pool.memset(causal_add[:], 0.0).then_inc(S("const0"), 1)
                    pool.iota(iota[:], [[1, P]], base=0, channel_multiplier=0,
                              allow_small_or_imprecise_dtypes=True).then_inc(S("const"), 1)
                    pool.wait_ge(S("const0"), 3)
                    pool.affine_select(out=ident[:], in_=ident[:], compare_op=ALU.not_equal, fill=1.0,
                                       base=0, pattern=[[-1, P]], channel_multiplier=1
                                       ).then_inc(S("const"), 1)
                    pool.affine_select(out=causalT[:], in_=causalT[:], compare_op=ALU.is_ge, fill=0.0,
                                       base=0, pattern=[[1, P]], channel_multiplier=-1
                                       ).then_inc(S("const1"), 1)
                    pool.affine_select(out=causal_add[:], in_=causal_add[:], compare_op=ALU.is_ge, fill=NEG,
                                       base=0, pattern=[[-1, P]], channel_multiplier=1
                                       ).then_inc(S("const"), 1)
                    pool.wait_ge(S("const1"), 1)
                    pool.memset(causalT[0:GCH, GCH:P], 0.0).then_inc(S("const"), 1)
                pool.wait_ge(S("proj_done"), L + 1)
                pool.dma_start(ar(A_WOUT, KD * D).rearrange("p (k n) -> p k n", k=KD),
                               cols(wout_of[L], 0, D)).then_inc(S("wout_loaded"), 16)
                if L:
                    for j, lq in enumerate((lq1, lk1, lq2, lk2)):
                        pool.dma_start(ar(A_RT + 256 + 64 * j, DDH), lq.broadcast_to([P, DDH])
                                       ).then_inc(S("lam_loaded"), 16)
                pool.wait_ge(S("o_transposed"), L + 1)
                pool.dma_start(ar(A_KEYN, HP * P).rearrange("p (g d) -> p g d", g=HP),
                               peer_sub_keys[L].rearrange("h q n d -> n (h q) d")
                               ).then_inc(S("keys_loaded"), 16)
                for blk in range(4):
                    pool.dma_start(ar(A_WQ + blk * WBLK, WBLK).rearrange("p (k n) -> p k n", k=KD),
                                   cols(peer_w_query[L], 512 * blk, 512 * blk + 512)
                                   ).then_inc(S(f"wq_loaded{blk}"), 16)

        @block.tensor
        def _(pe):
            pe.wait_ge(S("const"), 4)
            pe.wait_ge(S("small_loaded"), 16 * 6)
            nc.tensor.transpose(bank(7)[:, 0:52], gain_rows[0:52, :], ident[0:52, 0:52]
                                ).then_inc(S("gains_transposed"), 1)

            def norm_transposes(n):
                pe.wait_ge(S("hx_ready"), n + 1)
                pe.wait_ge(S("gains_ready"), 1)
                for k in range(KD):
                    for m in range(NT):
                        last = nc.tensor.transpose(
                            bank_all[:, k * SEQ + m * P:k * SEQ + (m + 1) * P],
                            ar(A_HX + m * D + k * P, P), ident[:])
                last.then_inc(S("hx_transposed"), 1)

            def mixer_out(L):
                pe.wait_ge(S("o_ready"), L + 1)
                src = A_R if L == 0 else A_O
                for k in range(KD):
                    for m in range(NT):
                        last = nc.tensor.transpose(
                            bank_all[:, k * SEQ + m * P:k * SEQ + (m + 1) * P],
                            ar(src + m * D + k * P, P), ident[:])
                last.then_inc(S("o_transposed"), 1)
                pe.wait_ge(S("wout_loaded"), 16 * (L + 1))
                pe.wait_ge(S("oT_ready"), L + 1)
                for m in range(NT):
                    for g in range(2):
                        for k in range(KD):
                            last = nc.tensor.matmul(bank(4 + 2 * m + g), hnT[:, k, m * P:(m + 1) * P],
                                                    ar(A_WOUT + k * D + g * 512, 512),
                                                    start=(k == 0), stop=(k == KD - 1))
                last.then_inc(S("mix_done"), 1)

            def projections(L):
                nonlocal unit
                pe.wait_ge(S("hnT_ready"), 2 * L + 1)

                def bank_free():
                    if unit >= 4:
                        pe.wait_ge(S("unit_evicted"), unit - 3)

                if L == 0:
                    pe.wait_ge(S("glr_loaded"), 16)
                    bank_free()
                    for k in range(KD):
                        last = nc.tensor.matmul(bank(4 + unit % 4)[0:GRANK, 0:SEQ],
                                                ar(A_WGLR + k * GRANK, GRANK), hnT[:, k, :],
                                                start=(k == 0), stop=(k == KD - 1))
                    last.then_inc(S("unit_done"), 1)
                    unit += 1
                for blk in range(6):
                    pe.wait_ge(S(f"win_loaded{blk}"), 16 * (L + 1))
                    if L == 0 and blk < 2:
                        for pair in range(2):
                            bank_free()
                            for c in range(2):
                                for k in range(KD):
                                    last = nc.tensor.matmul(
                                        bank(4 + unit % 4)[:, c * SEQ:(c + 1) * SEQ],
                                        ar(blk * WBLK + k * 512 + (2 * pair + c) * P, P), hnT[:, k, :],
                                        start=(k == 0), stop=(k == KD - 1))
                            last.then_inc(S("unit_done"), 1)
                            unit += 1
                    else:
                        for m in range(NT):
                            bank_free()
                            for k in range(KD):
                                last = nc.tensor.matmul(bank(4 + unit % 4), hnT[:, k, m * P:(m + 1) * P],
                                                        ar(blk * WBLK + k * 512, 512),
                                                        start=(k == 0), stop=(k == KD - 1))
                            last.then_inc(S("unit_done"), 1)
                            unit += 1
                pe.wait_ge(S("unit_evicted"), unit)
                nc.tensor.nop().then_inc(S("proj_done"), 1)

            def gla():
                for hh in range(GH):
                    last = nc.tensor.matmul(bank_all[:, hh * SEQ:(hh + 1) * SEQ],
                                            gate_up[:, hh * GDK:(hh + 1) * GDK],
                                            ar(A_GLR, SEQ)[0:GRANK, :], start=True, stop=True)
                last.then_inc(S("gate_done"), 1)
                pe.wait_ge(S("klT_ready"), 1)
                for m in range(NT):
                    for hh in range(GH):
                        last = nc.tensor.transpose(bank(2 + m)[:, hh * P:(hh + 1) * P],
                                                   ar(A_E4 + hh * SEQ + m * P, P), ident[:])
                last.then_inc(S("kn_transposed"), 1)
                for m in range(NT):
                    for hh in range(GH):
                        last = nc.tensor.matmul(bank(m)[:, hh * P:(hh + 1) * P],
                                                ar(A_E2 + hh * SEQ + m * P, P),
                                                ar(A_E1 + hh * SEQ + m * P, P), start=True, stop=True)
                last.then_inc(S("aT_done"), 1)
                pe.wait_ge(S("kn_ready"), 1)
                for n in range(NCH - 1):
                    m, r0 = n // 2, GCH * (n % 2)
                    for hh in range(GH):
                        idx = n * GH + hh
                        b = (4, 5, 6, 7, 2, 3)[idx // 2]
                        last = nc.tensor.matmul(
                            bank(b)[:, (idx % 2) * 256:(idx % 2) * 256 + 256],
                            arena[r0:r0 + GCH, A_KN + (m * GH + hh) * P:A_KN + (m * GH + hh + 1) * P],
                            arena[r0:r0 + GCH, A_V + m * D + hh * GDV:A_V + m * D + (hh + 1) * GDV],
                            start=True, stop=True)
                last.then_inc(S("kv_done"), 1)
                pe.wait_ge(S("aT_ready"), 1)
                pe.wait_ge(S("states_ready"), 1)
                for m in range(NT):
                    for hh in range(GH):
                        o = bank(4 + (m * GH + hh) // 2)
                        f = (hh % 2) * 256
                        parts = [n for n in (2 * m, 2 * m + 1) if n > 0]
                        nc.tensor.matmul(o[:, f:f + 256], ar(A_AT + (m * GH + hh) * P, P),
                                         ar(A_V + m * D + hh * GDV, GDV), start=True, stop=False,
                                         skip_group_check=True)
                        for n in parts:
                            r0 = GCH * (n % 2)
                            last = nc.tensor.matmul(
                                o[r0:r0 + GCH, f:f + 256],
                                ar(A_E3 + hh * SEQ + n * GCH, GCH),
                                ar(A_ST + ((n - 1) * GH + hh) * GDV, GDV), start=False, stop=(n == parts[-1]),
                                skip_group_check=True)
                last.then_inc(S("gla_o_done"), 1)

            def diff():
                pe.wait_ge(S("rope_ready"), 1)
                for s, src in ((0, A_DQ), (1, A_DK)):
                    for hh in range(DH):
                        for m in range(NT):
                            last = nc.tensor.transpose(
                                bank_all[:, s * 2048 + hh * SEQ + m * P:s * 2048 + hh * SEQ + (m + 1) * P],
                                ar(src + m * D + hh * P, P), ident[:])
                    last.then_inc(S("qk_transposed"), 1)
                pe.wait_ge(S("qk_ready"), 2)
                n = 0

                def scores(n):
                    hh, m = n // NT, n % NT
                    if n >= 1:
                        pe.wait_ge(S("s_evicted"), n)
                    for half in range(2):
                        r0 = half * DDH
                        last = nc.tensor.matmul(
                            bank(half)[:, (n % 2) * 256:(n % 2) * 256 + (m + 1) * P],
                            arena[r0:r0 + DDH, A_QT + hh * SEQ + m * P:A_QT + hh * SEQ + (m + 1) * P],
                            arena[r0:r0 + DDH, A_KT + hh * SEQ:A_KT + hh * SEQ + (m + 1) * P],
                            start=True, stop=True)
                    last.then_inc(S("s_done"), 1)

                scores(0)
                for n in range(DH * NT):
                    hh, m = n // NT, n % NT
                    if n + 1 < DH * NT:
                        scores(n + 1)
                    pe.wait_ge(S("attn_ready"), n + 1)
                    if n >= 2:
                        pe.wait_ge(S("attnT_ready"), n - 1)
                    for kt in range(m + 1):
                        last = nc.tensor.transpose(bank(2 + n % 2)[:, kt * P:(kt + 1) * P],
                                                   ar(A_ATT + (n % 2) * 256 + kt * P, P), ident[:])
                    last.then_inc(S("attn_transposed"), 1)
                    pe.wait_ge(S("attnT_ready"), n + 1)
                    o = bank(4 + 2 * m + hh // 4)[:, (hh % 4) * P:(hh % 4 + 1) * P]
                    for kt in range(m + 1):
                        last = nc.tensor.matmul(o, ar(A_ATTT + (n % 2) * 256 + kt * P, P),
                                                ar(A_DV + kt * D + hh * DDV, DDV),
                                                start=(kt == 0), stop=(kt == m))
                    last.then_inc(S("diff_o_done"), 1)

            def peer_search(L):
                nonlocal unit
                pe.wait_ge(S("hnT_ready"), 2 * L + 2)
                for g in range(HP):
                    if g % 4 == 0:
                        pe.wait_ge(S(f"wq_loaded{g // 4}"), 16 * (L + 1))
                    if g % 2 == 0 and unit >= 4:
                        pe.wait_ge(S("unit_evicted"), unit - 3)
                    for k in range(KD):
                        last = nc.tensor.matmul(bank(4 + unit % 4)[:, (g % 2) * SEQ:(g % 2 + 1) * SEQ],
                                                ar(A_WQ + (g // 4) * WBLK + k * 512 + (g % 4) * P, P),
                                                hnT[:, k, :], start=(k == 0), stop=(k == KD - 1))
                    if g % 2:
                        last.then_inc(S("unit_done"), 1)
                        unit += 1
                pe.wait_ge(S("keys_loaded"), 16 * (L + 1))
                for g in range(HP):
                    last = nc.tensor.transpose(bank_all[:, g * P:(g + 1) * P], ar(A_KEYN + g * P, P), ident[:])
                last.then_inc(S("keys_transposed"), 1)
                pe.wait_ge(S("keysT_ready"), L + 1)
                pe.wait_ge(S("unit_evicted"), unit)
                for m in range(NT):
                    for q in range(4):
                        if unit >= 4:
                            pe.wait_ge(S("unit_evicted"), unit - 3)
                        for g in range(4 * q, 4 * q + 4):
                            last = nc.tensor.matmul(bank(4 + unit % 4)[:, (g % 4) * P:(g % 4 + 1) * P],
                                                    ar(A_QRY + g * SEQ + m * P, P), ar(A_KEYT + g * P, P),
                                                    start=True, stop=True)
                        last.then_inc(S("unit_done"), 1)
                        unit += 1

            def slot_transposes(L):
                pe.wait_ge(S("chosen"), L + 1)
                for v, src in enumerate((A_IJ, A_IJ + NT * SLOTS, A_GG)):
                    for m in range(NT):
                        last = nc.tensor.transpose(bank_all[:, 6 * BANK + v * SEQ + m * P:6 * BANK + v * SEQ + (m + 1) * P],
                                                   ar(src + m * SLOTS, P), ident[:])
                last.then_inc(S("slots_transposed"), 1)

            def peer_up(L):
                b = L * NCHUNK

                def transposes(c0, u):
                    pe.wait_ge(S(f"raw_loaded{u % U4}"), 4 * c0 + (16 * (u // U4) + 16 + 16 * (2 * b // U4)))
                    if not isinstance(c0, int) or b + c0 + u - 1 > 0:
                        pe.wait_ge(S("u_lo"), c0 + (b + u - 1))
                    for k in range(KD):
                        last = nc.tensor.transpose(bank(2 * (u % 2), 2)[:, k * P:(k + 1) * P],
                                                   raw[:, u % U4, k * P:(k + 1) * P], ident[:])
                    last.then_inc(S("u_transposed"), 1)

                def products(c0, u):
                    pe.wait_ge(S("u_lo"), c0 + (b + u + 1))
                    if not isinstance(c0, int) or b + c0 + u - 1 > 0:
                        pe.wait_ge(S("gelu_done"), c0 + (b + u - 1))
                    n = 0
                    for k in range(KD):
                        for s, t in ((0, 0), (0, 1), (1, 0)):
                            last = nc.tensor.matmul(bank(4 + u % 2)[:, 0:SEQ],
                                                    split[:, u % 2, s, k * P:(k + 1) * P],
                                                    hnT_split[:, t, k, :], start=(n == 0), stop=(n == 23))
                            n += 1
                    last.then_inc(S("a_done"), 1)

                pe.wait_ge(S("hn_lo"), L + 1)
                transposes(0, 0)

                def body(c0, last_group):
                    for u in range(U4):
                        if not (last_group and u == U4 - 1):
                            transposes(c0, u + 1)
                        products(c0, u)

                body(0, False)
                with pe.Fori(1, NCHUNK // U4 - 1) as g0:
                    c0 = g0 * U4
                    body(c0, False)
                body(NCHUNK - U4, True)

            def peer_gates(L):
                b = L * NGRP
                pe.wait_ge(S("gelu_done"), (L + 1) * NCHUNK)

                def group(q0, r):
                    pe.wait_ge(S("onehots_ready"), q0 + (b + r + 1))
                    if not isinstance(q0, int) or b + q0 + r - 1 > 0:
                        pe.wait_ge(S("w_multiplied"), q0 + (b + r - 1))
                    for k in range(TOK4):
                        last = nc.tensor.matmul(bank(4 + r)[:, k * P:(k + 1) * P],
                                                OH(r, k, 0), OH(r, k, 1), start=True, stop=True)
                    last.then_inc(S("gates_done"), 1)

                for r in range(2):
                    group(0, r)
                with pe.Fori(1, NGRP // 2) as g0:
                    q0 = g0 * 2
                    for r in range(2):
                        group(q0, r)

            def peer_down(L):
                b = L * NCHUNK

                def chunk(c0, u, first, final):
                    pe.wait_ge(S("v_lo"), c0 + (b + u + 1))
                    pe.wait_ge(S("w_lo"), c0 + (b + u + 1))
                    for k in range(KD):
                        for n, (s, t) in enumerate(((0, 0), (0, 1), (1, 0))):
                            last = nc.tensor.matmul(bank_all[:, k * SEQ:(k + 1) * SEQ],
                                                    split[:, u % 2, s, k * P:(k + 1) * P],
                                                    wsplit[:, u % 2, t, :],
                                                    start=(first and k % 2 == 0 and n == 0),
                                                    stop=(final and n == 2), skip_group_check=True)
                    last.then_inc(S("v_used"), 1)

                for u in range(U4):
                    chunk(0, u, u == 0, False)
                with pe.Fori(1, NCHUNK // U4 - 1) as g0:
                    c0 = g0 * U4
                    for u in range(U4):
                        chunk(c0, u, False, False)
                for u in range(U4):
                    chunk(NCHUNK - U4, u, False, u == U4 - 1)
                pe.wait_ge(S("ffT_ready"), L + 1)
                for m in range(NT):
                    for k in range(KD):
                        last = nc.tensor.transpose(bank(4, 4)[:, m * D + k * P:m * D + (k + 1) * P],
                                                   hnT[:, k, m * P:(m + 1) * P], ident[:])
                last.then_inc(S("ff_transposed"), 1)

            unit = 0
            for L in range(2):
                norm_transposes(2 * L)
                projections(L)
                gla() if L == 0 else diff()
                mixer_out(L)
                norm_transposes(2 * L + 1)
                peer_search(L)
                slot_transposes(L)
                peer_up(L)
                peer_gates(L)
                peer_down(L)

        @block.scalar
        def _(act):
            A = nc.scalar.activation
            sl = S("small_loaded")
            for r0, src in ((0, norm_mix.rearrange("l (c p) -> (l c) p", p=P)),
                            (16, norm_ffn.rearrange("l (c p) -> (l c) p", p=P)),
                            (32, gla_norm[0].rearrange("h (c p) -> (h c) p", p=P)),
                            (40, diff_norm[0]),
                            (48, gla_b_gate.rearrange("l (c p) -> (l c) p", p=P))):
                act.dma_start(gain_rows[r0:r0 + src.shape[0], :], src).then_inc(sl, 16)
            act.dma_start(gate_up[:], gla_w_gate_up[0]).then_inc(sl, 16)
            act.dma_start(pos_i[:], positions.rearrange("o (m p) -> p (o m)", p=P),
                          allow_slow_non_contiguous=True).then_inc(S("pos_loaded"), 16)
            act.wait_ge(S("gains_transposed"), 1)
            A(gains[:, 0:52], bank(7)[:, 0:52], ACT.Copy).then_inc(S("gains_ready"), 1)

            def norm(n):
                if n == 0:
                    act.wait_ge(S("x_loaded"), 16)
                else:
                    act.wait_ge(S("h_updated"), n)
                for m in range(NT):
                    last = A(ar(A_HX + m * D, D), h[:, m, :], ACT.Square,
                             accum_out=stat[:, ST_SS + m:ST_SS + m + 1])
                last.then_inc(S("squares_summed"), 1)
                act.wait_ge(S("mean_ready"), n + 1 + (n > 0) + (n > 2))
                A(stat[:, ST_T:ST_T + NT], stat[:, ST_V:ST_V + NT], ACT.Sqrt).then_inc(S("root_ready"), 1)

            def normed_T(n):
                L, which = n // 2, n % 2
                act.wait_ge(S("hx_transposed"), n + 1)
                act.wait_ge(S("gains_ready"), 1)
                g0 = (G_FFN if which else G_MIX) + L * KD
                for k in range(KD):
                    last = A(hnT[:, k, :], bank_all[:, k * SEQ:(k + 1) * SEQ], ACT.Copy,
                             scale=gains[:, g0 + k:g0 + k + 1])
                last.then_inc(S("hnT_ready"), 1)
                if which:
                    act.wait_ge(S("hnT_ready"), n + 1)
                    A(hnT_split[:, 0], hnT[:], ACT.Copy).then_inc(S("hn_hi"), 1)

            unit = 0

            def evict(dst, rows=P, w=BANK, scale=1.0):
                nonlocal unit
                act.wait_ge(S("unit_done"), unit + 1)
                A(dst, bank(4 + unit % 4)[0:rows, 0:w], ACT.Copy, scale=scale).then_inc(S("unit_evicted"), 1)
                unit += 1

            def projections(L):
                if L == 0:
                    evict(arena[0:GRANK, A_GLR:A_GLR + SEQ], GRANK, SEQ)
                    for pair in range(2):
                        evict(ar(A_Q + pair * 512, 512), scale=GDK ** -0.5)
                    for pair in range(2):
                        evict(ar(A_K + pair * 512, 512))
                    for blk in range(4):
                        for m in range(NT):
                            evict(ar((A_V if blk < 2 else A_R) + m * D + (blk % 2) * 512, 512))
                else:
                    for blk in range(6):
                        for m in range(NT):
                            evict(ar((A_DQ, A_DK, A_DV)[blk // 2] + m * D + (blk % 2) * 512, 512),
                                  scale=DDH ** -0.5 if blk < 2 else 1.0)

            def gla():
                act.wait_ge(S("z_ready"), 1)
                A(ar(A_T, 1024), ar(A_Z, 1024), ACT.Abs).then_inc(S("act_chain"), 1)
                act.wait_ge(S("act_chain"), 1)
                A(ar(A_T, 1024), ar(A_T, 1024), ACT.Exp, scale=-1.0).then_inc(S("act_chain"), 1)
                act.wait_ge(S("act_chain"), 2)
                A(ar(A_T, 1024), ar(A_T, 1024), ACT.Ln, bias=1.0).then_inc(S("ln_ready"), 1)
                act.wait_ge(S("x1_ready"), 1)
                A(ar(A_E1, 1024), ar(A_X, 1024), ACT.Exp, scale=1 / GTAU).then_inc(S("exps_ready"), 1)
                A(ar(A_E2, 1024), ar(A_X, 1024), ACT.Exp, scale=-1 / GTAU).then_inc(S("exps_ready"), 1)
                A(ar(A_E3, 1024), ar(A_CUM, 1024), ACT.Exp, scale=1 / GTAU).then_inc(S("exps_ready"), 1)
                last_cum = ar(A_CUM, 1024).rearrange("p (g c) -> p g c", c=GCH)[:, :, GCH - 1]
                A(stat[:, ST_DEC:ST_DEC + GH * NCH], last_cum, ACT.Exp, scale=1 / GTAU).then_inc(S("exps_ready"), 1)
                act.wait_ge(S("x2_ready"), 1)
                A(ar(A_E4, 1024), ar(A_X, 1024), ACT.Exp, scale=1 / GTAU).then_inc(S("exps_ready"), 1)
                A(ar(A_R, NT * D), ar(A_R, NT * D), ACT.Silu).then_inc(S("silu_ready"), 1)
                act.wait_ge(S("kn_transposed"), 1)
                A(ar(A_KN, 1024), bank(2, 2), ACT.Copy).then_inc(S("kn_ready"), 1)
                act.wait_ge(S("gla_o_done"), 1)
                for j in range(NT * GH):
                    last = A(ar(A_X + j * GDV, GDV), bank_all[:, 4 * BANK + j * GDV:4 * BANK + (j + 1) * GDV], ACT.Square,
                             accum_out=stat[:, ST_SS + j:ST_SS + j + 1])
                last.then_inc(S("o_squares"), 1)
                act.wait_ge(S("mean_ready"), 2)
                A(stat[:, ST_T:ST_T + 8], stat[:, ST_V:ST_V + 8], ACT.Sqrt).then_inc(S("root_ready"), 1)

            def diff():
                act.wait_ge(S("angles_ready"), 1)
                A(ar(A_RT, 64), ar(A_RT, 64), ACT.Sin).then_inc(S("sincos_ready"), 1)
                act.wait_ge(S("lam_dots"), 1)
                A(stat[:, 50:52], stat[:, 48:50], ACT.Exp).then_inc(S("lam_exps"), 1)
                for s, dst in ((0, A_QT), (1, A_KT)):
                    act.wait_ge(S("qk_transposed"), s + 1)
                    A(ar(dst, 2048), bank(4 * s, 4), ACT.Copy).then_inc(S("qk_ready"), 1)
                for n in range(DH * NT):
                    m = n % NT
                    w = (m + 1) * P
                    act.wait_ge(S("max_ready"), n + 1)
                    for half in range(2):
                        o = A_S + (n % 2) * 512 + half * 256
                        last = A(ar(A_P + (n % 2) * 512 + half * 256, w), ar(o, w), ACT.Exp,
                                 bias=stat[:, 52 + (n % 2) * 2 + half:53 + (n % 2) * 2 + half],
                                 accum_out=stat[:, 56 + (n % 2) * 2 + half:57 + (n % 2) * 2 + half])
                    last.then_inc(S("exp_ready"), 1)
                    act.wait_ge(S("attn_transposed"), n + 1)
                    if n >= 2:
                        act.wait_ge(S("diff_o_done"), n - 1)
                    A(ar(A_ATTT + (n % 2) * 256, w), bank(2 + n % 2)[:, 0:w], ACT.Copy).then_inc(S("attnT_ready"), 1)
                act.wait_ge(S("diff_o_done"), DH * NT)
                act.wait_ge(S("max_ready"), DH * NT)
                for j in range(NT * DH):
                    last = A(ar(A_S + j * DDV, DDV), bank_all[:, 4 * BANK + j * DDV:4 * BANK + (j + 1) * DDV], ACT.Square,
                             accum_out=stat[:, ST_SS + j:ST_SS + j + 1])
                last.then_inc(S("o_squares"), 1)
                act.wait_ge(S("mean_ready"), 5)
                A(stat[:, 48:64], stat[:, 16:32], ACT.Sqrt).then_inc(S("root_ready"), 1)

            def mixer_out(L):
                act.wait_ge(S("o_transposed"), L + 1)
                g0 = G_DIFF if L else G_GLA
                for k in range(KD):
                    last = A(hnT[:, k, :], bank_all[:, k * SEQ:(k + 1) * SEQ], ACT.Copy,
                             scale=gains[:, g0 + k:g0 + k + 1])
                last.then_inc(S("oT_ready"), 1)

            def peer_search(L):
                for g in range(KD):
                    evict(ar(A_QRY + g * 512, 512))
                act.wait_ge(S("keys_transposed"), L + 1)
                A(ar(A_KEYT, HP * P), bank(0, 4), ACT.Copy).then_inc(S("keysT_ready"), 1)
                for m in range(NT):
                    for q in range(4):
                        evict(ar(A_SC + m * HP * NK + q * 512, 512))
                act.wait_ge(S("gate_args"), L + 1)
                A(ar(A_GG, NT * SLOTS), ar(A_GG, NT * SLOTS), ACT.Exp).then_inc(S("gate_exps"), 1)
                act.wait_ge(S("slots_transposed"), L + 1)
                A(slotT[:], bank_all[:, 6 * BANK:6 * BANK + 3 * SEQ], ACT.Copy).then_inc(S("slotT_ready"), 1)

            def peer_up(L):
                b = L * NCHUNK
                act.preload_act_table(ACT.Gelu)

                def hi(c0, u):
                    act.wait_ge(S("u_transposed"), c0 + (b + u + 1))
                    if not isinstance(c0, int) or b + c0 + u - 1 > 0:
                        act.wait_ge(S("a_done"), c0 + (b + u - 1))
                    A(split[:, u % 2, 0, :], bank(2 * (u % 2), 2), ACT.Copy).then_inc(S("u_hi"), 1)

                def gelu(c0, u):
                    act.wait_ge(S("a_done"), c0 + (b + u + 1))
                    A(W[:, c0 + u, :], bank(4 + u % 2)[:, 0:SEQ], ACT.Gelu).then_inc(S("gelu_done"), 1)

                hi(0, 0)

                def body(c0, last_group):
                    for u in range(U4):
                        if not (last_group and u == U4 - 1):
                            hi(c0, u + 1)
                        gelu(c0, u)

                body(0, False)
                with act.Fori(1, NCHUNK // U4 - 1) as g0:
                    c0 = g0 * U4
                    body(c0, False)
                body(NCHUNK - U4, True)

            def peer_down(L):
                b = L * NCHUNK
                act.wait_ge(S("w_multiplied"), (L + 1) * NGRP)

                def chunk(c0, u):
                    act.wait_ge(S(f"raw_loaded{u}"), 4 * c0 + (16 + 16 * ((2 * b + NCHUNK) // U4)))
                    if not isinstance(c0, int) or b + c0 + u - 1 > 0:
                        act.wait_ge(S("v_used"), c0 + (b + u - 1))
                    A(split[:, u % 2, 0, :], raw[:, u, :], ACT.Copy).then_inc(S("v_hi"), 1)
                    A(wsplit[:, u % 2, 0, :], W[:, c0 + u, :], ACT.Copy).then_inc(S("w_hi"), 1)

                for u in range(U4):
                    chunk(0, u)
                with act.Fori(1, NCHUNK // U4) as g0:
                    c0 = g0 * U4
                    for u in range(U4):
                        chunk(c0, u)
                act.wait_ge(S("v_used"), b + NCHUNK)
                A(hnT[:], bank(0, 4), ACT.Copy).then_inc(S("ffT_ready"), 1)

            for L in range(2):
                norm(2 * L)
                normed_T(2 * L)
                projections(L)
                gla() if L == 0 else diff()
                mixer_out(L)
                norm(2 * L + 1)
                normed_T(2 * L + 1)
                peer_search(L)
                peer_up(L)
                peer_down(L)
            norm(4)

        @block.vector
        def _(dve):
            V = nc.vector
            chain = 0

            def link(ins):
                nonlocal chain
                chain += 1
                ins.then_inc(S("dve_chain"), 1)
                dve.wait_ge(S("dve_chain"), chain)

            def rsqrt(ss, v, y, t, n, width, roots):
                V.tensor_scalar(stat[:, v:v + n], stat[:, ss:ss + n], 1.0 / width, EPS, ALU.mult, ALU.add
                                ).then_inc(S("mean_ready"), 1)
                dve.wait_ge(S("mean_ready"), roots)
                dve.wait_ge(S("root_ready"), roots)
                link(V.reciprocal(stat[:, y:y + n], stat[:, t:t + n]))
                link(V.tensor_tensor(stat[:, t:t + n], stat[:, y:y + n], stat[:, y:y + n], ALU.mult))
                link(V.tensor_tensor(stat[:, t:t + n], stat[:, t:t + n], stat[:, v:v + n], ALU.mult))
                link(V.tensor_scalar(stat[:, t:t + n], stat[:, t:t + n], -0.5, 1.5, ALU.mult, ALU.add))
                link(V.tensor_tensor(stat[:, y:y + n], stat[:, y:y + n], stat[:, t:t + n], ALU.mult))

            def norm(n):
                dve.wait_ge(S("squares_summed"), n + 1)
                rsqrt(ST_SS, ST_V, ST_Y, ST_T, NT, D, n + 1 + (n > 0) + (n > 2))
                if n == 4:
                    return
                for m in range(NT):
                    last = V.tensor_scalar(ar(A_HX + m * D, D), h[:, m, :], stat[:, ST_Y + m:ST_Y + m + 1], None,
                                           ALU.mult)
                last.then_inc(S("hx_ready"), 1)
                if n % 2:
                    dve.wait_ge(S("hn_hi"), n // 2 + 1)
                    V.tensor_tensor(hnT_split[:, 1], hnT[:], hnT_split[:, 0].bitcast(f32), ALU.subtract
                                    ).then_inc(S("hn_lo"), 1)

            def g16(off, w=GCH):
                return ar(off, 1024).rearrange("p (g c) -> p g c", c=w)

            def gla():
                dve.wait_ge(S("unit_evicted"), 13)
                dve.wait_ge(S("gate_done"), 1)
                dve.wait_ge(S("gains_ready"), 1)
                for hh in range(GH):
                    last = V.tensor_scalar(ar(A_Z + hh * SEQ, SEQ), bank_all[:, hh * SEQ:(hh + 1) * SEQ],
                                           gains[:, G_BG + hh:G_BG + hh + 1], None, ALU.add)
                last.then_inc(S("z_ready"), 1)
                V.memset(ar(A_ONES, 1024), 1.0).then_inc(S("scan_ones"), 1)
                dve.wait_ge(S("scan_ones"), 1)
                link(V.memset(g16(A_ONES)[:, :, 0], 0.0))
                dve.wait_ge(S("z_ready"), 1)
                dve.wait_ge(S("ln_ready"), 1)
                link(V.scalar_tensor_tensor(out=ar(A_Z, 1024), in0=ar(A_Z, 1024), scalar=0.0,
                                            in1=ar(A_T, 1024), op0=ALU.min, op1=ALU.subtract))
                link(V.tensor_tensor_scan(ar(A_CUM, 1024), ar(A_ONES, 1024), ar(A_Z, 1024), 0.0, ALU.mult, ALU.add))
                mid = g16(A_CUM)[:, :, GCH // 2 - 1:GCH // 2].broadcast_to([P, GH * NCH, GCH])
                end = g16(A_CUM)[:, :, GCH - 1:GCH].broadcast_to([P, GH * NCH, GCH])
                V.tensor_tensor(g16(A_X), g16(A_CUM), mid, ALU.subtract).then_inc(S("x1_ready"), 1)
                dve.wait_ge(S("exps_ready"), 2)
                V.tensor_tensor(g16(A_X), end, g16(A_CUM), ALU.subtract).then_inc(S("x2_ready"), 1)
                V.tensor_tensor(ar(A_E1, 1024), ar(A_E1, 1024), ar(A_Q, 1024), ALU.mult)
                V.tensor_tensor(ar(A_E2, 1024), ar(A_E2, 1024), ar(A_K, 1024), ALU.mult)
                dve.wait_ge(S("exps_ready"), 4)
                V.tensor_tensor(ar(A_E3, 1024), ar(A_E3, 1024), ar(A_Q, 1024), ALU.mult)
                link(V.memset(ar(A_AT, 1024), 0.0))
                dve.wait_ge(S("exps_ready"), 5)
                V.tensor_tensor(ar(A_E4, 1024), ar(A_E4, 1024), ar(A_K, 1024), ALU.mult
                                ).then_inc(S("klT_ready"), 1)
                dve.wait_ge(S("aT_done"), 1)
                for j in range(NT * GH):
                    last = V.copy_predicated(ar(A_AT + j * P, P), causalT[:].bitcast(i32),
                                             bank_all[:, j * P:(j + 1) * P])
                last.then_inc(S("aT_ready"), 1)
                dve.wait_ge(S("kv_done"), 1)
                link(V.tensor_copy(ar(A_ST, 1024), bank(4, 2)))
                for n, b in ((1, 6), (2, 2)):
                    for hh in range(GH):
                        last = V.scalar_tensor_tensor(
                            out=ar(A_ST + (n * GH + hh) * GDV, GDV), in0=ar(A_ST + ((n - 1) * GH + hh) * GDV, GDV),
                            scalar=stat[:, ST_DEC + hh * NCH + n:ST_DEC + hh * NCH + n + 1],
                            in1=bank_all[:, b * BANK + hh * GDV:b * BANK + (hh + 1) * GDV], op0=ALU.mult, op1=ALU.add)
                    if n == 1:
                        link(last)
                last.then_inc(S("states_ready"), 1)
                dve.wait_ge(S("o_squares"), 1)
                rsqrt(ST_SS, ST_V, ST_Y, ST_T, NT * GH, GDV, 2)
                dve.wait_ge(S("silu_ready"), 1)
                for j in range(NT * GH):
                    last = V.scalar_tensor_tensor(
                        out=ar(A_R + j * GDV, GDV), in0=bank_all[:, 4 * BANK + j * GDV:4 * BANK + (j + 1) * GDV],
                        scalar=stat[:, ST_Y + j:ST_Y + j + 1], in1=ar(A_R + j * GDV, GDV),
                        op0=ALU.mult, op1=ALU.mult)
                last.then_inc(S("o_ready"), 1)

            def diff():
                inv = [float(np.float32(THETA) ** np.float32(-i / ROPE)) for i in range(0, ROPE, 2)]
                two_pi = 2 * math.pi
                c1 = 6.28125
                c2 = float(np.float32(np.round((two_pi - c1) * 2 ** 20) / 2 ** 20))
                c3 = float(np.float32(two_pi - c1 - c2))
                magic = 1.5 * 2 ** 23
                dve.wait_ge(S("unit_evicted"), UNITS_DIFF)
                dve.wait_ge(S("pos_loaded"), 16)
                posf, ang, kk = A_RT + 64, A_RT + 128, A_RT + 192
                link(V.tensor_copy(ar(posf, NT), pos_i[:]))
                for m in range(NT):
                    for i, f in enumerate(inv):
                        last = V.tensor_scalar(ar(ang + m * 8 + i, 1), ar(posf + m, 1), f, None, ALU.mult)
                link(last)
                for s in range(2):
                    r, k = ar(A_RT + 16 * s, 16), ar(kk + 16 * s, 16)
                    link(V.tensor_scalar(k, ar(ang, 16), 1 / two_pi, 0.25 * s, ALU.mult, ALU.add))
                    link(V.tensor_scalar(k, k, magic, None, ALU.add))
                    link(V.tensor_scalar(k, k, magic, None, ALU.subtract))
                    link(V.scalar_tensor_tensor(out=r, in0=k, scalar=-c1, in1=ar(ang, 16), op0=ALU.mult, op1=ALU.add))
                    link(V.scalar_tensor_tensor(out=r, in0=k, scalar=-c2, in1=r, op0=ALU.mult, op1=ALU.add))
                    link(V.scalar_tensor_tensor(out=r, in0=k, scalar=-c3, in1=r, op0=ALU.mult, op1=ALU.add))
                    link(V.tensor_scalar(r, r, math.pi / 2 * s, 3.1415925, ALU.add, ALU.min))
                    link(V.tensor_scalar(r, r, -3.1415925, None, ALU.max))
                link(V.memset(ar(A_RT + 32, 32), 0.0))
                V.memset(ar(kk, 1), 0.0).then_inc(S("angles_ready"), 1)
                dve.wait_ge(S("lam_loaded"), 64)
                for s in range(2):
                    link(V.tensor_tensor_reduce(out=ar(A_RT + 512, DDH), in0=ar(A_RT + 256 + 128 * s, DDH),
                                                in1=ar(A_RT + 320 + 128 * s, DDH), scale=1.0, scalar=0.0,
                                                op0=ALU.mult, op1=ALU.add, accum_out=stat[:, 48 + s:49 + s]))
                V.memset(stat[:, 60:61], 0.0).then_inc(S("lam_dots"), 1)
                dve.wait_ge(S("lam_exps"), 1)
                lam_init = 0.8 - 0.6 * math.exp(-0.3)
                link(V.tensor_tensor(stat[:, 61:62], stat[:, 50:51], stat[:, 51:52], ALU.subtract))
                link(V.tensor_scalar(stat[:, 61:62], stat[:, 61:62], lam_init, -1.0, ALU.add, ALU.mult))
                dve.wait_ge(S("sincos_ready"), 1)
                for src in (A_DQ, A_DK):
                    for m in range(NT):
                        v = ar(src + m * D, D).rearrange("p (g d) -> p g d", d=DDH)
                        x1, x2 = v[:, :, 0:8], v[:, :, 8:16]

                        def cs(s):
                            return ar(A_RT + 16 * s + 8 * m, 8).rearrange("p (a d) -> p a d", a=1).broadcast_to([P, 16, 8])

                        t = [ar(A_RT + 1024 + 128 * j, 128).rearrange("p (g d) -> p g d", d=8) for j in range(4)]
                        V.tensor_tensor(t[0], x1, cs(1), ALU.mult)
                        V.tensor_tensor(t[1], x2, cs(0), ALU.mult)
                        V.tensor_tensor(t[2], x2, cs(1), ALU.mult)
                        link(V.tensor_tensor(t[3], x1, cs(0), ALU.mult))
                        V.tensor_tensor(x1, t[0], t[1], ALU.subtract)
                        link(V.tensor_tensor(x2, t[2], t[3], ALU.add))
                V.memset(ar(kk, 1), 0.0).then_inc(S("rope_ready"), 1)

                for n in range(DH * NT):
                    m = n % NT
                    w = (m + 1) * P
                    bf = n % 2
                    s2 = ar(A_S + bf * 512, 512).rearrange("p (a k) -> p a k", a=2)
                    p2 = bank(0, 2).rearrange("p (a k) -> p a k", a=2)[:, :, bf * 256:(bf + 1) * 256]
                    dve.wait_ge(S("s_done"), n + 1)
                    if n >= 2:
                        dve.wait_ge(S("exp_ready"), n - 1)
                    if m:
                        V.tensor_copy(s2[:, :, 0:P], p2[:, :, 0:P])
                    mask = causal_add[:].rearrange("p (a k) -> p a k", a=1).broadcast_to([P, 2, P])
                    V.tensor_tensor(s2[:, :, m * P:w], p2[:, :, m * P:w], mask, ALU.add
                                    ).then_inc(S("s_evicted"), 1)
                    dve.wait_ge(S("s_evicted"), n + 1)
                    V.tensor_reduce(stat[:, 52 + 2 * bf:54 + 2 * bf], s2[:, :, 0:w], AX.X, ALU.max, negate=True
                                    ).then_inc(S("max_ready"), 1)
                    dve.wait_ge(S("exp_ready"), n + 1)
                    link(V.reciprocal(stat[:, 62:64], stat[:, 56 + 2 * bf:58 + 2 * bf]))
                    link(V.tensor_tensor(stat[:, 63:64], stat[:, 63:64], stat[:, 61:62], ALU.mult))
                    pr = A_P + bf * 512
                    link(V.tensor_scalar(ar(pr + 256, w), ar(pr + 256, w), stat[:, 63:64], None, ALU.mult))
                    if n >= 2:
                        dve.wait_ge(S("attn_transposed"), n - 1)
                    V.scalar_tensor_tensor(out=ar(A_ATT + bf * 256, w), in0=ar(pr, w), scalar=stat[:, 62:63],
                                           in1=ar(pr + 256, w), op0=ALU.mult, op1=ALU.add
                                           ).then_inc(S("attn_ready"), 1)
                dve.wait_ge(S("o_squares"), 2)
                rsqrt(0, 16, 32, 48, NT * DH, DDV, 5)
                for m in range(NT):
                    for hh in range(DH):
                        j = m * DH + hh
                        last = V.tensor_scalar(ar(A_O + j * DDV, DDV),
                                               bank_all[:, 4 * BANK + j * DDV:4 * BANK + (j + 1) * DDV],
                                               stat[:, 32 + j:33 + j], 1.0 - lam_init, ALU.mult, ALU.mult)
                last.then_inc(S("o_ready"), 1)

            def mixer_out(L):
                dve.wait_ge(S("mix_done"), L + 1)
                V.tensor_tensor(h[:], h[:], bank(4, 4), ALU.add).then_inc(S("h_updated"), 1)
                dve.wait_ge(S("h_updated"), 2 * L + 1)

            def peer_search(L):
                n_ev = (UNITS_GLA if L == 0 else UNITS_GLA + 16 + 12) + 16
                dve.wait_ge(S("unit_evicted"), n_ev)
                sets = [(m * HP + g) for m in range(NT) for g in range(HP)]
                sc = lambda j: ar(A_SC + j * NK, NK)
                top = lambda j, r: ar(A_TS + j * TOPK + 8 * r, 8)
                idx = lambda j, r: ar(A_TI + j * TOPK + 8 * r, 8).bitcast(u32)
                for r in range(2):
                    for j in sets:
                        last = V.max(top(j, r), sc(j))
                    link(last)
                    for j in sets:
                        last = V.max_index(idx(j, r), top(j, r), sc(j))
                    link(last)
                    if r == 0:
                        for j in sets:
                            last = V.match_replace(sc(j), top(j, r), sc(j), NEG)
                        link(last)
                link(V.tensor_copy(ar(A_TIF, NT * HP * TOPK), ar(A_TI, NT * HP * TOPK).bitcast(u32)))

                def tops(off, m, half):
                    return ar(off + m * HP * TOPK, HP * TOPK).rearrange("p (h q k) -> p h q k", h=PH, q=2)[:, :, half, :]

                for m in range(NT):
                    a = tops(A_TS, m, 0).unsqueeze(3).broadcast_to([P, PH, TOPK, TOPK])
                    b = tops(A_TS, m, 1).unsqueeze(2).broadcast_to([P, PH, TOPK, TOPK])
                    last = V.tensor_tensor(ar(A_CAND + m * 2048, 2048).rearrange("p (h a b) -> p h a b", h=PH, a=TOPK),
                                           a, b, ALU.add)
                link(last)
                cand = lambda j: ar(A_CAND + j * 256, 256)
                bs = lambda j, r: ar(A_BS + j * TOPK + 8 * r, 8)
                bp = lambda j, r: ar(A_BP + j * TOPK + 8 * r, 8).bitcast(u32)
                for r in range(2):
                    for j in range(NT * PH):
                        last = V.max(bs(j, r), cand(j))
                    link(last)
                    for j in range(NT * PH):
                        last = V.max_index(bp(j, r), bs(j, r), cand(j))
                    link(last)
                    if r == 0:
                        for j in range(NT * PH):
                            last = V.match_replace(cand(j), bs(j, r), cand(j), NEG)
                        link(last)
                n_all = NT * SLOTS
                b3 = ar(A_BS, n_all).rearrange("p (g k) -> p g k", k=TOPK)
                g3 = ar(A_GG, n_all).rearrange("p (g k) -> p g k", k=TOPK)
                V.tensor_tensor(g3, b3, b3[:, :, 0:1].broadcast_to([P, NT * PH, TOPK]), ALU.subtract
                                ).then_inc(S("gate_args"), 1)
                pu = ar(A_BP, n_all).bitcast(u32)
                V.tensor_scalar(ar(A_PA, n_all).bitcast(u32), pu, 4, None, ALU.logical_shift_right)
                link(V.tensor_scalar(ar(A_PA + n_all, n_all).bitcast(u32), pu, 15, None, ALU.bitwise_and))
                link(V.tensor_copy(ar(A_PAF, 2 * n_all), ar(A_PA, 2 * n_all).bitcast(u32)))
                for half in range(2):
                    for m in range(NT):
                        e = ar(A_EQ + m * 2048, 2048)
                        place = ar(A_PAF + half * n_all + m * SLOTS, SLOTS).unsqueeze(2).broadcast_to([P, SLOTS, TOPK])
                        V.tensor_tensor(e.rearrange("p (s k) -> p s k", k=TOPK), place,
                                        iota[:, 0:TOPK].unsqueeze(1).broadcast_to([P, SLOTS, TOPK]), ALU.is_equal)
                    link(V.memset(ar(A_SM, 1), 0.0))
                    for m in range(NT):
                        e = ar(A_EQ + m * 2048, 2048)
                        e4 = e.rearrange("p (h s k) -> p h s k", h=PH, s=TOPK)
                        V.tensor_tensor(e4, e4, tops(A_TIF, m, half).unsqueeze(2).broadcast_to([P, PH, TOPK, TOPK]),
                                        ALU.mult)
                    link(V.memset(ar(A_SM, 1), 0.0))
                    for m in range(NT):
                        e = ar(A_EQ + m * 2048, 2048)
                        last = V.tensor_reduce(ar(A_IJ + half * n_all + m * SLOTS, SLOTS),
                                               e.rearrange("p (s k) -> p s k", k=TOPK), AX.X, ALU.add)
                    link(last)
                dve.wait_ge(S("gate_exps"), L + 1)
                link(V.tensor_reduce(ar(A_SM, NT * PH), g3, AX.X, ALU.add))
                link(V.reciprocal(ar(A_SM + 16, NT * PH), ar(A_SM, NT * PH)))
                V.tensor_tensor(g3, g3, ar(A_SM + 16, NT * PH).unsqueeze(2).broadcast_to([P, NT * PH, TOPK]), ALU.mult
                                ).then_inc(S("chosen"), 1)

            def peer_up(L):
                b = L * NCHUNK

                def lo(c0, u):
                    dve.wait_ge(S("u_hi"), c0 + (b + u + 1))
                    V.tensor_tensor(split[:, u % 2, 1, :], bank(2 * (u % 2), 2),
                                    split[:, u % 2, 0, :].bitcast(f32), ALU.subtract).then_inc(S("u_lo"), 1)

                with dve.Fori(0, NCHUNK // U4) as g0:
                    c0 = g0 * U4
                    for u in range(U4):
                        lo(c0, u)

            def peer_gates(L):
                b = L * NGRP
                dve.wait_ge(S("slotT_ready"), L + 1)
                dve.wait_ge(S("gelu_done"), (L + 1) * NCHUNK)

                def build(q0, r):
                    if not isinstance(q0, int) or b + q0 + r - 1 > 0:
                        dve.wait_ge(S("gates_done"), q0 + (b + r - 1))
                    for k in range(TOK4):
                        t = TOK4 * q0 + (TOK4 * r + k)
                        rb = r % 2
                        V.tensor_scalar(OH(rb, k, 0), iota[:], slotT[:, 1, bass.ds(t, 1)], None, ALU.is_equal)
                        last = V.tensor_scalar(OH(rb, k, 1), iota[:], slotT[:, 0, bass.ds(t, 1)],
                                               slotT[:, 2, bass.ds(t, 1)], ALU.is_equal, ALU.mult)
                    last.then_inc(S("onehots_ready"), 1)

                def multiply(q0, r):
                    dve.wait_ge(S("gates_done"), q0 + (b + r + 1))
                    w = W[:, :, bass.ds(TOK4 * q0 + TOK4 * r, TOK4)]
                    V.tensor_tensor(w, w, bank(4 + r).rearrange("p (k i) -> p i k", k=TOK4), ALU.mult
                                    ).then_inc(S("w_multiplied"), 1)

                build(0, 0)
                build(0, 1)
                multiply(0, 0)
                with dve.Fori(1, NGRP // 2) as g0:
                    q0 = g0 * 2
                    build(q0, 0)
                    multiply(q0 - 2, 1)
                    build(q0, 1)
                    multiply(q0, 0)
                multiply(NGRP - 2, 1)

            def peer_down(L):
                b = L * NCHUNK
                dve.wait_ge(S("w_multiplied"), (L + 1) * NGRP)
                with dve.Fori(0, NCHUNK // U4) as g0:
                    c0 = g0 * U4
                    for u in range(U4):
                        dve.wait_ge(S("v_hi"), c0 + (b + u + 1))
                        V.tensor_tensor(split[:, u % 2, 1, :], raw[:, u, :],
                                        split[:, u % 2, 0, :].bitcast(f32), ALU.subtract).then_inc(S("v_lo"), 1)
                        dve.wait_ge(S("w_hi"), c0 + (b + u + 1))
                        V.tensor_tensor(wsplit[:, u % 2, 1, :], W[:, c0 + u, :],
                                        wsplit[:, u % 2, 0, :].bitcast(f32), ALU.subtract).then_inc(S("w_lo"), 1)
                dve.wait_ge(S("ff_transposed"), L + 1)
                V.tensor_tensor(h[:], h[:], bank(4, 4), ALU.add).then_inc(S("h_updated"), 1)
                dve.wait_ge(S("h_updated"), 2 * L + 2)

            UNITS_GLA = 13
            UNITS_DIFF = UNITS_GLA + 16 + 12
            for L in range(2):
                norm(2 * L)
                gla() if L == 0 else diff()
                mixer_out(L)
                norm(2 * L + 1)
                peer_search(L)
                peer_up(L)
                peer_gates(L)
                peer_down(L)
            norm(4)
            dve.wait_ge(S("gfinal_loaded"), 16)
            for m in range(NT):
                last = V.scalar_tensor_tensor(out=ar(A_HX + m * D, D), in0=h[:, m, :],
                                              scalar=stat[:, ST_Y + m:ST_Y + m + 1], in1=raw[:, 0, :],
                                              op0=ALU.mult, op1=ALU.mult)
            last.then_inc(S("out_ready"), 1)


_INS = ["x", "positions", "norm_mix", "norm_ffn", "norm_final",
        "gla_w_in", "gla_w_gate_up", "gla_b_gate", "gla_norm", "gla_w_out",
        "diff_w_in", "diff_lambda_q1", "diff_lambda_k1", "diff_lambda_q2", "diff_lambda_k2",
        "diff_norm", "diff_w_out", "peer_w_query", "peer_sub_keys", "peer_u", "peer_v"]
_OUTS = [((1, SEQ, D), "float32")]


def kernel(**inputs):
    import numpy as _np
    import concourse.bacc as _bacc
    from concourse import mybir as _mybir
    from concourse.bass_utils import run_bass_kernel_spmd as _run

    nc = _bacc.Bacc("TRN2", target_bir_lowering=False, num_devices=1)
    arrays, args = {}, []
    for name in _INS:
        a = _np.ascontiguousarray(inputs[name])
        arrays[f"in_{name}_dram"] = a
        args.append(nc.dram_tensor(f"in_{name}_dram", a.shape, _mybir.dt.from_np(a.dtype), kind="ExternalInput").ap())
    for i, (shape, dtype) in enumerate(_OUTS):
        dt = _mybir.dt.from_np(_np.dtype(dtype))
        args.append(nc.dram_tensor(f"out_{i}_dram", shape, dt, kind="ExternalOutput").ap())
    trunk_kernel(nc, *args)
    r = _run(nc, [arrays], core_ids=[0])
    return r.results[0]["out_0_dram"]
```

```python
import math
from contextlib import ExitStack

import numpy as np
import concourse.bass as bass
from concourse import mybir

P = 128
D = 1024
KD = D // P
SEQ = 256
NT = SEQ // P
EPS = 1e-6
NEG = -3.0e38
BANK = 512

GH, GDK, GDV, GCH, GRANK, GTAU = 4, 128, 256, 64, 16, 16.0
NCH = SEQ // GCH
DH, DDH, DDV = 8, 64, 128
ROPE, THETA = 16, 500000.0
PH, NK, TOPK = 8, 128, 16
HP = 2 * PH
SLOTS = PH * TOPK
NCHUNK = 128
U4 = 4
HALF = NCHUNK // 2
TG = 8
NGRP = SEQ // TG

WBLK = KD * 512
A_WGLR = 6 * WBLK
A_Q, A_K, A_V, A_R, A_GLR = 24832, 25856, 26880, 28928, 30976
A_HX = 32768 - NT * D
A_WOUT = 0
A_WQ = 8192
A_X, A_CUM, A_E1, A_E2, A_E3, A_E4, A_Z, A_T, A_ONES, A_KN, A_AT, A_ST = (
    8192, 9216, 10240, 11264, 12288, 13312, 14336, 15360, 16384, 17408, 18432, 19456)
A_DQ, A_DK, A_DV = 24832, 26880, 28928
A_RT, A_QT, A_KT, A_S, A_P, A_ATT, A_ATTT, A_O = 8192, 10240, 12288, 14336, 15360, 16384, 16896, 18432
A_QRY, A_CAND, A_EQ, A_KEYN, A_KEYT, A_SC = 0, 16384, 20480, 24576, 26624, 28672
A_TS, A_TI, A_TIF, A_BS, A_BP, A_PA, A_PAF, A_IJ, A_GG, A_SM = (
    24576, 25088, 25600, 26112, 26368, 26624, 27136, 27648, 28160, 28416)


def trunk_kernel(nc, x, positions, norm_mix, norm_ffn, norm_final,
                 gla_w_in, gla_w_gate_up, gla_b_gate, gla_norm, gla_w_out,
                 diff_w_in, lq1, lk1, lq2, lk2, diff_norm, diff_w_out,
                 peer_w_query, peer_sub_keys, peer_u, peer_v, out):
    f32, f32r, bf16 = mybir.dt.float32, mybir.dt.float32r, mybir.dt.bfloat16
    i32, u32 = mybir.dt.int32, mybir.dt.uint32
    ALU, ACT, AX = mybir.AluOpType, mybir.ActivationFunctionType, mybir.AxisListType
    ctx = ExitStack()
    with ctx:
        def sb(name, shape, dt=f32):
            return ctx.enter_context(nc.sbuf_tensor(name, shape, dt))

        sems = {}

        def S(name):
            if name not in sems:
                sems[name] = ctx.enter_context(nc.semaphore(name))
            return sems[name]

        arena = sb("arena", [P, 32768])
        h = sb("h", [P, NT, D])
        hnT = sb("hnT", [P, KD, SEQ])
        hnT_split = sb("hnT_split", [P, 2, KD, SEQ], f32r)
        raw = sb("raw", [P, U4, D])
        split = sb("split", [P, 2, 2, D], f32r)
        wsplit = sb("wsplit", [P, 2, 2, SEQ], f32r)
        ident = sb("ident", [P, P])
        iota = sb("iota", [P, TOPK])
        iota_tok = sb("iota_tok", [P, NK, TG], bf16)
        causalT = sb("causalT", [P, P])
        causal_add = sb("causal_add", [P, P])
        slotT = sb("slotT", [P, 5, SEQ], bf16)
        onehot_j = sb("onehot_j", [P, 2, NK, TG], bf16)
        gains = sb("gains", [P, 56])
        gain_rows = sb("gain_rows", [56, P])
        stat = sb("stat", [P, 64])
        gate_up = slotT[0:GRANK, :, :].rearrange("p a t -> p (a t)")[:, 0:2 * GH * GDK].bitcast(f32)
        pos_i = sb("pos_i", [P, NT], i32)
        bank_all = ctx.enter_context(nc.psum_tensor("banks", [P, 8 * BANK], f32))

        def bank(b, n=1):
            return bank_all[:, b * BANK:(b + n) * BANK]

        def ar(off, n):
            return arena[:, off:off + n]

        W = arena[:, :].rearrange("p (i t) -> p i t", t=SEQ)
        SEARCH_STEPS = 5 + 3 + 5 + 2 + 12 + 2
        EXP_AT = 44
        G_MIX, G_FFN, G_GLA, G_DIFF, G_BG = 0, 16, 32, 40, 48
        ST_SS, ST_V, ST_Y, ST_T, ST_DEC = 0, 8, 16, 24, 32

        hn_words = hnT[:].rearrange("p k t -> p (k t)")
        onehot_i = hn_words[:, 0:HALF * TG // 2].bitcast(bf16).rearrange("p (i t) -> p i t", t=TG)
        onehot_g = hn_words[:, 256:256 + 2 * 3 * HALF * TG // 2].bitcast(bf16).rearrange(
            "p (b g i t) -> p b g i t", b=2, g=3, t=TG)

        block = ctx.enter_context(nc.Block())

        win_of = [gla_w_in[0], diff_w_in[0]]
        wout_of = [gla_w_out[0], diff_w_out[0]]

        def cols(w, a, b):
            return w.rearrange("(k p) n -> p k n", p=P)[:, :, a:b]

        @block.sync
        def _(sp):
            sp.dma_start(h[:], x[0].rearrange("(m p) d -> p m d", p=P)).then_inc(S("x_loaded"), 16)
            def load_u(L, c, u):
                sp.dma_start(raw[:, u, :], peer_u[L].rearrange("(c p) d -> p c d", p=P)[:, c, :]
                             ).then_inc(S(f"raw_loaded{u}"), 16)

            def load_v(L, c, u):
                sp.dma_start(raw[:, u, :], peer_v[L].rearrange("(c p) d -> p c d", p=P)[:, c, :]
                             ).then_inc(S(f"raw_loaded{u}"), 16)

            for L in range(2):
                b = L * NCHUNK
                for u in range(U4):
                    if L:
                        sp.wait_ge(S("v_lo"), 2 * (b - U4 + u + 1))
                    load_u(L, u, u)
                with sp.Fori(1, NCHUNK // U4) as g0:
                    c0 = g0 * U4
                    for u in range(U4):
                        sp.wait_ge(S("u_transposed"), c0 + (b + u - U4 + 1))
                        load_u(L, c0 + u, u)
                for u in range(U4):
                    sp.wait_ge(S("u_transposed"), b + NCHUNK - U4 + u + 1)
                    load_v(L, u, u)
                with sp.Fori(1, NCHUNK // U4) as g0:
                    c0 = g0 * U4
                    for u in range(U4):
                        sp.wait_ge(S("v_lo"), 2 * c0 + 2 * (b + u - U4 + 1))
                        load_v(L, c0 + u, u)
            sp.wait_ge(S("v_lo"), 4 * NCHUNK)
            sp.dma_start(raw[:, 0, :], norm_final.rearrange("(a n) -> a n", a=1).broadcast_to([P, D])
                         ).then_inc(S("gfinal_loaded"), 16)
            sp.wait_ge(S("out_ready"), 1)
            sp.dma_start(out[0].rearrange("(m p) d -> p m d", p=P),
                         ar(A_HX, NT * D).rearrange("p (m d) -> p m d", m=NT)).then_inc(S("out_stored"), 16)
            sp.wait_ge(S("out_stored"), 16)

        @block.gpsimd
        def _(pool):
            for L in range(2):
                if L == 0:
                    pool.dma_start(ar(A_WGLR, KD * GRANK).rearrange("p (k n) -> p k n", k=KD),
                                   cols(win_of[0], 3072, 3088)).then_inc(S("glr_loaded"), 16)
                for blk in range(6):
                    if L:
                        pool.wait_ge(S("w_lo"), 16 * (blk + 1))
                    pool.dma_start(ar(blk * WBLK, WBLK).rearrange("p (k n) -> p k n", k=KD),
                                   cols(win_of[L], 512 * blk, 512 * blk + 512)
                                   ).then_inc(S(f"win_loaded{blk}"), 16)
                if L == 0:
                    pool.memset(ident[:], 0.0).then_inc(S("const0"), 1)
                    pool.memset(causalT[:], 1.0).then_inc(S("const0"), 1)
                    pool.memset(causal_add[:], 0.0).then_inc(S("const0"), 1)
                    pool.iota(iota[:], [[1, TOPK]], base=0, channel_multiplier=0,
                              allow_small_or_imprecise_dtypes=True).then_inc(S("const"), 1)
                    pool.iota(iota_tok[:], [[1, NK], [0, TG]], base=0, channel_multiplier=0,
                              allow_small_or_imprecise_dtypes=True).then_inc(S("const"), 1)
                    pool.wait_ge(S("const0"), 3)
                    pool.affine_select(out=ident[:], in_=ident[:], compare_op=ALU.not_equal, fill=1.0,
                                       base=0, pattern=[[-1, P]], channel_multiplier=1
                                       ).then_inc(S("const"), 1)
                    pool.affine_select(out=causalT[:], in_=causalT[:], compare_op=ALU.is_ge, fill=0.0,
                                       base=0, pattern=[[1, P]], channel_multiplier=-1
                                       ).then_inc(S("const1"), 1)
                    pool.affine_select(out=causal_add[:], in_=causal_add[:], compare_op=ALU.is_ge, fill=NEG,
                                       base=0, pattern=[[-1, P]], channel_multiplier=1
                                       ).then_inc(S("const"), 1)
                    pool.wait_ge(S("const1"), 1)
                    pool.memset(causalT[0:GCH, GCH:P], 0.0).then_inc(S("const"), 1)
                pool.wait_ge(S("proj_done"), L + 1)
                pool.dma_start(ar(A_WOUT, KD * D).rearrange("p (k n) -> p k n", k=KD),
                               cols(wout_of[L], 0, D)).then_inc(S("wout_loaded"), 16)
                if L:
                    for j, lq in enumerate((lq1, lk1, lq2, lk2)):
                        pool.dma_start(ar(A_RT + 256 + 64 * j, DDH), lq.broadcast_to([P, DDH])
                                       ).then_inc(S("lam_loaded"), 16)
                pool.wait_ge(S("o_transposed"), L + 1)
                pool.dma_start(ar(A_KEYN, HP * P).rearrange("p (g d) -> p g d", g=HP),
                               peer_sub_keys[L].rearrange("h q n d -> n (h q) d")
                               ).then_inc(S("keys_loaded"), 16)
                for blk in range(4):
                    pool.dma_start(ar(A_WQ + blk * WBLK, WBLK).rearrange("p (k n) -> p k n", k=KD),
                                   cols(peer_w_query[L], 512 * blk, 512 * blk + 512)
                                   ).then_inc(S(f"wq_loaded{blk}"), 16)

        @block.tensor
        def _(pe):
            pe.wait_ge(S("const"), 5)
            pe.wait_ge(S("small_loaded"), 16 * 6)
            nc.tensor.transpose(bank(7)[:, 0:52], gain_rows[0:52, :], ident[0:52, 0:52]
                                ).then_inc(S("gains_transposed"), 1)

            def norm_transposes(n):
                pe.wait_ge(S("hx_ready"), n + 1)
                pe.wait_ge(S("gains_ready"), 1)
                for k in range(KD):
                    for m in range(NT):
                        last = nc.tensor.transpose(
                            bank_all[:, k * SEQ + m * P:k * SEQ + (m + 1) * P],
                            ar(A_HX + m * D + k * P, P), ident[:])
                last.then_inc(S("hx_transposed"), 1)

            def mixer_out(L):
                pe.wait_ge(S("o_ready"), L + 1)
                src = A_R if L == 0 else A_O
                for k in range(KD):
                    for m in range(NT):
                        last = nc.tensor.transpose(
                            bank_all[:, k * SEQ + m * P:k * SEQ + (m + 1) * P],
                            ar(src + m * D + k * P, P), ident[:])
                last.then_inc(S("o_transposed"), 1)
                pe.wait_ge(S("wout_loaded"), 16 * (L + 1))
                pe.wait_ge(S("oT_ready"), L + 1)
                for m in range(NT):
                    for g in range(2):
                        for k in range(KD):
                            last = nc.tensor.matmul(bank(4 + 2 * m + g), hnT[:, k, m * P:(m + 1) * P],
                                                    ar(A_WOUT + k * D + g * 512, 512),
                                                    start=(k == 0), stop=(k == KD - 1))
                last.then_inc(S("mix_done"), 1)

            def projections(L):
                nonlocal unit
                pe.wait_ge(S("hnT_ready"), 2 * L + 1)

                def bank_free():
                    if unit >= 4:
                        pe.wait_ge(S("unit_evicted"), unit - 3)

                if L == 0:
                    pe.wait_ge(S("glr_loaded"), 16)
                    bank_free()
                    for k in range(KD):
                        last = nc.tensor.matmul(bank(4 + unit % 4)[0:GRANK, 0:SEQ],
                                                ar(A_WGLR + k * GRANK, GRANK), hnT[:, k, :],
                                                start=(k == 0), stop=(k == KD - 1))
                    last.then_inc(S("unit_done"), 1)
                    unit += 1
                for blk in range(6):
                    pe.wait_ge(S(f"win_loaded{blk}"), 16 * (L + 1))
                    if L == 0 and blk < 2:
                        for pair in range(2):
                            bank_free()
                            for c in range(2):
                                for k in range(KD):
                                    last = nc.tensor.matmul(
                                        bank(4 + unit % 4)[:, c * SEQ:(c + 1) * SEQ],
                                        ar(blk * WBLK + k * 512 + (2 * pair + c) * P, P), hnT[:, k, :],
                                        start=(k == 0), stop=(k == KD - 1))
                            last.then_inc(S("unit_done"), 1)
                            unit += 1
                    else:
                        for m in range(NT):
                            bank_free()
                            for k in range(KD):
                                last = nc.tensor.matmul(bank(4 + unit % 4), hnT[:, k, m * P:(m + 1) * P],
                                                        ar(blk * WBLK + k * 512, 512),
                                                        start=(k == 0), stop=(k == KD - 1))
                            last.then_inc(S("unit_done"), 1)
                            unit += 1
                pe.wait_ge(S("unit_evicted"), unit)
                nc.tensor.nop().then_inc(S("proj_done"), 1)

            def gla():
                for hh in range(GH):
                    last = nc.tensor.matmul(bank_all[:, hh * SEQ:(hh + 1) * SEQ],
                                            gate_up[:, hh * GDK:(hh + 1) * GDK],
                                            ar(A_GLR, SEQ)[0:GRANK, :], start=True, stop=True)
                last.then_inc(S("gate_done"), 1)
                pe.wait_ge(S("klT_ready"), 1)
                for m in range(NT):
                    for hh in range(GH):
                        last = nc.tensor.transpose(bank(2 + m)[:, hh * P:(hh + 1) * P],
                                                   ar(A_E4 + hh * SEQ + m * P, P), ident[:])
                last.then_inc(S("kn_transposed"), 1)
                for m in range(NT):
                    for hh in range(GH):
                        last = nc.tensor.matmul(bank(m)[:, hh * P:(hh + 1) * P],
                                                ar(A_E2 + hh * SEQ + m * P, P),
                                                ar(A_E1 + hh * SEQ + m * P, P), start=True, stop=True)
                last.then_inc(S("aT_done"), 1)
                pe.wait_ge(S("kn_ready"), 1)
                for n in range(NCH - 1):
                    m, r0 = n // 2, GCH * (n % 2)
                    for hh in range(GH):
                        idx = n * GH + hh
                        b = (4, 5, 6, 7, 2, 3)[idx // 2]
                        last = nc.tensor.matmul(
                            bank(b)[:, (idx % 2) * 256:(idx % 2) * 256 + 256],
                            arena[r0:r0 + GCH, A_KN + (m * GH + hh) * P:A_KN + (m * GH + hh + 1) * P],
                            arena[r0:r0 + GCH, A_V + m * D + hh * GDV:A_V + m * D + (hh + 1) * GDV],
                            start=True, stop=True)
                last.then_inc(S("kv_done"), 1)
                pe.wait_ge(S("aT_ready"), 1)
                pe.wait_ge(S("states_ready"), 1)
                for m in range(NT):
                    for hh in range(GH):
                        o = bank(4 + (m * GH + hh) // 2)
                        f = (hh % 2) * 256
                        parts = [n for n in (2 * m, 2 * m + 1) if n > 0]
                        nc.tensor.matmul(o[:, f:f + 256], ar(A_AT + (m * GH + hh) * P, P),
                                         ar(A_V + m * D + hh * GDV, GDV), start=True, stop=False,
                                         skip_group_check=True)
                        for n in parts:
                            r0 = GCH * (n % 2)
                            last = nc.tensor.matmul(
                                o[r0:r0 + GCH, f:f + 256],
                                ar(A_E3 + hh * SEQ + n * GCH, GCH),
                                ar(A_ST + ((n - 1) * GH + hh) * GDV, GDV), start=False, stop=(n == parts[-1]),
                                skip_group_check=True)
                last.then_inc(S("gla_o_done"), 1)

            def diff():
                pe.wait_ge(S("rope_ready"), 1)
                for s, src in ((0, A_DQ), (1, A_DK)):
                    for hh in range(DH):
                        for m in range(NT):
                            last = nc.tensor.transpose(
                                bank_all[:, s * 2048 + hh * SEQ + m * P:s * 2048 + hh * SEQ + (m + 1) * P],
                                ar(src + m * D + hh * P, P), ident[:])
                    last.then_inc(S("qk_transposed"), 1)
                pe.wait_ge(S("qk_ready"), 2)
                n = 0

                def scores(n):
                    hh, m = n // NT, n % NT
                    if n >= 1:
                        pe.wait_ge(S("s_evicted"), n)
                    for half in range(2):
                        r0 = half * DDH
                        last = nc.tensor.matmul(
                            bank(half)[:, (n % 2) * 256:(n % 2) * 256 + (m + 1) * P],
                            arena[r0:r0 + DDH, A_QT + hh * SEQ + m * P:A_QT + hh * SEQ + (m + 1) * P],
                            arena[r0:r0 + DDH, A_KT + hh * SEQ:A_KT + hh * SEQ + (m + 1) * P],
                            start=True, stop=True)
                    last.then_inc(S("s_done"), 1)

                scores(0)
                for n in range(DH * NT):
                    hh, m = n // NT, n % NT
                    if n + 1 < DH * NT:
                        scores(n + 1)
                    pe.wait_ge(S("attn_ready"), n + 1)
                    if n >= 2:
                        pe.wait_ge(S("attnT_ready"), n - 1)
                    for kt in range(m + 1):
                        last = nc.tensor.transpose(bank(2 + n % 2)[:, kt * P:(kt + 1) * P],
                                                   ar(A_ATT + (n % 2) * 256 + kt * P, P), ident[:])
                    last.then_inc(S("attn_transposed"), 1)
                    pe.wait_ge(S("attnT_ready"), n + 1)
                    o = bank(4 + 2 * m + hh // 4)[:, (hh % 4) * P:(hh % 4 + 1) * P]
                    for kt in range(m + 1):
                        last = nc.tensor.matmul(o, ar(A_ATTT + (n % 2) * 256 + kt * P, P),
                                                ar(A_DV + kt * D + hh * DDV, DDV),
                                                start=(kt == 0), stop=(kt == m))
                    last.then_inc(S("diff_o_done"), 1)

            def peer_search(L):
                nonlocal unit
                pe.wait_ge(S("hnT_ready"), 2 * L + 2)
                for g in range(HP):
                    if g % 4 == 0:
                        pe.wait_ge(S(f"wq_loaded{g // 4}"), 16 * (L + 1))
                    if g % 2 == 0 and unit >= 4:
                        pe.wait_ge(S("unit_evicted"), unit - 3)
                    for k in range(KD):
                        last = nc.tensor.matmul(bank(4 + unit % 4)[:, (g % 2) * SEQ:(g % 2 + 1) * SEQ],
                                                ar(A_WQ + (g // 4) * WBLK + k * 512 + (g % 4) * P, P),
                                                hnT[:, k, :], start=(k == 0), stop=(k == KD - 1))
                    if g % 2:
                        last.then_inc(S("unit_done"), 1)
                        unit += 1
                pe.wait_ge(S("keys_loaded"), 16 * (L + 1))
                for g in range(HP):
                    last = nc.tensor.transpose(bank_all[:, g * P:(g + 1) * P], ar(A_KEYN + g * P, P), ident[:])
                last.then_inc(S("keys_transposed"), 1)
                pe.wait_ge(S("keysT_ready"), L + 1)
                pe.wait_ge(S("unit_evicted"), unit)
                for m in range(NT):
                    for q in range(4):
                        if unit >= 4:
                            pe.wait_ge(S("unit_evicted"), unit - 3)
                        for g in range(4 * q, 4 * q + 4):
                            last = nc.tensor.matmul(bank(4 + unit % 4)[:, (g % 4) * P:(g % 4 + 1) * P],
                                                    ar(A_QRY + g * SEQ + m * P, P), ar(A_KEYT + g * P, P),
                                                    start=True, stop=True)
                        last.then_inc(S("unit_done"), 1)
                        unit += 1

            def slot_transposes(L):
                pe.wait_ge(S("chosen"), L + 1)
                for v, src in enumerate((A_IJ, A_IJ + NT * SLOTS, A_GG)):
                    for m in range(NT):
                        last = nc.tensor.transpose(bank_all[:, 6 * BANK + v * SEQ + m * P:6 * BANK + v * SEQ + (m + 1) * P],
                                                   ar(src + m * SLOTS, P), ident[:])
                last.then_inc(S("slots_transposed"), 1)

            def peer_up(L):
                b = L * NCHUNK

                def transposes(c0, u):
                    pe.wait_ge(S(f"raw_loaded{u % U4}"), 4 * c0 + (16 * (u // U4) + 16 + 16 * (2 * b // U4)))
                    if not isinstance(c0, int) or b + c0 + u - 1 > 0:
                        pe.wait_ge(S("u_lo"), c0 + (b + u - 1))
                    for k in range(KD):
                        last = nc.tensor.transpose(bank(2 * (u % 2), 2)[:, k * P:(k + 1) * P],
                                                   raw[:, u % U4, k * P:(k + 1) * P], ident[:])
                    last.then_inc(S("u_transposed"), 1)

                def products(c0, u):
                    pe.wait_ge(S("u_lo"), c0 + (b + u + 1))
                    if not isinstance(c0, int) or b + c0 + u - 1 > 0:
                        pe.wait_ge(S("gelu_done"), c0 + (b + u - 1))
                    n = 0
                    for k in range(KD):
                        for s, t in ((0, 0), (0, 1), (1, 0)):
                            last = nc.tensor.matmul(bank(4 + u % 2)[:, 0:SEQ],
                                                    split[:, u % 2, s, k * P:(k + 1) * P],
                                                    hnT_split[:, t, k, :], start=(n == 0), stop=(n == 23))
                            n += 1
                    last.then_inc(S("a_done"), 1)

                pe.wait_ge(S("hn_lo"), L + 1)
                transposes(0, 0)

                def body(c0, last_group):
                    for u in range(U4):
                        if not (last_group and u == U4 - 1):
                            transposes(c0, u + 1)
                        products(c0, u)
                        if u % 2 and second:
                            gates(L, 0, (c0 - HALF) // 2 if isinstance(c0, int) else g0 * (U4 // 2) - HALF // 2, u // 2)

                second = False
                body(0, False)
                with pe.Fori(1, HALF // U4) as g0:
                    body(g0 * U4, False)
                slot_transposes(L)
                second = True
                body(HALF, False)
                with pe.Fori(HALF // U4 + 1, NCHUNK // U4 - 1) as g0:
                    body(g0 * U4, False)
                body(NCHUNK - U4, True)

            def gates(L, half, p0, r):
                b = (2 * L + half) * NGRP
                pe.wait_ge(S("onehots_ready"), p0 + (b + r + 1))
                if not isinstance(p0, int) or b + p0 + r - 1 > 0:
                    pe.wait_ge(S("w_multiplied"), p0 + (b + r - 1))
                for k in range(TG):
                    for g in range(3):
                        last = nc.tensor.matmul(bank(6 + r)[:, k * HALF:(k + 1) * HALF],
                                                onehot_j[:, r, :, k], onehot_g[:, r, g, :, k],
                                                start=(g == 0), stop=(g == 2))
                last.then_inc(S("gates_done"), 1)

            def peer_down(L):
                b = L * NCHUNK

                def chunk(c0, u, first, final):
                    pe.wait_ge(S("w_lo"), c0 + (b + u + 1))
                    for k in range(KD):
                        if k % 4 == 0:
                            pe.wait_ge(S("v_lo"), 2 * c0 + (2 * (b + u) + 1 + k // 4))
                        for n, (s, t) in enumerate(((0, 0), (0, 1), (1, 0))):
                            last = nc.tensor.matmul(bank_all[:, k * SEQ:(k + 1) * SEQ],
                                                    split[:, u % 2, s, k * P:(k + 1) * P],
                                                    wsplit[:, u % 2, t, :],
                                                    start=(first and k % 2 == 0 and n == 0),
                                                    stop=(final and n == 2), skip_group_check=True)
                    last.then_inc(S("v_used"), 1)

                for u in range(U4):
                    chunk(0, u, u == 0, False)
                    if u % 2:
                        gates(L, 1, 0, u // 2)
                with pe.Fori(1, HALF // U4) as g0:
                    for u in range(U4):
                        chunk(g0 * U4, u, False, False)
                        if u % 2:
                            gates(L, 1, g0 * 2, u // 2)
                with pe.Fori(HALF // U4, NCHUNK // U4 - 1) as g0:
                    for u in range(U4):
                        chunk(g0 * U4, u, False, False)
                for u in range(U4):
                    chunk(NCHUNK - U4, u, False, u == U4 - 1)
                pe.wait_ge(S("ffT_ready"), L + 1)
                for m in range(NT):
                    for k in range(KD):
                        last = nc.tensor.transpose(bank(4, 4)[:, m * D + k * P:m * D + (k + 1) * P],
                                                   hnT[:, k, m * P:(m + 1) * P], ident[:])
                last.then_inc(S("ff_transposed"), 1)

            unit = 0
            for L in range(2):
                norm_transposes(2 * L)
                projections(L)
                gla() if L == 0 else diff()
                mixer_out(L)
                norm_transposes(2 * L + 1)
                peer_search(L)
                peer_up(L)
                peer_down(L)

        @block.scalar
        def _(act):
            A = nc.scalar.activation
            sl = S("small_loaded")
            for r0, src in ((0, norm_mix.rearrange("l (c p) -> (l c) p", p=P)),
                            (16, norm_ffn.rearrange("l (c p) -> (l c) p", p=P)),
                            (32, gla_norm[0].rearrange("h (c p) -> (h c) p", p=P)),
                            (40, diff_norm[0]),
                            (48, gla_b_gate.rearrange("l (c p) -> (l c) p", p=P))):
                act.dma_start(gain_rows[r0:r0 + src.shape[0], :], src).then_inc(sl, 16)
            act.dma_start(gate_up, gla_w_gate_up[0]).then_inc(sl, 16)
            act.dma_start(pos_i[:], positions.rearrange("o (m p) -> p (o m)", p=P),
                          allow_slow_non_contiguous=True).then_inc(S("pos_loaded"), 16)
            act.wait_ge(S("gains_transposed"), 1)
            A(gains[:, 0:52], bank(7)[:, 0:52], ACT.Copy).then_inc(S("gains_ready"), 1)

            def norm(n):
                if n == 0:
                    act.wait_ge(S("x_loaded"), 16)
                else:
                    act.wait_ge(S("h_updated"), n)
                for m in range(NT):
                    last = A(ar(A_HX + m * D, D), h[:, m, :], ACT.Square,
                             accum_out=stat[:, ST_SS + m:ST_SS + m + 1])
                last.then_inc(S("squares_summed"), 1)
                act.wait_ge(S("mean_ready"), n + 1 + (n > 0) + (n > 2))
                A(stat[:, ST_T:ST_T + NT], stat[:, ST_V:ST_V + NT], ACT.Sqrt).then_inc(S("root_ready"), 1)

            def normed_T(n):
                L, which = n // 2, n % 2
                act.wait_ge(S("hx_transposed"), n + 1)
                act.wait_ge(S("gains_ready"), 1)
                g0 = (G_FFN if which else G_MIX) + L * KD
                for k in range(KD):
                    last = A(hnT[:, k, :], bank_all[:, k * SEQ:(k + 1) * SEQ], ACT.Copy,
                             scale=gains[:, g0 + k:g0 + k + 1])
                last.then_inc(S("hnT_ready"), 1)
                if which:
                    act.wait_ge(S("hnT_ready"), n + 1)
                    A(hnT_split[:, 0], hnT[:], ACT.Copy).then_inc(S("hn_hi"), 1)

            unit = 0

            def evict(dst, rows=P, w=BANK, scale=1.0):
                nonlocal unit
                act.wait_ge(S("unit_done"), unit + 1)
                A(dst, bank(4 + unit % 4)[0:rows, 0:w], ACT.Copy, scale=scale).then_inc(S("unit_evicted"), 1)
                unit += 1

            def projections(L):
                if L == 0:
                    evict(arena[0:GRANK, A_GLR:A_GLR + SEQ], GRANK, SEQ)
                    for pair in range(2):
                        evict(ar(A_Q + pair * 512, 512), scale=GDK ** -0.5)
                    for pair in range(2):
                        evict(ar(A_K + pair * 512, 512))
                    for blk in range(4):
                        for m in range(NT):
                            evict(ar((A_V if blk < 2 else A_R) + m * D + (blk % 2) * 512, 512))
                else:
                    for blk in range(6):
                        for m in range(NT):
                            evict(ar((A_DQ, A_DK, A_DV)[blk // 2] + m * D + (blk % 2) * 512, 512),
                                  scale=DDH ** -0.5 if blk < 2 else 1.0)

            def gla():
                act.wait_ge(S("z_ready"), 1)
                A(ar(A_T, 1024), ar(A_Z, 1024), ACT.Abs).then_inc(S("act_chain"), 1)
                act.wait_ge(S("act_chain"), 1)
                A(ar(A_T, 1024), ar(A_T, 1024), ACT.Exp, scale=-1.0).then_inc(S("act_chain"), 1)
                act.wait_ge(S("act_chain"), 2)
                A(ar(A_T, 1024), ar(A_T, 1024), ACT.Ln, bias=1.0).then_inc(S("ln_ready"), 1)
                act.wait_ge(S("x1_ready"), 1)
                A(ar(A_E1, 1024), ar(A_X, 1024), ACT.Exp, scale=1 / GTAU).then_inc(S("exps_ready"), 1)
                A(ar(A_E2, 1024), ar(A_X, 1024), ACT.Exp, scale=-1 / GTAU).then_inc(S("exps_ready"), 1)
                A(ar(A_E3, 1024), ar(A_CUM, 1024), ACT.Exp, scale=1 / GTAU).then_inc(S("exps_ready"), 1)
                last_cum = ar(A_CUM, 1024).rearrange("p (g c) -> p g c", c=GCH)[:, :, GCH - 1]
                A(stat[:, ST_DEC:ST_DEC + GH * NCH], last_cum, ACT.Exp, scale=1 / GTAU).then_inc(S("exps_ready"), 1)
                act.wait_ge(S("x2_ready"), 1)
                A(ar(A_E4, 1024), ar(A_X, 1024), ACT.Exp, scale=1 / GTAU).then_inc(S("exps_ready"), 1)
                A(ar(A_R, NT * D), ar(A_R, NT * D), ACT.Silu).then_inc(S("silu_ready"), 1)
                act.wait_ge(S("kn_transposed"), 1)
                A(ar(A_KN, 1024), bank(2, 2), ACT.Copy).then_inc(S("kn_ready"), 1)
                act.wait_ge(S("gla_o_done"), 1)
                for j in range(NT * GH):
                    last = A(ar(A_X + j * GDV, GDV), bank_all[:, 4 * BANK + j * GDV:4 * BANK + (j + 1) * GDV], ACT.Square,
                             accum_out=stat[:, ST_SS + j:ST_SS + j + 1])
                last.then_inc(S("o_squares"), 1)
                act.wait_ge(S("mean_ready"), 2)
                A(stat[:, ST_T:ST_T + 8], stat[:, ST_V:ST_V + 8], ACT.Sqrt).then_inc(S("root_ready"), 1)

            def diff():
                act.wait_ge(S("angles_ready"), 1)
                A(ar(A_RT, 64), ar(A_RT, 64), ACT.Sin).then_inc(S("sincos_ready"), 1)
                act.wait_ge(S("lam_dots"), 1)
                A(stat[:, 50:52], stat[:, 48:50], ACT.Exp).then_inc(S("lam_exps"), 1)
                for s, dst in ((0, A_QT), (1, A_KT)):
                    act.wait_ge(S("qk_transposed"), s + 1)
                    A(ar(dst, 2048), bank(4 * s, 4), ACT.Copy).then_inc(S("qk_ready"), 1)
                for n in range(DH * NT):
                    m = n % NT
                    w = (m + 1) * P
                    act.wait_ge(S("max_ready"), n + 1)
                    for half in range(2):
                        o = A_S + (n % 2) * 512 + half * 256
                        last = A(ar(A_P + (n % 2) * 512 + half * 256, w), ar(o, w), ACT.Exp,
                                 bias=stat[:, 52 + (n % 2) * 2 + half:53 + (n % 2) * 2 + half],
                                 accum_out=stat[:, 56 + (n % 2) * 2 + half:57 + (n % 2) * 2 + half])
                    last.then_inc(S("exp_ready"), 1)
                    act.wait_ge(S("attn_transposed"), n + 1)
                    if n >= 2:
                        act.wait_ge(S("diff_o_done"), n - 1)
                    A(ar(A_ATTT + (n % 2) * 256, w), bank(2 + n % 2)[:, 0:w], ACT.Copy).then_inc(S("attnT_ready"), 1)
                act.wait_ge(S("diff_o_done"), DH * NT)
                act.wait_ge(S("max_ready"), DH * NT)
                for j in range(NT * DH):
                    last = A(ar(A_S + j * DDV, DDV), bank_all[:, 4 * BANK + j * DDV:4 * BANK + (j + 1) * DDV], ACT.Square,
                             accum_out=stat[:, ST_SS + j:ST_SS + j + 1])
                last.then_inc(S("o_squares"), 1)
                act.wait_ge(S("mean_ready"), 5)
                A(stat[:, 48:64], stat[:, 16:32], ACT.Sqrt).then_inc(S("root_ready"), 1)

            def mixer_out(L):
                act.wait_ge(S("o_transposed"), L + 1)
                g0 = G_DIFF if L else G_GLA
                for k in range(KD):
                    last = A(hnT[:, k, :], bank_all[:, k * SEQ:(k + 1) * SEQ], ACT.Copy,
                             scale=gains[:, g0 + k:g0 + k + 1])
                last.then_inc(S("oT_ready"), 1)

            def peer_search(L):
                for g in range(KD):
                    evict(ar(A_QRY + g * 512, 512))
                act.wait_ge(S("keys_transposed"), L + 1)
                A(ar(A_KEYT, HP * P), bank(0, 4), ACT.Copy).then_inc(S("keysT_ready"), 1)
                for m in range(NT):
                    for q in range(4):
                        evict(ar(A_SC + m * HP * NK + q * 512, 512))

            def peer_up(L):
                b = L * NCHUNK
                act.preload_act_table(ACT.Gelu)

                def hi(c0, u):
                    act.wait_ge(S("u_transposed"), c0 + (b + u + 1))
                    if not isinstance(c0, int) or b + c0 + u - 1 > 0:
                        act.wait_ge(S("a_done"), c0 + (b + u - 1))
                    A(split[:, u % 2, 0, :], bank(2 * (u % 2), 2), ACT.Copy).then_inc(S("u_hi"), 1)

                def gelu(c0, u):
                    act.wait_ge(S("a_done"), c0 + (b + u + 1))
                    A(W[:, c0 + u, :], bank(4 + u % 2)[:, 0:SEQ], ACT.Gelu).then_inc(S("gelu_done"), 1)

                hi(0, 0)

                def body(c0, last_group):
                    for u in range(U4):
                        if not (last_group and u == U4 - 1):
                            hi(c0, u + 1)
                        gelu(c0, u)

                body(0, False)
                with act.Fori(1, EXP_AT // U4) as g0:
                    body(g0 * U4, False)
                act.wait_ge(S("gate_args"), L + 1)
                A(ar(A_GG, NT * SLOTS), ar(A_GG, NT * SLOTS), ACT.Exp).then_inc(S("gate_exps"), 1)
                act.preload_act_table(ACT.Gelu)
                with act.Fori(EXP_AT // U4, NCHUNK // U4 - 1) as g0:
                    body(g0 * U4, False)
                body(NCHUNK - U4, True)

            def peer_down(L):
                b = L * NCHUNK
                act.wait_ge(S("w_multiplied"), (2 * L + 1) * NGRP)

                def chunk(c0, u):
                    act.wait_ge(S(f"raw_loaded{u}"), 4 * c0 + (16 + 16 * ((2 * b + NCHUNK) // U4)))
                    if not isinstance(c0, int) or b + c0 + u - 1 > 0:
                        act.wait_ge(S("v_used"), c0 + (b + u - 1))
                    A(wsplit[:, u % 2, 0, :], W[:, c0 + u, :], ACT.Copy).then_inc(S("w_hi"), 1)
                    for f in range(2):
                        A(split[:, u % 2, 0, f * 512:(f + 1) * 512], raw[:, u, f * 512:(f + 1) * 512],
                          ACT.Copy).then_inc(S("v_hi"), 1)

                for u in range(U4):
                    chunk(0, u)
                with act.Fori(1, HALF // U4) as g0:
                    for u in range(U4):
                        chunk(g0 * U4, u)
                act.wait_ge(S("w_multiplied"), (2 * L + 2) * NGRP)
                with act.Fori(HALF // U4, NCHUNK // U4) as g0:
                    for u in range(U4):
                        chunk(g0 * U4, u)
                act.wait_ge(S("v_used"), b + NCHUNK)
                A(hnT[:], bank(0, 4), ACT.Copy).then_inc(S("ffT_ready"), 1)

            for L in range(2):
                norm(2 * L)
                normed_T(2 * L)
                projections(L)
                gla() if L == 0 else diff()
                mixer_out(L)
                norm(2 * L + 1)
                normed_T(2 * L + 1)
                peer_search(L)
                peer_up(L)
                peer_down(L)
            norm(4)

        @block.vector
        def _(dve):
            V = nc.vector
            chain = 0

            def link(ins):
                nonlocal chain
                chain += 1
                ins.then_inc(S("dve_chain"), 1)
                dve.wait_ge(S("dve_chain"), chain)

            def rsqrt(ss, v, y, t, n, width, roots):
                V.tensor_scalar(stat[:, v:v + n], stat[:, ss:ss + n], 1.0 / width, EPS, ALU.mult, ALU.add
                                ).then_inc(S("mean_ready"), 1)
                dve.wait_ge(S("mean_ready"), roots)
                dve.wait_ge(S("root_ready"), roots)
                link(V.reciprocal(stat[:, y:y + n], stat[:, t:t + n]))
                link(V.tensor_tensor(stat[:, t:t + n], stat[:, y:y + n], stat[:, y:y + n], ALU.mult))
                link(V.tensor_tensor(stat[:, t:t + n], stat[:, t:t + n], stat[:, v:v + n], ALU.mult))
                link(V.tensor_scalar(stat[:, t:t + n], stat[:, t:t + n], -0.5, 1.5, ALU.mult, ALU.add))
                link(V.tensor_tensor(stat[:, y:y + n], stat[:, y:y + n], stat[:, t:t + n], ALU.mult))

            def norm(n):
                dve.wait_ge(S("squares_summed"), n + 1)
                rsqrt(ST_SS, ST_V, ST_Y, ST_T, NT, D, n + 1 + (n > 0) + (n > 2))
                if n == 4:
                    return
                for m in range(NT):
                    last = V.tensor_scalar(ar(A_HX + m * D, D), h[:, m, :], stat[:, ST_Y + m:ST_Y + m + 1], None,
                                           ALU.mult)
                last.then_inc(S("hx_ready"), 1)
                if n % 2:
                    dve.wait_ge(S("hn_hi"), n // 2 + 1)
                    V.tensor_tensor(hnT_split[:, 1], hnT[:], hnT_split[:, 0].bitcast(f32), ALU.subtract
                                    ).then_inc(S("hn_lo"), 1)

            def g16(off, w=GCH):
                return ar(off, 1024).rearrange("p (g c) -> p g c", c=w)

            def gla():
                dve.wait_ge(S("unit_evicted"), 13)
                dve.wait_ge(S("gate_done"), 1)
                dve.wait_ge(S("gains_ready"), 1)
                for hh in range(GH):
                    last = V.tensor_scalar(ar(A_Z + hh * SEQ, SEQ), bank_all[:, hh * SEQ:(hh + 1) * SEQ],
                                           gains[:, G_BG + hh:G_BG + hh + 1], None, ALU.add)
                last.then_inc(S("z_ready"), 1)
                V.memset(ar(A_ONES, 1024), 1.0).then_inc(S("scan_ones"), 1)
                dve.wait_ge(S("scan_ones"), 1)
                link(V.memset(g16(A_ONES)[:, :, 0], 0.0))
                dve.wait_ge(S("z_ready"), 1)
                dve.wait_ge(S("ln_ready"), 1)
                link(V.scalar_tensor_tensor(out=ar(A_Z, 1024), in0=ar(A_Z, 1024), scalar=0.0,
                                            in1=ar(A_T, 1024), op0=ALU.min, op1=ALU.subtract))
                link(V.tensor_tensor_scan(ar(A_CUM, 1024), ar(A_ONES, 1024), ar(A_Z, 1024), 0.0, ALU.mult, ALU.add))
                mid = g16(A_CUM)[:, :, GCH // 2 - 1:GCH // 2].broadcast_to([P, GH * NCH, GCH])
                end = g16(A_CUM)[:, :, GCH - 1:GCH].broadcast_to([P, GH * NCH, GCH])
                V.tensor_tensor(g16(A_X), g16(A_CUM), mid, ALU.subtract).then_inc(S("x1_ready"), 1)
                dve.wait_ge(S("exps_ready"), 2)
                V.tensor_tensor(g16(A_X), end, g16(A_CUM), ALU.subtract).then_inc(S("x2_ready"), 1)
                V.tensor_tensor(ar(A_E1, 1024), ar(A_E1, 1024), ar(A_Q, 1024), ALU.mult)
                V.tensor_tensor(ar(A_E2, 1024), ar(A_E2, 1024), ar(A_K, 1024), ALU.mult)
                dve.wait_ge(S("exps_ready"), 4)
                V.tensor_tensor(ar(A_E3, 1024), ar(A_E3, 1024), ar(A_Q, 1024), ALU.mult)
                link(V.memset(ar(A_AT, 1024), 0.0))
                dve.wait_ge(S("exps_ready"), 5)
                V.tensor_tensor(ar(A_E4, 1024), ar(A_E4, 1024), ar(A_K, 1024), ALU.mult
                                ).then_inc(S("klT_ready"), 1)
                dve.wait_ge(S("aT_done"), 1)
                for j in range(NT * GH):
                    last = V.copy_predicated(ar(A_AT + j * P, P), causalT[:].bitcast(i32),
                                             bank_all[:, j * P:(j + 1) * P])
                last.then_inc(S("aT_ready"), 1)
                dve.wait_ge(S("kv_done"), 1)
                link(V.tensor_copy(ar(A_ST, 1024), bank(4, 2)))
                for n, b in ((1, 6), (2, 2)):
                    for hh in range(GH):
                        last = V.scalar_tensor_tensor(
                            out=ar(A_ST + (n * GH + hh) * GDV, GDV), in0=ar(A_ST + ((n - 1) * GH + hh) * GDV, GDV),
                            scalar=stat[:, ST_DEC + hh * NCH + n:ST_DEC + hh * NCH + n + 1],
                            in1=bank_all[:, b * BANK + hh * GDV:b * BANK + (hh + 1) * GDV], op0=ALU.mult, op1=ALU.add)
                    if n == 1:
                        link(last)
                last.then_inc(S("states_ready"), 1)
                dve.wait_ge(S("o_squares"), 1)
                rsqrt(ST_SS, ST_V, ST_Y, ST_T, NT * GH, GDV, 2)
                dve.wait_ge(S("silu_ready"), 1)
                for j in range(NT * GH):
                    last = V.scalar_tensor_tensor(
                        out=ar(A_R + j * GDV, GDV), in0=bank_all[:, 4 * BANK + j * GDV:4 * BANK + (j + 1) * GDV],
                        scalar=stat[:, ST_Y + j:ST_Y + j + 1], in1=ar(A_R + j * GDV, GDV),
                        op0=ALU.mult, op1=ALU.mult)
                last.then_inc(S("o_ready"), 1)

            def diff():
                inv = [float(np.float32(THETA) ** np.float32(-i / ROPE)) for i in range(0, ROPE, 2)]
                two_pi = 2 * math.pi
                c1 = 6.28125
                c2 = float(np.float32(np.round((two_pi - c1) * 2 ** 20) / 2 ** 20))
                c3 = float(np.float32(two_pi - c1 - c2))
                magic = 1.5 * 2 ** 23
                dve.wait_ge(S("unit_evicted"), UNITS_DIFF)
                dve.wait_ge(S("pos_loaded"), 16)
                posf, ang, kk = A_RT + 64, A_RT + 128, A_RT + 192
                link(V.tensor_copy(ar(posf, NT), pos_i[:]))
                for m in range(NT):
                    for i, f in enumerate(inv):
                        last = V.tensor_scalar(ar(ang + m * 8 + i, 1), ar(posf + m, 1), f, None, ALU.mult)
                link(last)
                for s in range(2):
                    r, k = ar(A_RT + 16 * s, 16), ar(kk + 16 * s, 16)
                    link(V.tensor_scalar(k, ar(ang, 16), 1 / two_pi, 0.25 * s, ALU.mult, ALU.add))
                    link(V.tensor_scalar(k, k, magic, None, ALU.add))
                    link(V.tensor_scalar(k, k, magic, None, ALU.subtract))
                    link(V.scalar_tensor_tensor(out=r, in0=k, scalar=-c1, in1=ar(ang, 16), op0=ALU.mult, op1=ALU.add))
                    link(V.scalar_tensor_tensor(out=r, in0=k, scalar=-c2, in1=r, op0=ALU.mult, op1=ALU.add))
                    link(V.scalar_tensor_tensor(out=r, in0=k, scalar=-c3, in1=r, op0=ALU.mult, op1=ALU.add))
                    link(V.tensor_scalar(r, r, math.pi / 2 * s, 3.1415925, ALU.add, ALU.min))
                    link(V.tensor_scalar(r, r, -3.1415925, None, ALU.max))
                link(V.memset(ar(A_RT + 32, 32), 0.0))
                V.memset(ar(kk, 1), 0.0).then_inc(S("angles_ready"), 1)
                dve.wait_ge(S("lam_loaded"), 64)
                for s in range(2):
                    link(V.tensor_tensor_reduce(out=ar(A_RT + 512, DDH), in0=ar(A_RT + 256 + 128 * s, DDH),
                                                in1=ar(A_RT + 320 + 128 * s, DDH), scale=1.0, scalar=0.0,
                                                op0=ALU.mult, op1=ALU.add, accum_out=stat[:, 48 + s:49 + s]))
                V.memset(stat[:, 60:61], 0.0).then_inc(S("lam_dots"), 1)
                dve.wait_ge(S("lam_exps"), 1)
                lam_init = 0.8 - 0.6 * math.exp(-0.3)
                link(V.tensor_tensor(stat[:, 61:62], stat[:, 50:51], stat[:, 51:52], ALU.subtract))
                link(V.tensor_scalar(stat[:, 61:62], stat[:, 61:62], lam_init, -1.0, ALU.add, ALU.mult))
                dve.wait_ge(S("sincos_ready"), 1)
                for src in (A_DQ, A_DK):
                    for m in range(NT):
                        v = ar(src + m * D, D).rearrange("p (g d) -> p g d", d=DDH)
                        x1, x2 = v[:, :, 0:8], v[:, :, 8:16]

                        def cs(s):
                            return ar(A_RT + 16 * s + 8 * m, 8).rearrange("p (a d) -> p a d", a=1).broadcast_to([P, 16, 8])

                        t = [ar(A_RT + 1024 + 128 * j, 128).rearrange("p (g d) -> p g d", d=8) for j in range(4)]
                        V.tensor_tensor(t[0], x1, cs(1), ALU.mult)
                        V.tensor_tensor(t[1], x2, cs(0), ALU.mult)
                        V.tensor_tensor(t[2], x2, cs(1), ALU.mult)
                        link(V.tensor_tensor(t[3], x1, cs(0), ALU.mult))
                        V.tensor_tensor(x1, t[0], t[1], ALU.subtract)
                        link(V.tensor_tensor(x2, t[2], t[3], ALU.add))
                V.memset(ar(kk, 1), 0.0).then_inc(S("rope_ready"), 1)

                for n in range(DH * NT):
                    m = n % NT
                    w = (m + 1) * P
                    bf = n % 2
                    s2 = ar(A_S + bf * 512, 512).rearrange("p (a k) -> p a k", a=2)
                    p2 = bank(0, 2).rearrange("p (a k) -> p a k", a=2)[:, :, bf * 256:(bf + 1) * 256]
                    dve.wait_ge(S("s_done"), n + 1)
                    if n >= 2:
                        dve.wait_ge(S("exp_ready"), n - 1)
                    if m:
                        V.tensor_copy(s2[:, :, 0:P], p2[:, :, 0:P])
                    mask = causal_add[:].rearrange("p (a k) -> p a k", a=1).broadcast_to([P, 2, P])
                    V.tensor_tensor(s2[:, :, m * P:w], p2[:, :, m * P:w], mask, ALU.add
                                    ).then_inc(S("s_evicted"), 1)
                    dve.wait_ge(S("s_evicted"), n + 1)
                    V.tensor_reduce(stat[:, 52 + 2 * bf:54 + 2 * bf], s2[:, :, 0:w], AX.X, ALU.max, negate=True
                                    ).then_inc(S("max_ready"), 1)
                    dve.wait_ge(S("exp_ready"), n + 1)
                    link(V.reciprocal(stat[:, 62:64], stat[:, 56 + 2 * bf:58 + 2 * bf]))
                    link(V.tensor_tensor(stat[:, 63:64], stat[:, 63:64], stat[:, 61:62], ALU.mult))
                    pr = A_P + bf * 512
                    link(V.tensor_scalar(ar(pr + 256, w), ar(pr + 256, w), stat[:, 63:64], None, ALU.mult))
                    if n >= 2:
                        dve.wait_ge(S("attn_transposed"), n - 1)
                    V.scalar_tensor_tensor(out=ar(A_ATT + bf * 256, w), in0=ar(pr, w), scalar=stat[:, 62:63],
                                           in1=ar(pr + 256, w), op0=ALU.mult, op1=ALU.add
                                           ).then_inc(S("attn_ready"), 1)
                dve.wait_ge(S("o_squares"), 2)
                rsqrt(0, 16, 32, 48, NT * DH, DDV, 5)
                for m in range(NT):
                    for hh in range(DH):
                        j = m * DH + hh
                        last = V.tensor_scalar(ar(A_O + j * DDV, DDV),
                                               bank_all[:, 4 * BANK + j * DDV:4 * BANK + (j + 1) * DDV],
                                               stat[:, 32 + j:33 + j], 1.0 - lam_init, ALU.mult, ALU.mult)
                last.then_inc(S("o_ready"), 1)

            def mixer_out(L):
                dve.wait_ge(S("mix_done"), L + 1)
                V.tensor_tensor(h[:], h[:], bank(4, 4), ALU.add).then_inc(S("h_updated"), 1)
                dve.wait_ge(S("h_updated"), 2 * L + 1)

            def lo(c0, u, b):
                dve.wait_ge(S("u_hi"), c0 + (b + u + 1))
                V.tensor_tensor(split[:, u % 2, 1, :], bank(2 * (u % 2), 2),
                                split[:, u % 2, 0, :].bitcast(f32), ALU.subtract).then_inc(S("u_lo"), 1)

            def peer_search(L):
                b = L * NCHUNK
                dve.wait_ge(S("unit_evicted"), (UNITS_GLA if L == 0 else UNITS_GLA + 16 + 12) + 16)
                n_set, n_all = NT * HP, NT * SLOTS
                c = 0

                def next_chunk():
                    nonlocal c
                    lo(c, 0, b) if c % 2 == 0 else lo(c - 1, 1, b)
                    c += 1

                def ordered():
                    dve.wait_ge(S("search_step"), steps)

                steps = L * SEARCH_STEPS

                def step(ins):
                    nonlocal steps
                    steps += 1
                    ins.then_inc(S("search_step"), 1)

                def two_rounds(n, width, src, top, idx, per_chunk):
                    for r in range(2):
                        for kind in range(3 if r == 0 else 2):
                            for j in range(n):
                                if kind == 0:
                                    last = V.max(top(j, r), src(j))
                                elif kind == 1:
                                    last = V.max_index(idx(j, r), top(j, r), src(j))
                                else:
                                    last = V.match_replace(src(j), top(j, r), src(j), NEG)
                                if j == n - 1:
                                    step(last)
                                if j % per_chunk == per_chunk - 1:
                                    next_chunk()
                            ordered()

                next_chunk()
                two_rounds(n_set, NK, lambda j: ar(A_SC + j * NK, NK),
                           lambda j, r: ar(A_TS + j * TOPK + 8 * r, 8),
                           lambda j, r: ar(A_TI + j * TOPK + 8 * r, 8).bitcast(u32), 8)
                step(V.tensor_copy(ar(A_TIF, n_set * TOPK), ar(A_TI, n_set * TOPK).bitcast(u32)))

                def tops(off, m, half):
                    return ar(off + m * HP * TOPK, HP * TOPK).rearrange("p (h q k) -> p h q k", h=PH, q=2)[:, :, half, :]

                for m in range(NT):
                    x1 = tops(A_TS, m, 0).unsqueeze(3).broadcast_to([P, PH, TOPK, TOPK])
                    x2 = tops(A_TS, m, 1).unsqueeze(2).broadcast_to([P, PH, TOPK, TOPK])
                    step(V.tensor_tensor(ar(A_CAND + m * 2048, 2048).rearrange("p (h a b) -> p h a b", h=PH, a=TOPK),
                                         x1, x2, ALU.add))
                    next_chunk()
                ordered()
                two_rounds(NT * PH, 256, lambda j: ar(A_CAND + j * 256, 256),
                           lambda j, r: ar(A_BS + j * TOPK + 8 * r, 8),
                           lambda j, r: ar(A_BP + j * TOPK + 8 * r, 8).bitcast(u32), 8)
                b3 = ar(A_BS, n_all).rearrange("p (g k) -> p g k", k=TOPK)
                g3 = ar(A_GG, n_all).rearrange("p (g k) -> p g k", k=TOPK)
                V.tensor_tensor(g3, b3, b3[:, :, 0:1].broadcast_to([P, NT * PH, TOPK]), ALU.subtract
                                ).then_inc(S("gate_args"), 1)
                pu = ar(A_BP, n_all).bitcast(u32)
                V.tensor_scalar(ar(A_PA, n_all).bitcast(u32), pu, 4, None, ALU.logical_shift_right)
                step(V.tensor_scalar(ar(A_PA + n_all, n_all).bitcast(u32), pu, 15, None, ALU.bitwise_and))
                next_chunk()
                ordered()
                step(V.tensor_copy(ar(A_PAF, 2 * n_all), ar(A_PA, 2 * n_all).bitcast(u32)))
                for half in range(2):
                    for kind in range(3):
                        for m in range(NT):
                            e = ar(A_EQ + m * 2048, 2048)
                            e3 = e.rearrange("p (s k) -> p s k", k=TOPK)
                            e4 = e.rearrange("p (h s k) -> p h s k", h=PH, s=TOPK)
                            if m == 0:
                                ordered()
                            if kind == 0:
                                place = ar(A_PAF + half * n_all + m * SLOTS, SLOTS).unsqueeze(2)
                                step(V.tensor_tensor(e3, place.broadcast_to([P, SLOTS, TOPK]),
                                                     iota[:].unsqueeze(1).broadcast_to([P, SLOTS, TOPK]),
                                                     ALU.is_equal))
                            elif kind == 1:
                                listed = tops(A_TIF, m, half).unsqueeze(2).broadcast_to([P, PH, TOPK, TOPK])
                                step(V.tensor_tensor(e4, e4, listed, ALU.mult))
                            else:
                                step(V.tensor_reduce(ar(A_IJ + half * n_all + m * SLOTS, SLOTS), e3, AX.X, ALU.add))
                            next_chunk()
                dve.wait_ge(S("gate_exps"), L + 1)
                step(V.tensor_reduce(ar(A_SM, NT * PH), g3, AX.X, ALU.add))
                next_chunk()
                ordered()
                step(V.reciprocal(ar(A_SM + 16, NT * PH), ar(A_SM, NT * PH)))
                ordered()
                V.tensor_tensor(g3, g3, ar(A_SM + 16, NT * PH).unsqueeze(2).broadcast_to([P, NT * PH, TOPK]), ALU.mult
                                ).then_inc(S("chosen"), 1)
                assert steps == (L + 1) * SEARCH_STEPS, steps
                while c < HALF + 1:
                    next_chunk()
                dve.wait_ge(S("slots_transposed"), L + 1)
                V.tensor_copy(slotT[:, 0:2, :].rearrange("p a t -> p (a t)"), bank(6))
                rest = ar(A_EQ, SEQ)
                link(V.tensor_copy(slotT[:, 2, :], bank(7)[:, 0:SEQ]))
                link(V.tensor_tensor(rest, bank(7)[:, 0:SEQ], slotT[:, 2, :], ALU.subtract))
                link(V.tensor_copy(slotT[:, 3, :], rest))
                link(V.tensor_tensor(rest, rest, slotT[:, 3, :], ALU.subtract))
                link(V.tensor_copy(slotT[:, 4, :], rest))

            def build(L, half, p0, r):
                b = (2 * L + half) * NGRP
                if not isinstance(p0, int) or b + p0 + r - 1 > 0:
                    dve.wait_ge(S("gates_done"), p0 + (b + r - 1))
                if not isinstance(p0, int) or b + p0 + r > 0:
                    dve.wait_ge(S("onehots_ready"), p0 + (b + r))
                rb = r % 2
                t0 = TG * p0 + TG * r

                def of(row, n):
                    return slotT[:, row, bass.ds(t0, TG)].unsqueeze(1).broadcast_to([P, n, TG])

                V.tensor_tensor(onehot_i, iota_tok[:, half * HALF:(half + 1) * HALF, :], of(0, HALF),
                                ALU.is_equal).then_inc(S("onehot_i_ready"), 1)
                V.tensor_tensor(onehot_j[:, rb], iota_tok[:], of(1, NK), ALU.is_equal)
                dve.wait_ge(S("onehot_i_ready"), p0 + (b + r + 1))
                for g in range(3):
                    last = V.tensor_tensor(onehot_g[:, rb, g], onehot_i, of(2 + g, HALF), ALU.mult)
                last.then_inc(S("onehots_ready"), 1)

            def multiply(L, half, p0, r):
                b = (2 * L + half) * NGRP
                dve.wait_ge(S("gates_done"), p0 + (b + r + 1))
                w = W[:, half * HALF:(half + 1) * HALF, bass.ds(TG * p0 + TG * r, TG)]
                V.tensor_tensor(w, w, bank(6 + r).rearrange("p (k i) -> p i k", k=TG), ALU.mult
                                ).then_inc(S("w_multiplied"), 1)

            def peer_up_second(L):
                b = L * NCHUNK
                dve.wait_ge(S("gelu_done"), b + HALF)
                build(L, 0, 0, 0)

                def pairs(c0, p0, last_group):
                    for r in range(2):
                        lo(c0, 2 * r + 1, b)
                        if not (last_group and r == 1):
                            build(L, 0, p0, r + 1)
                            lo(c0, 2 * r + 2, b)
                        multiply(L, 0, p0, r)

                with dve.Fori(0, NGRP // 2 - 1) as g0:
                    pairs(g0 * U4 + HALF, g0 * 2, False)
                pairs(NCHUNK - U4, NGRP - 2, True)

            def peer_down(L):
                b = L * NCHUNK
                dve.wait_ge(S("gelu_done"), b + NCHUNK)
                build(L, 1, 0, 0)

                def split_v(c0, u):
                    dve.wait_ge(S("w_hi"), c0 + (b + u + 1))
                    V.tensor_tensor(wsplit[:, u % 2, 1, :], W[:, c0 + u, :],
                                    wsplit[:, u % 2, 0, :].bitcast(f32), ALU.subtract).then_inc(S("w_lo"), 1)
                    for f in range(2):
                        dve.wait_ge(S("v_hi"), 2 * c0 + (2 * (b + u) + 1 + f))
                        V.tensor_tensor(split[:, u % 2, 1, f * 512:(f + 1) * 512], raw[:, u, f * 512:(f + 1) * 512],
                                        split[:, u % 2, 0, f * 512:(f + 1) * 512].bitcast(f32), ALU.subtract
                                        ).then_inc(S("v_lo"), 1)

                split_v(0, 0)

                def pairs(c0, p0, last_group):
                    for r in range(2):
                        split_v(c0, 2 * r + 1)
                        if not (last_group and r == 1):
                            build(L, 1, p0, r + 1)
                            split_v(c0 + U4 if r else c0, 0 if r else 2)
                        multiply(L, 1, p0, r)

                with dve.Fori(0, NGRP // 2 - 1) as g0:
                    pairs(g0 * U4, g0 * 2, False)
                pairs(HALF - U4, NGRP - 2, True)
                with dve.Fori(HALF // U4, NCHUNK // U4) as g0:
                    for u in range(U4):
                        split_v(g0 * U4, u)
                dve.wait_ge(S("ff_transposed"), L + 1)
                V.tensor_tensor(h[:], h[:], bank(4, 4), ALU.add).then_inc(S("h_updated"), 1)
                dve.wait_ge(S("h_updated"), 2 * L + 2)

            UNITS_GLA = 13
            UNITS_DIFF = UNITS_GLA + 16 + 12
            for L in range(2):
                norm(2 * L)
                gla() if L == 0 else diff()
                mixer_out(L)
                norm(2 * L + 1)
                peer_search(L)
                peer_up_second(L)
                peer_down(L)
            norm(4)
            dve.wait_ge(S("gfinal_loaded"), 16)
            for m in range(NT):
                last = V.scalar_tensor_tensor(out=ar(A_HX + m * D, D), in0=h[:, m, :],
                                              scalar=stat[:, ST_Y + m:ST_Y + m + 1], in1=raw[:, 0, :],
                                              op0=ALU.mult, op1=ALU.mult)
            last.then_inc(S("out_ready"), 1)


_INS = ["x", "positions", "norm_mix", "norm_ffn", "norm_final",
        "gla_w_in", "gla_w_gate_up", "gla_b_gate", "gla_norm", "gla_w_out",
        "diff_w_in", "diff_lambda_q1", "diff_lambda_k1", "diff_lambda_q2", "diff_lambda_k2",
        "diff_norm", "diff_w_out", "peer_w_query", "peer_sub_keys", "peer_u", "peer_v"]
_OUTS = [((1, SEQ, D), "float32")]


def kernel(**inputs):
    import numpy as _np
    import concourse.bacc as _bacc
    from concourse import mybir as _mybir
    from concourse.bass_utils import run_bass_kernel_spmd as _run

    nc = _bacc.Bacc("TRN2", target_bir_lowering=False, num_devices=1)
    arrays, args = {}, []
    for name in _INS:
        a = _np.ascontiguousarray(inputs[name])
        arrays[f"in_{name}_dram"] = a
        args.append(nc.dram_tensor(f"in_{name}_dram", a.shape, _mybir.dt.from_np(a.dtype), kind="ExternalInput").ap())
    for i, (shape, dtype) in enumerate(_OUTS):
        dt = _mybir.dt.from_np(_np.dtype(dtype))
        args.append(nc.dram_tensor(f"out_{i}_dram", shape, dt, kind="ExternalOutput").ap())
    trunk_kernel(nc, *args)
    r = _run(nc, [arrays], core_ids=[0])
    return r.results[0]["out_0_dram"]
```

```python
import math
from contextlib import ExitStack

import numpy as np
import concourse.bass as bass
from concourse import mybir

P = 128
D = 1024
KD = D // P
SEQ = 256
NT = SEQ // P
EPS = 1e-6
NEG = -3.0e38
BANK = 512

GH, GDK, GDV, GCH, GRANK, GTAU = 4, 128, 256, 64, 16, 16.0
NCH = SEQ // GCH
DH, DDH, DDV = 8, 64, 128
ROPE, THETA = 16, 500000.0
PH, NK, TOPK = 8, 128, 16
HP = 2 * PH
SLOTS = PH * TOPK
NCHUNK = 128
U4 = 4
HALF = NCHUNK // 2
TG = 8
NGRP = SEQ // TG

WBLK = KD * 512
A_WGLR = 6 * WBLK
A_Q, A_K, A_V, A_R, A_GLR = 24832, 25856, 26880, 28928, 30976
A_HX = 32768 - NT * D
A_WOUT = 0
A_WQ = 8192
A_E1, A_AT, A_KN, A_ST = 31232, 8192, 9216, 10240
A_DQ, A_DK, A_DV = 24832, 26880, 28928
A_RT, A_QT, A_KT, A_S, A_P, A_ATT, A_ATTT, A_O, A_SQ = 31232, 10240, 12288, 14336, 15360, 16384, 16896, 18432, 20480
A_QRY, A_CAND, A_EQ, A_KEYN, A_KEYT, A_SC = 0, 16384, 20480, 24576, 26624, 28672
A_TS, A_TI, A_TIF, A_BS, A_BP, A_PA, A_PAF, A_IJ, A_GG, A_SM = (
    24576, 25088, 25600, 26112, 26368, 26624, 27136, 27648, 28160, 28416)


def trunk_kernel(nc, x, positions, norm_mix, norm_ffn, norm_final,
                 gla_w_in, gla_w_gate_up, gla_b_gate, gla_norm, gla_w_out,
                 diff_w_in, lq1, lk1, lq2, lk2, diff_norm, diff_w_out,
                 peer_w_query, peer_sub_keys, peer_u, peer_v, out):
    f32, f32r, bf16 = mybir.dt.float32, mybir.dt.float32r, mybir.dt.bfloat16
    i32, u32 = mybir.dt.int32, mybir.dt.uint32
    ALU, ACT, AX = mybir.AluOpType, mybir.ActivationFunctionType, mybir.AxisListType
    ctx = ExitStack()
    with ctx:
        def sb(name, shape, dt=f32):
            return ctx.enter_context(nc.sbuf_tensor(name, shape, dt))

        sems = {}

        def S(name):
            if name not in sems:
                sems[name] = ctx.enter_context(nc.semaphore(name))
            return sems[name]

        arena = sb("arena", [P, 32768])
        h = sb("h", [P, NT, D])
        hnT = sb("hnT", [P, KD, SEQ])
        hnT_split = sb("hnT_split", [P, 2, KD, SEQ], f32r)
        raw = sb("raw", [P, U4, D])
        split = sb("split", [P, 2, 2, D], f32r)
        wsplit = sb("wsplit", [P, 2, 2, SEQ], f32r)
        ident = sb("ident", [P, P])
        iota = sb("iota", [P, TOPK])
        iota_tok = sb("iota_tok", [P, NK, TG], bf16)
        causalT = sb("causalT", [P, P])
        causal_add = sb("causal_add", [P, P])
        slotT = sb("slotT", [P, 5, SEQ], bf16)
        onehot_j = sb("onehot_j", [P, 2, NK, TG], bf16)
        gains = sb("gains", [P, 36])
        gain_rows = sb("gain_rows", [36, P])
        gains_ffn = sb("gains_ffn", [P, 2 * KD])
        stat = sb("stat", [P, 64])
        gate_up = slotT[0:GRANK, :, :].rearrange("p a t -> p (a t)")[:, 0:2 * GH * GDK].bitcast(f32)
        pos_i = sb("pos_i", [P, NT], i32)
        bank_all = ctx.enter_context(nc.psum_tensor("banks", [P, 8 * BANK], f32))

        def bank(b, n=1):
            return bank_all[:, b * BANK:(b + n) * BANK]

        def ar(off, n):
            return arena[:, off:off + n]

        W = arena[:, :].rearrange("p (i t) -> p i t", t=SEQ)
        SEARCH_STEPS = 5 + 3 + 5 + 2 + 12 + 2
        EXP_AT = 44
        DENSE = {}
        step0 = unit0 = 0
        for L in range(2):
            if L == 0:
                unit0 += 1
            for which, n_blk, place, loaded in (("in", 6, 0, "win_loaded"), ("out", 2, A_WOUT, "wout_loaded"),
                                                ("query", 4, A_WQ, "wq_loaded")):
                DENSE[L, which] = [(step0 + KD * b, unit0 + 2 * b, place + b * WBLK, f"{loaded}{b}",
                                    which == "query" or (which == "in" and L == 0 and b < 2))
                                   for b in range(n_blk)]
                step0 += KD * n_blk
                unit0 += 2 * n_blk
            unit0 += 8
        WS = 4

        def wbuf(n, part):
            return split[:].rearrange("p a b d -> p (a b d)")[:, ((n % WS) * 2 + part) * 512:
                                                             ((n % WS) * 2 + part + 1) * 512]

        def last_step(L, which):
            return DENSE[L, which][-1][0] + KD

        def last_unit(L, which):
            return DENSE[L, which][-1][1] + 2

        QA, QI = 4, 32
        FIRST_DVE = HALF // U4 - 2
        first_dve = [NCHUNK // U4] + [FIRST_DVE + 1] + [FIRST_DVE] * 2

        def by_dve(u):
            return NCHUNK // U4 - first_dve[u]

        def plain_loads(L, u, v):
            return L * (first_dve[u] + NCHUNK // U4) + (first_dve[u] if v else 0)

        G_MIX, G_GLA, G_DIFF, G_BG, N_GAINS = 0, 16, 24, 32, 36
        ST_SS, ST_V, ST_Y, ST_T, ST_DEC = 0, 8, 16, 24, 32

        hn_words = hnT[:].rearrange("p k t -> p (k t)")
        onehot_i = hn_words[:, 0:HALF * TG // 2].bitcast(bf16).rearrange("p (i t) -> p i t", t=TG)
        onehot_g = hn_words[:, 256:256 + 2 * 3 * HALF * TG // 2].bitcast(bf16).rearrange(
            "p (b g i t) -> p b g i t", b=2, g=3, t=TG)

        g_z, g_t, g_cum, g_x = (raw[:, u, :] for u in range(4))
        g_e3, g_e4, g_e2 = g_z, g_t, g_x
        g_ones = onehot_j[:].rearrange("p b j t -> p (b j t)").bitcast(f32)
        KV_BANKS = (0, 2, 5)

        block = ctx.enter_context(nc.Block())

        win_of = [gla_w_in[0], diff_w_in[0]]
        wout_of = [gla_w_out[0], diff_w_out[0]]

        def cols(w, a, b):
            return w.rearrange("(k p) n -> p k n", p=P)[:, :, a:b]

        @block.sync
        def _(sp):
            sp.dma_start(h[:], x[0].rearrange("(m p) d -> p m d", p=P)).then_inc(S("x_loaded"), 16)
            sp.wait_ge(S("small_loaded"), 16 * 7)
            for half, loaded in ((0, "win_top_loaded"), (1, "win_bottom_loaded")):
                k0 = half * KD // 2
                sp.dma_start(ar(k0 * 512, WBLK // 2).rearrange("p (k n) -> p k n", n=512),
                             win_of[0].rearrange("(k p) n -> p k n", p=P)[:, k0:k0 + KD // 2, 0:512]
                             ).then_inc(S(loaded), 16)

            def load_u(L, c, u):
                sp.dma_start(raw[:, u, :], peer_u[L].rearrange("(c p) d -> p c d", p=P)[:, c, :]
                             ).then_inc(S(f"raw_loaded{u}"), 16)

            def load_u_blocks(L, c, u):
                chunk = peer_u[L].rearrange("(c e j) (a d) -> a j c e d", e=QA, j=QI, a=QA)
                for a in range(QA):
                    sp.dma_start(raw[a * QI:(a + 1) * QI, u, :].rearrange("j (e d) -> j e d", e=QA),
                                 chunk[a][:, c]).then_inc(S(f"raw_blocks_loaded{u}"), 16)

            def load_v(L, c, u):
                sp.dma_start(raw[:, u, :], peer_v[L].rearrange("(c p) d -> p c d", p=P)[:, c, :]
                             ).then_inc(S(f"raw_loaded{u}"), 16)

            for L in range(2):
                b = L * NCHUNK
                if L == 0:
                    sp.wait_ge(S("o_squares"), 1)
                for u in range(U4):
                    if L:
                        sp.wait_ge(S("v_lo"), 2 * (b - U4 + u + 1))
                    load_u(L, u, u)
                def next_u(c0, u, load):
                    sp.wait_ge(S("u_transposed"), c0 + (b + u - U4 + 1))
                    load(L, c0 + u, u)

                with sp.Fori(1, FIRST_DVE) as g0:
                    for u in range(U4):
                        next_u(g0 * U4, u, load_u)
                for u in range(U4):
                    next_u(FIRST_DVE * U4, u, load_u if u < 2 else load_u_blocks)
                with sp.Fori(FIRST_DVE + 1, NCHUNK // U4) as g0:
                    for u in range(U4):
                        next_u(g0 * U4, u, load_u_blocks if u else load_u)
                for u in range(U4):
                    sp.wait_ge(S("u_transposed"), b + NCHUNK - U4 + u + 1)
                    load_v(L, u, u)
                with sp.Fori(1, NCHUNK // U4) as g0:
                    c0 = g0 * U4
                    for u in range(U4):
                        sp.wait_ge(S("v_lo"), 2 * c0 + 2 * (b + u - U4 + 1))
                        load_v(L, c0 + u, u)
            sp.wait_ge(S("v_lo"), 4 * NCHUNK)
            sp.dma_start(raw[:, 0, :], norm_final.rearrange("(a n) -> a n", a=1).broadcast_to([P, D])
                         ).then_inc(S("gfinal_loaded"), 16)
            for m in range(NT):
                sp.wait_ge(S("out_ready"), m + 1)
                sp.dma_start(out[0, m * P:(m + 1) * P, :], ar(A_HX + m * D, D)).then_inc(S("out_stored"), 16)
            sp.wait_ge(S("out_stored"), 16 * NT)

        @block.gpsimd
        def _(pool):
            for L in range(2):
                if L == 0:
                    pool.memset(ident[:], 0.0).then_inc(S("const0"), 1)
                    pool.wait_ge(S("const0"), 1)
                    pool.affine_select(out=ident[:], in_=ident[:], compare_op=ALU.not_equal, fill=1.0,
                                       base=0, pattern=[[-1, P]], channel_multiplier=1
                                       ).then_inc(S("ident_ready"), 1)
                    pool.dma_start(ar(A_WGLR, KD * GRANK).rearrange("p (k n) -> p k n", k=KD),
                                   cols(win_of[0], 3072, 3088)).then_inc(S("glr_loaded"), 16)
                    pool.wait_ge(S("x_loaded"), 16)
                    pool.wait_ge(S("small_loaded"), 16 * 7)
                for blk in range(6):
                    if L:
                        pool.wait_ge(S("w_lo"), 16 * (blk + 1))
                    if L or blk:
                        pool.dma_start(ar(blk * WBLK, WBLK).rearrange("p (k n) -> p k n", k=KD),
                                       cols(win_of[L], 512 * blk, 512 * blk + 512)
                                       ).then_inc(S(f"win_loaded{blk}"), 16)
                if L == 0:
                    pool.memset(causalT[:], 1.0).then_inc(S("const0"), 1)
                    pool.memset(causal_add[:], 0.0).then_inc(S("const0"), 1)
                    pool.iota(iota[:], [[1, TOPK]], base=0, channel_multiplier=0,
                              allow_small_or_imprecise_dtypes=True).then_inc(S("const"), 1)
                    pool.iota(iota_tok[:], [[1, NK], [0, TG]], base=0, channel_multiplier=0,
                              allow_small_or_imprecise_dtypes=True).then_inc(S("const"), 1)
                    pool.wait_ge(S("const0"), 3)
                    pool.affine_select(out=causalT[:], in_=causalT[:], compare_op=ALU.is_ge, fill=0.0,
                                       base=0, pattern=[[1, P]], channel_multiplier=-1
                                       ).then_inc(S("const1"), 1)
                    pool.affine_select(out=causal_add[:], in_=causal_add[:], compare_op=ALU.is_ge, fill=NEG,
                                       base=0, pattern=[[-1, P]], channel_multiplier=1
                                       ).then_inc(S("const"), 1)
                    pool.wait_ge(S("const1"), 1)
                    pool.memset(causalT[0:GCH, GCH:P], 0.0).then_inc(S("const"), 1)
                if L:
                    pool.wait_ge(S("hx_transposed"), 3 * KD // 2)
                    for j, lq in enumerate((lq1, lk1, lq2, lk2)):
                        pool.dma_start(ar(A_RT + 256 + 64 * j, DDH), lq.broadcast_to([P, DDH])
                                       ).then_inc(S("lam_loaded"), 16)
                pool.wait_ge(S("ws_lo"), DENSE[L, "in"][1][0] + KD)
                for blk in range(2):
                    pool.dma_start(ar(A_WOUT + blk * WBLK, WBLK).rearrange("p (k n) -> p k n", k=KD),
                                   cols(wout_of[L], 512 * blk, 512 * blk + 512)
                                   ).then_inc(S(f"wout_loaded{blk}"), 16)
                if L == 0:
                    pool.wait_ge(S("gla_o_done"), 4)
                else:
                    pool.wait_ge(S("o_transposed"), KD // 2 * (L + 1))
                for blk in range(4):
                    pool.dma_start(ar(A_WQ + blk * WBLK, WBLK).rearrange("p (k n) -> p k n", k=KD),
                                   peer_w_query[L].rearrange("(p k) n -> p k n", k=KD)[:, :, 512 * blk:512 * blk + 512]
                                   ).then_inc(S(f"wq_loaded{blk}"), 16)
                    if blk == 1:
                        pool.dma_start(ar(A_KEYN, HP * P).rearrange("p (g d) -> p g d", g=HP),
                                       peer_sub_keys[L].rearrange("h q n d -> n (h q) d")
                                       ).then_inc(S("keys_loaded"), 16)

        @block.tensor
        def _(pe):
            pe.wait_ge(S("ident_ready"), 1)
            pe.wait_ge(S("small_loaded"), 16 * 7)
            nc.tensor.transpose(bank(7)[:, 0:N_GAINS], gain_rows[:], ident[0:N_GAINS, 0:N_GAINS]
                                ).then_inc(S("gains_transposed"), 1)

            def transposes(ready, n, src, done):
                for m, b in ((0, 0), (0, 1), (1, 0), (0, 2), (1, 1), (0, 3), (1, 2), (1, 3)):
                    if b == 0:
                        pe.wait_ge(S(ready), n + m + 1)
                    for k in (2 * b, 2 * b + 1):
                        last = nc.tensor.transpose(
                            bank_all[:, k * SEQ + m * P:k * SEQ + (m + 1) * P],
                            ar(src + m * D + k * P, P), ident[:])
                    if m:
                        last.then_inc(S(done), 1)

            def norm_transposes(n):
                transposes("hx_ready", NT * n, A_HX, "hx_transposed")

            def mixer_out(L):
                transposes("o_ready", NT * L, A_R if L == 0 else A_O, "o_transposed")
                dense(L, "out")

            def dense(L, which, beside={}):
                inputs = KD // 2 * (3 * L + ("in", "out", "query").index(which))
                for blk, (st, un, place, loaded, transposed_out) in enumerate(DENSE[L, which]):
                    if un >= 3:
                        pe.wait_ge(S("unit_evicted"), un - 2)
                    for k in range(KD):
                        pe.wait_ge(S("ws_lo"), st + k + 1)
                        pe.wait_ge(S("in_lo"), inputs + k // 2 + 1)
                        for j in range(2 * NT if transposed_out else NT):
                            for n, (a, b) in enumerate(((0, 0), (0, 1), (1, 0))):
                                if transposed_out:
                                    last = nc.tensor.matmul(
                                        bank(4 + (un + j // 2) % 4)[:, (j % 2) * SEQ:(j % 2 + 1) * SEQ],
                                        wbuf(st + k, a)[:, j * P:(j + 1) * P], hnT_split[:, b, k, :],
                                        start=(k == 0 and n == 0 and j % 2 == 0), stop=(k == KD - 1 and n == 2),
                                        skip_group_check=True)
                                else:
                                    last = nc.tensor.matmul(
                                        bank(4 + (un + j) % 4), hnT_split[:, b, k, j * P:(j + 1) * P],
                                        wbuf(st + k, a), start=(k == 0 and n == 0),
                                        stop=(k == KD - 1 and n == 2))
                        last.then_inc(S("ws_used"), 1)
                        if (blk, k) in beside:
                            beside[blk, k]()
                    nonlocal unit
                    unit = un + 2

            def gla_gate_inner():
                pe.wait_ge(S("hnT_ready"), KD // 2)
                pe.wait_ge(S("glr_loaded"), 16)
                for k in range(KD):
                    last = nc.tensor.matmul(bank(4)[0:GRANK, 0:SEQ], ar(A_WGLR + k * GRANK, GRANK), hnT[:, k, :],
                                            start=(k == 0), stop=(k == KD - 1))
                last.then_inc(S("gate_inner_done"), 1)

            def gla_gate():
                pe.wait_ge(S("unit_evicted"), 1)
                for hh in range(GH):
                    last = nc.tensor.matmul(bank_all[:, hh * SEQ:(hh + 1) * SEQ],
                                            gate_up[:, hh * GDK:(hh + 1) * GDK],
                                            ar(A_GLR, SEQ)[0:GRANK, :], start=True, stop=True)
                last.then_inc(S("gate_done"), 1)

            def gla_scores():
                pe.wait_ge(S("klT_ready"), 1)
                for m in range(NT):
                    for hh in range(GH):
                        last = nc.tensor.transpose(bank(2 + m)[:, hh * P:(hh + 1) * P],
                                                   g_e4[:, hh * SEQ + m * P:hh * SEQ + (m + 1) * P], ident[:])
                last.then_inc(S("kn_transposed"), 1)
                for m in range(NT):
                    for hh in range(GH):
                        last = nc.tensor.matmul(bank(m)[:, hh * P:(hh + 1) * P],
                                                g_e2[:, hh * SEQ + m * P:hh * SEQ + (m + 1) * P],
                                                ar(A_E1 + hh * SEQ + m * P, P), start=True, stop=True)
                last.then_inc(S("aT_done"), 1)

            def gla_kv():
                pe.wait_ge(S("kn_ready"), 1)
                pe.wait_ge(S("aT_ready"), 1)
                pe.wait_ge(S("unit_evicted"), DENSE[0, "in"][4][1] + 2)
                for n in range(NCH - 1):
                    m, r0 = n // 2, GCH * (n % 2)
                    for hh in range(GH):
                        o = KV_BANKS[n] * BANK + hh * GDV
                        last = nc.tensor.matmul(
                            bank_all[:, o:o + GDV],
                            arena[r0:r0 + GCH, A_KN + (m * GH + hh) * P:A_KN + (m * GH + hh + 1) * P],
                            arena[r0:r0 + GCH, A_V + m * D + hh * GDV:A_V + m * D + (hh + 1) * GDV],
                            start=True, stop=True)
                last.then_inc(S("kv_done"), 1)

            def gla():
                pe.wait_ge(S("states_ready"), 1)
                for b in (1, 2, 3, 0):
                    if b in (3, 0):
                        pe.wait_ge(S("unit_evicted"), last_unit(0, "in") - (b == 3))
                    for m, hh in ((b // 2, 2 * (b % 2)), (b // 2, 2 * (b % 2) + 1)):
                        o = bank(4 + b)
                        f = (hh % 2) * 256
                        parts = [n for n in (2 * m, 2 * m + 1) if n > 0]
                        nc.tensor.matmul(o[:, f:f + 256], ar(A_AT + (m * GH + hh) * P, P),
                                         ar(A_V + m * D + hh * GDV, GDV), start=True, stop=False,
                                         skip_group_check=True)
                        for n in parts:
                            r0 = GCH * (n % 2)
                            last = nc.tensor.matmul(
                                o[r0:r0 + GCH, f:f + 256],
                                g_e3[:, hh * SEQ + n * GCH:hh * SEQ + (n + 1) * GCH],
                                ar(A_ST + ((n - 1) * GH + hh) * GDV, GDV), start=False, stop=(n == parts[-1]),
                                skip_group_check=True)
                    last.then_inc(S("gla_o_done"), 1)

            def qk_transposes(s, src):
                pe.wait_ge(S("rope_ready"), s + 1)
                if s:
                    pe.wait_ge(S("qk_ready"), s)
                for hh in range(DH):
                    for m in range(NT):
                        last = nc.tensor.transpose(bank_all[:, hh * SEQ + m * P:hh * SEQ + (m + 1) * P],
                                                   ar(src + m * D + hh * P, P), ident[:])
                last.then_inc(S("qk_transposed"), 1)

            def diff():
                pe.wait_ge(S("qk_ready"), 2)

                def scores(n):
                    hh, m = n // NT, n % NT
                    if n >= 1:
                        pe.wait_ge(S("s_evicted"), n)
                    for half in range(2):
                        r0 = half * DDH
                        last = nc.tensor.matmul(
                            bank(half)[:, 0:(m + 1) * P],
                            arena[r0:r0 + DDH, A_QT + hh * SEQ + m * P:A_QT + hh * SEQ + (m + 1) * P],
                            arena[r0:r0 + DDH, A_KT + hh * SEQ:A_KT + hh * SEQ + (m + 1) * P],
                            start=True, stop=True)
                    last.then_inc(S("s_done"), 1)

                def attn_transposes(n):
                    pe.wait_ge(S("attn_ready"), n + 1)
                    if n >= 2:
                        pe.wait_ge(S("attnT_ready"), n - 1)
                    for kt in range(n % NT + 1):
                        last = nc.tensor.transpose(bank(2 + n % 2)[:, kt * P:(kt + 1) * P],
                                                   ar(A_ATT + (n % 2) * 256 + kt * P, P), ident[:])
                    last.then_inc(S("attn_transposed"), 1)

                def outputs(n):
                    hh, m = n // NT, n % NT
                    pe.wait_ge(S("attnT_ready"), n + 1)
                    o = bank(4 + 2 * m + hh // 4)[:, (hh % 4) * P:(hh % 4 + 1) * P]
                    for kt in range(m + 1):
                        last = nc.tensor.matmul(o, ar(A_ATTT + (n % 2) * 256 + kt * P, P),
                                                ar(A_DV + kt * D + hh * DDV, DDV),
                                                start=(kt == 0), stop=(kt == m))
                    last.then_inc(S("diff_o_done"), 1)

                scores(0)
                scores(1)
                pe.wait_ge(S("unit_evicted"), last_unit(1, "in"))
                for n in range(DH * NT):
                    if n + 2 < DH * NT:
                        scores(n + 2)
                    attn_transposes(n)
                    if n:
                        outputs(n - 1)
                outputs(DH * NT - 1)

            def peer_search(L):
                nonlocal unit
                dense(L, "query", {(3, 1): lambda: key_transposes(L)})
                pe.wait_ge(S("keysT_ready"), L + 1)
                u_transposes(L, 0, 0)
                for n in range(4 * NT):
                    q, m = n // NT, n % NT
                    pe.wait_ge(S("unit_evicted"), unit - 3)
                    for g in range(4 * q, 4 * q + 4):
                        last = nc.tensor.matmul(bank(4 + unit % 4)[:, (g % 4) * P:(g % 4 + 1) * P],
                                                ar(A_QRY + g * SEQ + m * P, P), ar(A_KEYT + g * P, P),
                                                start=True, stop=True)
                    last.then_inc(S("scores_done"), 1)
                    unit += 1

            def key_transposes(L):
                pe.wait_ge(S("keys_loaded"), 16 * (L + 1))
                for g in range(HP):
                    last = nc.tensor.transpose(bank_all[:, g * P:(g + 1) * P], ar(A_KEYN + g * P, P), ident[:])
                last.then_inc(S("keys_transposed"), 1)

            def u_transposes(L, c0, u):
                b = L * NCHUNK
                pe.wait_ge(S(f"raw_loaded{u % U4}"), 4 * c0 + (16 * (u // U4) + 16 + 16 * plain_loads(L, u % U4, False)))
                if not isinstance(c0, int) or b + c0 + u - 1 > 0:
                    pe.wait_ge(S("u_lo"), c0 + (b + u - 1))
                for k in range(KD):
                    last = nc.tensor.transpose(bank(2 * (u % 2), 2)[:, k * P:(k + 1) * P],
                                               raw[:, u % U4, :].rearrange("p (c k) -> p k c", k=KD)[:, k],
                                               ident[:])
                last.then_inc(S("u_transposed"), 1)

            def slot_transposes(L):
                pe.wait_ge(S("chosen"), L + 1)
                for v, src in enumerate((A_IJ, A_IJ + NT * SLOTS, A_GG)):
                    for m in range(NT):
                        last = nc.tensor.transpose(bank_all[:, 6 * BANK + v * SEQ + m * P:6 * BANK + v * SEQ + (m + 1) * P],
                                                   ar(src + m * SLOTS, P), ident[:])
                last.then_inc(S("slots_transposed"), 1)

            def peer_up(L):
                b = L * NCHUNK

                def products(c0, u):
                    pe.wait_ge(S("u_lo"), c0 + (b + u + 1))
                    if not isinstance(c0, int) or b + c0 + u - 1 > 0:
                        pe.wait_ge(S("gelu_done"), c0 + (b + u - 1))
                    n = 0
                    for k in range(KD):
                        for s, t in ((0, 0), (0, 1), (1, 0)):
                            last = nc.tensor.matmul(bank(4 + u % 2)[:, 0:SEQ],
                                                    split[:, u % 2, s, k * P:(k + 1) * P],
                                                    hnT_split[:, t, k, :], start=(n == 0), stop=(n == 23))
                            n += 1
                    last.then_inc(S("a_done"), 1)

                def body(c0, last_group, p0=None):
                    for u in range(U4):
                        if u == U4 - 1 and not last_group or plain or u == 0 and last_plain:
                            u_transposes(L, c0, u + 1)
                        if last_group and u == U4 - 1:
                            gates(L, 0, p0, 1)
                        products(c0, u)
                        if u % 2 and second and not (last_group and u == U4 - 1):
                            gates(L, 0, p0, u // 2)

                second = last_plain = False
                plain = True
                pe.wait_ge(S("unit_evicted"), unit)
                body(0, False)
                with pe.Fori(1, FIRST_DVE) as g0:
                    body(g0 * U4, False)
                plain, last_plain = False, True
                body(FIRST_DVE * U4, False)
                last_plain = False
                slot_transposes(L)
                body(HALF - U4, False)
                second = True
                body(HALF, False, 0)
                with pe.Fori(0, (NCHUNK - HALF) // U4 // 2 - 1) as g0:
                    for g in (1, 2):
                        body(g0 * (2 * U4) + (HALF + g * U4), False, g0 * 4 + 2 * g)
                body(NCHUNK - U4, True, NGRP - 2)

            def gates(L, half, p0, r):
                b = (2 * L + half) * NGRP
                pe.wait_ge(S("onehots_ready"), p0 + (b + r + 1))
                if not isinstance(p0, int) or b + p0 + r - 1 > 0:
                    pe.wait_ge(S("w_multiplied"), p0 + (b + r - 1))
                for k in range(TG):
                    for g in range(3):
                        last = nc.tensor.matmul(bank(6 + r)[:, k * HALF:(k + 1) * HALF],
                                                onehot_j[:, r, :, k], onehot_g[:, r, g, :, k],
                                                start=(g == 0), stop=(g == 2))
                last.then_inc(S("gates_done"), 1)

            def peer_down(L):
                b = L * NCHUNK

                def chunk(c0, u, first, final):
                    pe.wait_ge(S("w_lo"), c0 + (b + u + 1))
                    for k in range(KD):
                        if k % 4 == 0:
                            pe.wait_ge(S("v_lo"), 2 * c0 + (2 * (b + u) + 1 + k // 4))
                        for n, (s, t) in enumerate(((0, 0), (0, 1), (1, 0))):
                            last = nc.tensor.matmul(bank_all[:, k * SEQ:(k + 1) * SEQ],
                                                    split[:, u % 2, s, k * P:(k + 1) * P],
                                                    wsplit[:, u % 2, t, :],
                                                    start=(first and k % 2 == 0 and n == 0),
                                                    stop=(final and n == 2), skip_group_check=True)
                    last.then_inc(S("v_used"), 1)

                for u in range(U4):
                    chunk(0, u, u == 0, False)
                    if u % 2:
                        gates(L, 1, 0, u // 2)
                with pe.Fori(1, HALF // U4 - 1) as g0:
                    for u in range(U4):
                        chunk(g0 * U4, u, False, False)
                        if u % 2:
                            gates(L, 1, g0 * 2, u // 2)
                for u in range(U4):
                    chunk(HALF - U4, u, False, False)
                    if u in (1, 2):
                        gates(L, 1, NGRP - 2, u - 1)
                with pe.Fori(HALF // U4, NCHUNK // U4 - 1) as g0:
                    for u in range(U4):
                        chunk(g0 * U4, u, False, False)
                for u in range(U4):
                    chunk(NCHUNK - U4, u, False, u == U4 - 1)
                for half in range(2):
                    for k in range(half * KD // 2, (half + 1) * KD // 2):
                        if k % 2 == 0:
                            pe.wait_ge(S("ffT_ready"), 4 * L + k // 2 + 1)
                        for m in range(NT):
                            last = nc.tensor.transpose(bank(4, 4)[:, m * D + k * P:m * D + (k + 1) * P],
                                                       hnT[:, k, m * P:(m + 1) * P], ident[:])
                    last.then_inc(S("ff_transposed"), 1)

            unit = 0
            for L in range(2):
                norm_transposes(2 * L)
                if L == 0:
                    dense(L, "in", {(0, 3): gla_gate_inner, (0, 7): gla_gate, (4, 1): gla_scores, (5, 3): gla_kv})
                    gla()
                else:
                    dense(L, "in", {(4, 3): lambda: qk_transposes(0, A_DQ), (5, 4): lambda: qk_transposes(1, A_DK)})
                    diff()
                mixer_out(L)
                norm_transposes(2 * L + 1)
                peer_search(L)
                peer_up(L)
                peer_down(L)

        @block.scalar
        def _(act):
            A = nc.scalar.activation
            sl = S("small_loaded")
            for r0, src in ((0, norm_mix.rearrange("l (c p) -> (l c) p", p=P)),
                            (G_GLA, gla_norm[0].rearrange("h (c p) -> (h c) p", p=P)),
                            (G_DIFF, diff_norm[0]),
                            (G_BG, gla_b_gate.rearrange("l (c p) -> (l c) p", p=P))):
                act.dma_start(gain_rows[r0:r0 + src.shape[0], :], src).then_inc(sl, 16)
            for L in range(2):
                act.dma_start(gains_ffn[:, L * KD:(L + 1) * KD], norm_ffn[L].rearrange("(p k) -> p k", k=KD)
                              ).then_inc(sl, 16)
            act.dma_start(gate_up, gla_w_gate_up[0]).then_inc(sl, 16)
            act.dma_start(pos_i[:], positions.rearrange("o (m p) -> p (o m)", p=P),
                          allow_slow_non_contiguous=True).then_inc(S("pos_loaded"), 16)
            def norm(n):
                act.preload_act_table(ACT.Sqrt)
                if n == 0:
                    act.wait_ge(S("x_loaded"), 16)
                elif n % 2:
                    act.wait_ge(S("unit_evicted"), last_unit(n // 2, "out") - 1)
                else:
                    act.wait_ge(S("h_updated"), 4 * (n // 2) - 1)
                A(ar(A_HX, D), h[:, 0, :], ACT.Square, accum_out=stat[:, ST_SS:ST_SS + 1]
                  ).then_inc(S("squares_summed"), 1)
                act.wait_ge(S("mean_ready"), n + 1 + (n > 0) + (n > 2))
                A(stat[:, ST_T:ST_T + NT], stat[:, ST_V:ST_V + NT], ACT.Sqrt).then_inc(S("root_ready"), 1)

            def gained(gain, transposed, done, n, banks):
                for b in banks:
                    act.wait_ge(S(transposed), 4 * n + b + 1)
                    for k in (2 * b, 2 * b + 1):
                        last = A(hnT[:, k, :], bank_all[:, k * SEQ:(k + 1) * SEQ], ACT.Copy,
                                 scale=gain[:, k:k + 1])
                    last.then_inc(S(done), 1)
                    act.wait_ge(S(done), 4 * n + b + 1)
                    A(hnT_split[:, 0, 2 * b:2 * b + 2], hnT[:, 2 * b:2 * b + 2], ACT.Copy).then_inc(S("in_hi"), 1)

            def normed_T(n):
                gain = gains_ffn[:, n // 2 * KD:] if n % 2 else gains[:, G_MIX + n // 2 * KD:]
                args = gain, "hx_transposed", "hnT_ready", n
                if n == 0:
                    act.wait_ge(S("gains_transposed"), 1)
                    A(gains[:], bank(7)[:, 0:N_GAINS], ACT.Copy).then_inc(S("gains_ready"), 1)
                    act.wait_ge(S("gains_ready"), 1)
                    gained(*args, (0,))
                    first_high_parts(0, "in")
                    gained(*args, (1, 2, 3))
                else:
                    first_high_parts(n // 2, "query" if n % 2 else "in")
                    gained(*args, range(4))

            def mixer_out(L):
                first_high_parts(L, "out")
                gained(gains[:, G_DIFF if L else G_GLA:], "o_transposed", "oT_ready", L, range(4))
                dense(L, "out", None)

            def high_part(L, which, b, k):
                st, _, place, loaded, _ = DENSE[L, which][b]
                if which == "in" and b == 0:
                    if L == 0 and k % (KD // 2) == 0:
                        act.wait_ge(S("win_bottom_loaded" if k else "win_top_loaded"), 16)
                    elif L and k == 0:
                        act.wait_ge(S(loaded), 16)
                elif k == 0:
                    act.wait_ge(S(loaded), 16 * (L + 1))
                if st + k >= WS:
                    act.wait_ge(S("ws_used"), st + k - WS + 1)
                A(wbuf(st + k, 0), ar(place + k * 512, 512), ACT.Copy).then_inc(S("ws_hi"), 1)

            def first_high_parts(L, which):
                for k in range(WS):
                    high_part(L, which, 0, k)

            def dense(L, which, place_of, beside={}):
                blocks = DENSE[L, which]

                def outputs(b):
                    st, un = blocks[b][0], blocks[b][1]
                    act.wait_ge(S("ws_used"), st + KD)
                    for j in range(2):
                        dst, scale, function = place_of(b, j)
                        A(dst, bank(4 + (un + j) % 4), function, scale=scale).then_inc(S("unit_evicted"), 1)

                for b, (st, un, place, loaded, _) in enumerate(blocks):
                    for k in range(KD):
                        if b or k >= WS:
                            high_part(L, which, b, k)
                        if k == 2 and b and place_of:
                            outputs(b - 1)
                        if (b, k) in beside:
                            beside[b, k]()
                if place_of:
                    outputs(len(blocks) - 1)

            def projections(L):
                def place_of(b, j):
                    if L == 0:
                        if b < 2:
                            return ar((A_Q, A_K)[b] + j * 512, 512), (GDK ** -0.5, 1.0)[b], ACT.Copy
                        return (ar((A_V, A_R)[b // 2 - 1] + j * D + (b % 2) * 512, 512), 1.0,
                                ACT.Copy if b < 4 else ACT.Silu)
                    return (ar((A_DQ, A_DK, A_DV)[b // 2] + j * D + (b % 2) * 512, 512),
                            DDH ** -0.5 if b < 2 else 1.0, ACT.Copy)

                if L == 0:
                    dense(L, "in", place_of, {(0, 6): gate_inner_out, (1, 3): gla_abs, (1, 4): gla_exp, (1, 7): gla_ln,
                                              (2, 5): lambda: gla_exp12(0), (2, 6): lambda: gla_exp12(1),
                                              (2, 7): gla_exp3, (3, 0): gla_exp4, (4, 5): gla_keys})
                else:
                    dense(L, "in", place_of, {(2, 4): sincos, (2, 6): lam_exps,
                                              (4, 6): lambda: qk_out(0, A_QT), (5, 7): lambda: qk_out(1, A_KT)})

            def gate_inner_out():
                act.wait_ge(S("gate_inner_done"), 1)
                A(arena[0:GRANK, A_GLR:A_GLR + SEQ], bank(4)[0:GRANK, 0:SEQ], ACT.Copy
                  ).then_inc(S("unit_evicted"), 1)

            def gla_abs():
                act.wait_ge(S("z_ready"), 1)
                A(g_t, g_z, ACT.Abs).then_inc(S("act_chain"), 1)

            def gla_exp():
                act.wait_ge(S("act_chain"), 1)
                A(g_t, g_t, ACT.Exp, scale=-1.0).then_inc(S("act_chain"), 1)

            def gla_ln():
                act.wait_ge(S("act_chain"), 2)
                A(g_t, g_t, ACT.Ln, bias=1.0).then_inc(S("ln_ready"), 1)

            def gla_exp12(sign):
                act.wait_ge(S("x1_ready"), 1)
                if sign:
                    act.wait_ge(S("exps_ready"), 1)
                A(g_e2 if sign else ar(A_E1, 1024), g_x, ACT.Exp, scale=(-1 if sign else 1) / GTAU
                  ).then_inc(S("exps_ready"), 1)

            def gla_exp3():
                A(g_e3, g_cum, ACT.Exp, scale=1 / GTAU).then_inc(S("exps_ready"), 1)
                last_cum = g_cum.rearrange("p (g c) -> p g c", c=GCH)[:, :, GCH - 1]
                A(stat[:, ST_DEC:ST_DEC + GH * NCH], last_cum, ACT.Exp, scale=1 / GTAU).then_inc(S("exps_ready"), 1)

            def gla_exp4():
                act.wait_ge(S("x2_ready"), 1)
                A(g_e4, g_t, ACT.Exp, scale=1 / GTAU).then_inc(S("exps_ready"), 1)

            def gla_keys():
                act.wait_ge(S("kn_transposed"), 1)
                A(ar(A_KN, 1024), bank(2, 2), ACT.Copy).then_inc(S("kn_ready"), 1)

            def gla():
                act.preload_act_table(ACT.Sqrt)
                for n, b in enumerate((1, 2, 3, 0)):
                    act.wait_ge(S("gla_o_done"), n + 1)
                    for j in (2 * b, 2 * b + 1):
                        last = A(raw[:, 2 + j // 4, j % 4 * GDV:(j % 4 + 1) * GDV],
                                 bank_all[:, 4 * BANK + j * GDV:4 * BANK + (j + 1) * GDV], ACT.Square,
                                 accum_out=stat[:, ST_SS + j:ST_SS + j + 1])
                last.then_inc(S("o_squares"), 1)
                act.wait_ge(S("mean_ready"), 2)
                A(stat[:, ST_T:ST_T + 8], stat[:, ST_V:ST_V + 8], ACT.Sqrt).then_inc(S("root_ready"), 1)

            def sincos():
                act.wait_ge(S("angles_ready"), 1)
                A(ar(A_RT, 64), ar(A_RT, 64), ACT.Sin).then_inc(S("sincos_ready"), 1)

            def lam_exps():
                act.wait_ge(S("lam_dots"), 1)
                A(stat[:, 50:52], stat[:, 48:50], ACT.Exp).then_inc(S("lam_exps"), 1)

            def qk_out(s, dst):
                act.wait_ge(S("qk_transposed"), s + 1)
                A(ar(dst, 2048), bank(0, 4), ACT.Copy).then_inc(S("qk_ready"), 1)

            def diff():
                def exps(n):
                    w = (n % NT + 1) * P
                    act.wait_ge(S("max_ready"), n + 1)
                    if n >= 2:
                        act.wait_ge(S("attn_ready"), n - 1)
                    for half in range(2):
                        o = A_S + (n % 2) * 512 + half * 256
                        last = A(ar(A_P + (n % 2) * 512 + half * 256, w), ar(o, w), ACT.Exp,
                                 bias=stat[:, 52 + (n % 2) * 2 + half:53 + (n % 2) * 2 + half],
                                 accum_out=stat[:, 56 + (n % 2) * 2 + half:57 + (n % 2) * 2 + half])
                    last.then_inc(S("exp_ready"), 1)

                def squares(part):
                    for m in range(NT):
                        for hh in range(part * DH // 2, (part + 1) * DH // 2):
                            j = m * DH + hh
                            last = A(ar(A_SQ + j * DDV, DDV), bank_all[:, 4 * BANK + j * DDV:4 * BANK + (j + 1) * DDV],
                                     ACT.Square, accum_out=stat[:, ST_SS + j:ST_SS + j + 1])
                    return last

                exps(0)
                for n in range(DH * NT):
                    w = (n % NT + 1) * P
                    if n + 1 < DH * NT:
                        exps(n + 1)
                    if n == DH * NT // 2 + 2:
                        squares(0)
                    act.wait_ge(S("attn_transposed"), n + 1)
                    if n >= 2:
                        act.wait_ge(S("diff_o_done"), n - 1)
                    A(ar(A_ATTT + (n % 2) * 256, w), bank(2 + n % 2)[:, 0:w], ACT.Copy).then_inc(S("attnT_ready"), 1)
                act.preload_act_table(ACT.Sqrt)
                act.wait_ge(S("diff_o_done"), DH * NT)
                squares(1).then_inc(S("o_squares"), 1)
                act.wait_ge(S("mean_ready"), 5)
                A(stat[:, 48:64], stat[:, 16:32], ACT.Sqrt).then_inc(S("root_ready"), 1)

            def peer_search(L):
                dense(L, "query", lambda b, j: (ar(A_QRY + (2 * b + j) * 512, 512), 1.0, ACT.Copy),
                      {(3, 4): lambda: keys_out(L)})
                act.wait_ge(S("ws_used"), last_step(L, "query"))
                u_hi(L, 0, 0)
                for n in range(4 * NT):
                    q, m = n // NT, n % NT
                    act.wait_ge(S("scores_done"), 8 * L + n + 1)
                    A(ar(A_SC + m * HP * NK + q * 512, 512), bank(4 + (last_unit(L, "query") + n) % 4),
                      ACT.Copy).then_inc(S("unit_evicted"), 1)

            def keys_out(L):
                act.wait_ge(S("keys_transposed"), L + 1)
                A(ar(A_KEYT, HP * P), bank(0, 4), ACT.Copy).then_inc(S("keysT_ready"), 1)

            def u_hi(L, c0, u):
                b = L * NCHUNK
                act.wait_ge(S("u_transposed"), c0 + (b + u + 1))
                if not isinstance(c0, int) or b + c0 + u - 1 > 0:
                    act.wait_ge(S("a_done"), c0 + (b + u - 1))
                A(split[:, u % 2, 0, :], bank(2 * (u % 2), 2), ACT.Copy).then_inc(S("u_hi"), 1)

            def peer_up(L):
                b = L * NCHUNK
                act.preload_act_table(ACT.Gelu)

                def gelu(c0, u):
                    act.wait_ge(S("a_done"), c0 + (b + u + 1))
                    A(W[:, c0 + u, :], bank(4 + u % 2)[:, 0:SEQ], ACT.Gelu).then_inc(S("gelu_done"), 1)

                def body(c0, last_group, reload=False):
                    for u in range(U4):
                        if not (last_group and u == U4 - 1):
                            u_hi(L, c0, u + 1)
                        if reload and u == 0:
                            act.preload_act_table(ACT.Gelu)
                        if last_group and u == U4 - 1:
                            act.wait_ge(S("w_multiplied"), (2 * L + 1) * NGRP)
                            v_chunk(L, 0, 0)
                        gelu(c0, u)

                body(0, False)
                with act.Fori(1, EXP_AT // U4) as g0:
                    body(g0 * U4, False)
                act.wait_ge(S("gate_args"), L + 1)
                A(ar(A_GG, NT * SLOTS), ar(A_GG, NT * SLOTS), ACT.Exp).then_inc(S("gate_exps"), 1)
                body(EXP_AT, False, reload=True)
                body(EXP_AT + U4, False)
                with act.Fori(0, (NCHUNK - EXP_AT) // U4 // 2 - 1) as g0:
                    for g in (2, 3):
                        body(g0 * (2 * U4) + (EXP_AT + g * U4), False)
                body(NCHUNK - U4, True)

            def v_chunk(L, c0, u):
                b = L * NCHUNK
                act.wait_ge(S(f"raw_loaded{u}"), 4 * c0 + (16 + 16 * plain_loads(L, u, True)))
                if isinstance(c0, int) and c0 + u < 2:
                    act.wait_ge(S("a_done"), b + NCHUNK - 1 + u)
                if not isinstance(c0, int) or b + c0 + u - 1 > 0:
                    act.wait_ge(S("v_used"), c0 + (b + u - 1))
                A(wsplit[:, u % 2, 0, :], W[:, c0 + u, :], ACT.Copy).then_inc(S("w_hi"), 1)
                for f in range(2):
                    A(split[:, u % 2, 0, f * 512:(f + 1) * 512], raw[:, u, f * 512:(f + 1) * 512],
                      ACT.Copy).then_inc(S("v_hi"), 1)

            def peer_down(L):
                b = L * NCHUNK
                for u in range(1, U4):
                    v_chunk(L, 0, u)
                with act.Fori(1, HALF // U4) as g0:
                    for u in range(U4):
                        v_chunk(L, g0 * U4, u)
                act.wait_ge(S("w_multiplied"), (2 * L + 2) * NGRP)
                with act.Fori(HALF // U4, NCHUNK // U4) as g0:
                    for u in range(U4):
                        v_chunk(L, g0 * U4, u)
                act.wait_ge(S("v_used"), b + NCHUNK)
                for k in range(0, KD, 2):
                    A(hnT[:, k:k + 2], bank(k // 2), ACT.Copy).then_inc(S("ffT_ready"), 1)

            for L in range(2):
                norm(2 * L)
                normed_T(2 * L)
                projections(L)
                gla() if L == 0 else diff()
                mixer_out(L)
                norm(2 * L + 1)
                normed_T(2 * L + 1)
                peer_search(L)
                peer_up(L)
                peer_down(L)
            norm(4)

        @block.vector
        def _(dve):
            V = nc.vector
            chain = 0

            def link(ins):
                nonlocal chain
                chain += 1
                ins.then_inc(S("dve_chain"), 1)
                dve.wait_ge(S("dve_chain"), chain)

            def rsqrt(ss, v, y, t, n, width, roots):
                V.tensor_scalar(stat[:, v:v + n], stat[:, ss:ss + n], 1.0 / width, EPS, ALU.mult, ALU.add
                                ).then_inc(S("mean_ready"), 1)
                dve.wait_ge(S("mean_ready"), roots)
                dve.wait_ge(S("root_ready"), roots)
                link(V.reciprocal(stat[:, y:y + n], stat[:, t:t + n]))
                link(V.scalar_tensor_tensor(out=stat[:, t:t + n], in0=stat[:, y:y + n], scalar=-0.5,
                                            in1=stat[:, y:y + n], op0=ALU.mult, op1=ALU.mult))
                link(V.tensor_tensor(stat[:, t:t + n], stat[:, t:t + n], stat[:, v:v + n], ALU.mult))
                link(V.scalar_tensor_tensor(out=stat[:, y:y + n], in0=stat[:, t:t + n], scalar=1.5,
                                            in1=stat[:, y:y + n], op0=ALU.add, op1=ALU.mult))

            def norm(n):
                if n == 0:
                    dve.wait_ge(S("x_loaded"), 16)
                link(V.tensor_tensor_reduce(out=ar(A_HX + D, D), in0=h[:, 1, :], in1=h[:, 1, :], scale=1.0,
                                            scalar=0.0, op0=ALU.mult, op1=ALU.add,
                                            accum_out=stat[:, ST_SS + 1:ST_SS + 2]))
                dve.wait_ge(S("squares_summed"), n + 1)
                rsqrt(ST_SS, ST_V, ST_Y, ST_T, NT, D, n + 1 + (n > 0) + (n > 2))
                if n == 4:
                    return
                for m in range(NT):
                    dst, src = ar(A_HX + m * D, D), h[:, m, :]
                    if n % 2:
                        dst = dst.rearrange("p (k c) -> p k c", k=KD)
                        src = src.rearrange("p (c k) -> p k c", k=KD)
                    V.tensor_scalar(dst, src, stat[:, ST_Y + m:ST_Y + m + 1], None, ALU.mult
                                    ).then_inc(S("hx_ready"), 1)
                if n == 0:
                    in_lo(0, (0,))
                first_low_parts(n // 2, "query" if n % 2 else "in")
                in_lo(3 * (n // 2) + (2 if n % 2 else 0), range(4) if n else (1, 2, 3))

            def in_lo(n, banks):
                for b in banks:
                    dve.wait_ge(S("in_hi"), 4 * n + b + 1)
                    V.tensor_tensor(hnT_split[:, 1, 2 * b:2 * b + 2], hnT[:, 2 * b:2 * b + 2],
                                    hnT_split[:, 0, 2 * b:2 * b + 2].bitcast(f32), ALU.subtract
                                    ).then_inc(S("in_lo"), 1)

            def low_part(L, which, b, k):
                st, _, place, _, _ = DENSE[L, which][b]
                dve.wait_ge(S("ws_hi"), st + k + 1)
                V.tensor_tensor(wbuf(st + k, 1), ar(place + k * 512, 512), wbuf(st + k, 0).bitcast(f32),
                                ALU.subtract).then_inc(S("ws_lo"), 1)

            def first_low_parts(L, which):
                for k in range(WS):
                    low_part(L, which, 0, k)

            def dense(L, which, beside={}):
                blocks = DENSE[L, which]

                def add_output(b):
                    st, un = blocks[b][0], blocks[b][1]
                    dve.wait_ge(S("ws_used"), st + KD)
                    for m in range(NT):
                        hs = h[:, m, b * 512:(b + 1) * 512]
                        V.tensor_tensor(hs, hs, bank(4 + (un + m) % 4), ALU.add).then_inc(S("unit_evicted"), 1)

                for b, (st, un, place, loaded, _) in enumerate(blocks):
                    for k in range(KD):
                        if b or k >= WS:
                            low_part(L, which, b, k)
                        if k == 2 and b and which == "out":
                            add_output(b - 1)
                        if (b, k) in beside:
                            beside[b, k]()
                if which == "out":
                    add_output(len(blocks) - 1)
                    dve.wait_ge(S("unit_evicted"), last_unit(L, "out"))

            def chunked(ap):
                return ap.rearrange("p (g c) -> p g c", c=GCH)

            def gla_z():
                dve.wait_ge(S("gate_done"), 1)
                dve.wait_ge(S("gains_ready"), 1)
                for hh in range(GH):
                    last = V.tensor_scalar(g_z[:, hh * SEQ:(hh + 1) * SEQ], bank_all[:, hh * SEQ:(hh + 1) * SEQ],
                                           gains[:, G_BG + hh:G_BG + hh + 1], None, ALU.add)
                last.then_inc(S("z_ready"), 1)

            def gla_ones():
                dve.wait_ge(S("const"), 4)
                link(V.memset(g_ones, 1.0))
                link(V.memset(chunked(g_ones)[:, :, 0], 0.0))

            def gla_scan():
                dve.wait_ge(S("z_ready"), 1)
                dve.wait_ge(S("ln_ready"), 1)
                link(V.scalar_tensor_tensor(out=g_z, in0=g_z, scalar=0.0, in1=g_t, op0=ALU.min, op1=ALU.subtract))
                link(V.tensor_tensor_scan(g_cum, g_ones, g_z, 0.0, ALU.mult, ALU.add))

            def gla_arguments():
                c = chunked(g_cum)
                V.tensor_tensor(chunked(g_x), c, c[:, :, GCH // 2 - 1:GCH // 2].broadcast_to([P, GH * NCH, GCH]),
                                ALU.subtract).then_inc(S("x1_ready"), 1)
                V.tensor_tensor(chunked(g_t), c[:, :, GCH - 1:GCH].broadcast_to([P, GH * NCH, GCH]), c,
                                ALU.subtract).then_inc(S("x2_ready"), 1)

            def gla_q_k():
                dve.wait_ge(S("unit_evicted"), DENSE[0, "in"][1][1] + 2)
                dve.wait_ge(S("exps_ready"), 2)
                V.tensor_tensor(ar(A_E1, 1024), ar(A_E1, 1024), ar(A_Q, 1024), ALU.mult)
                V.tensor_tensor(g_e2, g_e2, ar(A_K, 1024), ALU.mult)

            def gla_decayed():
                dve.wait_ge(S("exps_ready"), 5)
                V.tensor_tensor(g_e3, g_e3, ar(A_Q, 1024), ALU.mult)
                V.tensor_tensor(g_e4, g_e4, ar(A_K, 1024), ALU.mult).then_inc(S("klT_ready"), 1)

            def gla_causal():
                dve.wait_ge(S("aT_done"), 1)
                for j in range(NT * GH):
                    last = V.copy_predicated(ar(A_AT + j * P, P), causalT[:].bitcast(i32),
                                             bank_all[:, j * P:(j + 1) * P])
                last.then_inc(S("aT_ready"), 1)

            def gla_states():
                dve.wait_ge(S("kv_done"), 1)
                link(V.tensor_copy(ar(A_ST, 1024), bank(KV_BANKS[0], 2)))
                for n in (1, 2):
                    for hh in range(GH):
                        last = V.scalar_tensor_tensor(
                            out=ar(A_ST + (n * GH + hh) * GDV, GDV), in0=ar(A_ST + ((n - 1) * GH + hh) * GDV, GDV),
                            scalar=stat[:, ST_DEC + hh * NCH + n:ST_DEC + hh * NCH + n + 1],
                            in1=bank_all[:, KV_BANKS[n] * BANK + hh * GDV:KV_BANKS[n] * BANK + (hh + 1) * GDV],
                            op0=ALU.mult, op1=ALU.add)
                    if n == 1:
                        link(last)
                last.then_inc(S("states_ready"), 1)

            def gla():
                dve.wait_ge(S("o_squares"), 1)
                rsqrt(ST_SS, ST_V, ST_Y, ST_T, NT * GH, GDV, 2)
                dve.wait_ge(S("unit_evicted"), last_unit(0, "in"))
                for j in range(NT * GH):
                    last = V.scalar_tensor_tensor(
                        out=ar(A_R + j * GDV, GDV), in0=bank_all[:, 4 * BANK + j * GDV:4 * BANK + (j + 1) * GDV],
                        scalar=stat[:, ST_Y + j:ST_Y + j + 1], in1=ar(A_R + j * GDV, GDV),
                        op0=ALU.mult, op1=ALU.mult)
                    if j % GH == GH - 1:
                        last.then_inc(S("o_ready"), 1)

            inv = [float(np.float32(THETA) ** np.float32(-i / ROPE)) for i in range(0, ROPE, 2)]
            two_pi = 2 * math.pi
            c1 = 6.28125
            c2 = float(np.float32(np.round((two_pi - c1) * 2 ** 20) / 2 ** 20))
            c3 = float(np.float32(two_pi - c1 - c2))
            magic = 1.5 * 2 ** 23
            posf, ang, kk = A_RT + 64, A_RT + 128, A_RT + 192
            lam_init = 0.8 - 0.6 * math.exp(-0.3)

            def angles():
                dve.wait_ge(S("pos_loaded"), 16)
                link(V.tensor_copy(ar(posf, NT), pos_i[:]))
                for m in range(NT):
                    for i, f in enumerate(inv):
                        last = V.tensor_scalar(ar(ang + m * 8 + i, 1), ar(posf + m, 1), f, None, ALU.mult)
                link(last)

            def reduced(s):
                r, k = ar(A_RT + 16 * s, 16), ar(kk + 16 * s, 16)
                link(V.tensor_scalar(k, ar(ang, 16), 1 / two_pi, 0.25 * s, ALU.mult, ALU.add))
                link(V.tensor_scalar(k, k, magic, None, ALU.add))
                link(V.tensor_scalar(k, k, magic, None, ALU.subtract))
                link(V.scalar_tensor_tensor(out=r, in0=k, scalar=-c1, in1=ar(ang, 16), op0=ALU.mult, op1=ALU.add))
                link(V.scalar_tensor_tensor(out=r, in0=k, scalar=-c2, in1=r, op0=ALU.mult, op1=ALU.add))
                link(V.scalar_tensor_tensor(out=r, in0=k, scalar=-c3, in1=r, op0=ALU.mult, op1=ALU.add))
                link(V.tensor_scalar(r, r, math.pi / 2 * s, 3.1415925, ALU.add, ALU.min))
                link(V.tensor_scalar(r, r, -3.1415925, None, ALU.max))
                if s:
                    V.memset(ar(A_RT + 32, 32), 0.0).then_inc(S("angles_ready"), 1)

            def lam_dots():
                dve.wait_ge(S("lam_loaded"), 64)
                for s in range(2):
                    link(V.tensor_tensor_reduce(out=ar(A_RT + 512, DDH), in0=ar(A_RT + 256 + 128 * s, DDH),
                                                in1=ar(A_RT + 320 + 128 * s, DDH), scale=1.0, scalar=0.0,
                                                op0=ALU.mult, op1=ALU.add, accum_out=stat[:, 48 + s:49 + s]))
                V.memset(stat[:, 60:61], 0.0).then_inc(S("lam_dots"), 1)

            def minus_lambda():
                dve.wait_ge(S("lam_exps"), 1)
                link(V.tensor_tensor(stat[:, 61:62], stat[:, 50:51], stat[:, 51:52], ALU.subtract))
                link(V.tensor_scalar(stat[:, 61:62], stat[:, 61:62], lam_init, -1.0, ALU.add, ALU.mult))

            def rope(s, m):
                if m == 0:
                    dve.wait_ge(S("sincos_ready"), 1)
                    dve.wait_ge(S("unit_evicted"), DENSE[1, "in"][2 * s + 1][1] + 2)
                v = ar((A_DQ, A_DK)[s] + m * D, D).rearrange("p (g d) -> p g d", d=DDH)
                x1, x2 = v[:, :, 0:8], v[:, :, 8:16]

                def cs(s):
                    return ar(A_RT + 16 * s + 8 * m, 8).rearrange("p (a d) -> p a d", a=1).broadcast_to([P, 16, 8])

                t = [ar(A_RT + 1024 + 128 * j, 128).rearrange("p (g d) -> p g d", d=8) for j in range(4)]
                V.tensor_tensor(t[0], x1, cs(1), ALU.mult)
                V.tensor_tensor(t[1], x2, cs(0), ALU.mult)
                V.tensor_tensor(t[2], x2, cs(1), ALU.mult)
                link(V.tensor_tensor(t[3], x1, cs(0), ALU.mult))
                V.tensor_tensor(x1, t[0], t[1], ALU.subtract)
                link(V.tensor_tensor(x2, t[2], t[3], ALU.add))
                if m == NT - 1:
                    V.memset(ar(kk, 1), 0.0).then_inc(S("rope_ready"), 1)

            def diff():
                def mask_and_max(n):
                    m, bf = n % NT, n % 2
                    w = (m + 1) * P
                    s2 = ar(A_S + bf * 512, 512).rearrange("p (a k) -> p a k", a=2)
                    p2 = bank(0, 2).rearrange("p (a k) -> p a k", a=2)
                    dve.wait_ge(S("s_done"), n + 1)
                    if n >= 2:
                        dve.wait_ge(S("exp_ready"), n - 1)
                    if m:
                        V.tensor_copy(s2[:, :, 0:P], p2[:, :, 0:P])
                    mask = causal_add[:].rearrange("p (a k) -> p a k", a=1).broadcast_to([P, 2, P])
                    V.tensor_tensor(s2[:, :, m * P:w], p2[:, :, m * P:w], mask, ALU.add
                                    ).then_inc(S("s_evicted"), 1)
                    dve.wait_ge(S("s_evicted"), n + 1)
                    V.tensor_reduce(stat[:, 52 + 2 * bf:54 + 2 * bf], s2[:, :, 0:w], AX.X, ALU.max, negate=True
                                    ).then_inc(S("max_ready"), 1)

                mask_and_max(0)
                for n in range(DH * NT):
                    bf, w = n % 2, (n % NT + 1) * P
                    if n + 1 < DH * NT:
                        mask_and_max(n + 1)
                    dve.wait_ge(S("exp_ready"), n + 1)
                    if n:
                        dve.wait_ge(S("attn_ready"), n)
                    link(V.reciprocal(stat[:, 62:64], stat[:, 56 + 2 * bf:58 + 2 * bf]))
                    link(V.tensor_tensor(stat[:, 63:64], stat[:, 63:64], stat[:, 61:62], ALU.mult))
                    pr = A_P + bf * 512
                    link(V.tensor_scalar(ar(pr + 256, w), ar(pr + 256, w), stat[:, 63:64], None, ALU.mult))
                    if n >= 2:
                        dve.wait_ge(S("attn_transposed"), n - 1)
                    V.scalar_tensor_tensor(out=ar(A_ATT + bf * 256, w), in0=ar(pr, w), scalar=stat[:, 62:63],
                                           in1=ar(pr + 256, w), op0=ALU.mult, op1=ALU.add
                                           ).then_inc(S("attn_ready"), 1)
                dve.wait_ge(S("o_squares"), 2)
                rsqrt(0, 16, 32, 48, NT * DH, DDV, 5)
                for m in range(NT):
                    for hh in range(DH):
                        j = m * DH + hh
                        last = V.tensor_scalar(ar(A_O + j * DDV, DDV),
                                               bank_all[:, 4 * BANK + j * DDV:4 * BANK + (j + 1) * DDV],
                                               stat[:, 32 + j:33 + j], 1.0 - lam_init, ALU.mult, ALU.mult)
                    last.then_inc(S("o_ready"), 1)

            def mixer_out(L):
                first_low_parts(L, "out")
                in_lo(3 * L + 1, range(4))
                dense(L, "out")

            def lo(c0, u, b):
                dve.wait_ge(S("u_hi"), c0 + (b + u + 1))
                V.tensor_tensor(split[:, u % 2, 1, :], bank(2 * (u % 2), 2),
                                split[:, u % 2, 0, :].bitcast(f32), ALU.subtract).then_inc(S("u_lo"), 1)

            def u_blocks(L, c0, u):
                b, f = L * NCHUNK, u % U4
                dve.wait_ge(S(f"raw_blocks_loaded{f}"),
                            4 * QA * c0 + 16 * QA * (u // U4 + L * by_dve(f) - first_dve[f] + 1))
                dve.wait_ge(S("u_transposed"), c0 + (b + u))
                dve.wait_ge(S("u_hi"), c0 + (b + u - 1))
                dve.wait_ge(S("u_lo"), c0 + (b + u - 1))
                V.transpose(bank(2 * (u % 2), 2).rearrange("p (k e j) -> p e k j", e=QA, j=QI),
                            raw[:, f, :].rearrange("p (e i k) -> p e k i", e=QA, i=QI)
                            ).then_inc(S("u_transposed"), 1)

            def peer_search(L):
                b = L * NCHUNK
                n_set, n_all = NT * HP, NT * SLOTS
                c = 0

                def next_chunk():
                    nonlocal c
                    if (c + 1) // U4 >= first_dve[(c + 1) % U4]:
                        u_blocks(L, (c + 1) // U4 * U4, (c + 1) % U4)
                    lo(c, 0, b) if c % 2 == 0 else lo(c - 1, 1, b)
                    c += 1

                def ordered():
                    dve.wait_ge(S("search_step"), steps)

                steps = L * SEARCH_STEPS

                def step(ins):
                    nonlocal steps
                    steps += 1
                    ins.then_inc(S("search_step"), 1)

                def two_rounds(n, width, src, top, idx, per_chunk):
                    ops = 0
                    for r in range(2):
                        for kind in range(3 if r == 0 else 2):
                            for j in range(n):
                                if kind == 0:
                                    last = V.max(top(j, r), src(j))
                                elif kind == 1:
                                    last = V.max_index(idx(j, r), top(j, r), src(j))
                                else:
                                    last = V.match_replace(src(j), top(j, r), src(j), NEG)
                                if j == n - 1:
                                    step(last)
                                ops += 1
                                if ops % per_chunk == 0:
                                    next_chunk()
                            ordered()

                next_chunk()
                dve.wait_ge(S("unit_evicted"), last_unit(L, "query") + 8)
                two_rounds(n_set, NK, lambda j: ar(A_SC + j * NK, NK),
                           lambda j, r: ar(A_TS + j * TOPK + 8 * r, 8),
                           lambda j, r: ar(A_TI + j * TOPK + 8 * r, 8).bitcast(u32), 8)
                step(V.tensor_copy(ar(A_TIF, n_set * TOPK), ar(A_TI, n_set * TOPK).bitcast(u32)))

                def tops(off, m, half):
                    return ar(off + m * HP * TOPK, HP * TOPK).rearrange("p (h q k) -> p h q k", h=PH, q=2)[:, :, half, :]

                for m in range(NT):
                    x1 = tops(A_TS, m, 0).unsqueeze(3).broadcast_to([P, PH, TOPK, TOPK])
                    x2 = tops(A_TS, m, 1).unsqueeze(2).broadcast_to([P, PH, TOPK, TOPK])
                    step(V.tensor_tensor(ar(A_CAND + m * 2048, 2048).rearrange("p (h a b) -> p h a b", h=PH, a=TOPK),
                                         x1, x2, ALU.add))
                    next_chunk()
                ordered()
                two_rounds(NT * PH, 256, lambda j: ar(A_CAND + j * 256, 256),
                           lambda j, r: ar(A_BS + j * TOPK + 8 * r, 8),
                           lambda j, r: ar(A_BP + j * TOPK + 8 * r, 8).bitcast(u32), 6)
                b3 = ar(A_BS, n_all).rearrange("p (g k) -> p g k", k=TOPK)
                g3 = ar(A_GG, n_all).rearrange("p (g k) -> p g k", k=TOPK)
                V.tensor_tensor(g3, b3, b3[:, :, 0:1].broadcast_to([P, NT * PH, TOPK]), ALU.subtract
                                ).then_inc(S("gate_args"), 1)
                pu = ar(A_BP, n_all).bitcast(u32)
                V.tensor_scalar(ar(A_PA, n_all).bitcast(u32), pu, 4, None, ALU.logical_shift_right)
                step(V.tensor_scalar(ar(A_PA + n_all, n_all).bitcast(u32), pu, 15, None, ALU.bitwise_and))
                next_chunk()
                ordered()
                step(V.tensor_copy(ar(A_PAF, 2 * n_all), ar(A_PA, 2 * n_all).bitcast(u32)))
                for half in range(2):
                    for kind in range(3):
                        for m in range(NT):
                            e = ar(A_EQ + m * 2048, 2048)
                            e3 = e.rearrange("p (s k) -> p s k", k=TOPK)
                            e4 = e.rearrange("p (h s k) -> p h s k", h=PH, s=TOPK)
                            if m == 0:
                                ordered()
                            if kind == 0:
                                place = ar(A_PAF + half * n_all + m * SLOTS, SLOTS).unsqueeze(2)
                                step(V.tensor_tensor(e3, place.broadcast_to([P, SLOTS, TOPK]),
                                                     iota[:].unsqueeze(1).broadcast_to([P, SLOTS, TOPK]),
                                                     ALU.is_equal))
                            elif kind == 1:
                                listed = tops(A_TIF, m, half).unsqueeze(2).broadcast_to([P, PH, TOPK, TOPK])
                                step(V.tensor_tensor(e4, e4, listed, ALU.mult))
                            else:
                                step(V.tensor_reduce(ar(A_IJ + half * n_all + m * SLOTS, SLOTS), e3, AX.X, ALU.add))
                            next_chunk()
                dve.wait_ge(S("gate_exps"), L + 1)
                step(V.tensor_reduce(ar(A_SM, NT * PH), g3, AX.X, ALU.add))
                next_chunk()
                ordered()
                step(V.reciprocal(ar(A_SM + 16, NT * PH), ar(A_SM, NT * PH)))
                ordered()
                V.tensor_tensor(g3, g3, ar(A_SM + 16, NT * PH).unsqueeze(2).broadcast_to([P, NT * PH, TOPK]), ALU.mult
                                ).then_inc(S("chosen"), 1)
                assert steps == (L + 1) * SEARCH_STEPS, steps
                while c < HALF - U4 + 1:
                    next_chunk()
                dve.wait_ge(S("slots_transposed"), L + 1)
                V.tensor_copy(slotT[:, 0:2, :].rearrange("p a t -> p (a t)"), bank(6))
                rest = ar(A_EQ, SEQ)
                link(V.tensor_copy(slotT[:, 2, :], bank(7)[:, 0:SEQ]))
                link(V.tensor_tensor(rest, bank(7)[:, 0:SEQ], slotT[:, 2, :], ALU.subtract))
                next_chunk()
                link(V.tensor_copy(slotT[:, 3, :], rest))
                link(V.tensor_tensor(rest, rest, slotT[:, 3, :], ALU.subtract))
                link(V.tensor_copy(slotT[:, 4, :], rest))
                next_chunk()
                next_chunk()
                build(L, 0, 0, 0)
                while c < HALF + 1:
                    next_chunk()

            def build(L, half, p0, r, parts=(0, 1)):
                b = (2 * L + half) * NGRP
                rb = r % 2
                t0 = TG * p0 + TG * r

                def of(row, n):
                    return slotT[:, row, bass.ds(t0, TG)].unsqueeze(1).broadcast_to([P, n, TG])

                if 0 in parts:
                    if not isinstance(p0, int) or b + p0 + r > 0:
                        dve.wait_ge(S("onehots_ready"), p0 + (b + r))
                    V.tensor_tensor(onehot_i, iota_tok[:, half * HALF:(half + 1) * HALF, :], of(0, HALF),
                                    ALU.is_equal).then_inc(S("onehot_i_ready"), 1)
                if 1 not in parts:
                    return
                if not isinstance(p0, int) or b + p0 + r - 1 > 0:
                    dve.wait_ge(S("gates_done"), p0 + (b + r - 1))
                V.tensor_tensor(onehot_j[:, rb], iota_tok[:], of(1, NK), ALU.is_equal)
                dve.wait_ge(S("onehot_i_ready"), p0 + (b + r + 1))
                parts = slotT[:, 2:5, bass.ds(t0, TG)].unsqueeze(2).broadcast_to([P, 3, HALF, TG])
                V.tensor_tensor(onehot_g[:, rb], onehot_i.unsqueeze(1).broadcast_to([P, 3, HALF, TG]), parts,
                                ALU.mult).then_inc(S("onehots_ready"), 1)

            def multiply(L, half, p0, r):
                b = (2 * L + half) * NGRP
                dve.wait_ge(S("gates_done"), p0 + (b + r + 1))
                w = W[:, half * HALF:(half + 1) * HALF, bass.ds(p0 * TG + TG * r, TG)]
                V.tensor_tensor(w, w, bank(6 + r % 2).rearrange("p (k i) -> p i k", k=TG), ALU.mult
                                ).then_inc(S("w_multiplied"), 1)

            def peer_up_second(L):
                b = L * NCHUNK
                dve.wait_ge(S("gelu_done"), b + HALF)

                def pairs(c0, p0, first_group, last_group):
                    for r in range(2):
                        if r == 0:
                            u_blocks(L, c0, 2)
                        lo(c0, 2 * r + 1, b)
                        if not (first_group and r == 0):
                            multiply(L, 0, p0, r - 1)
                        if not (last_group and r == 1):
                            build(L, 0, p0, r + 1, (0,))
                            u_blocks(L, c0, 5 if r else 3)
                            lo(c0, 2 * r + 2, b)
                            build(L, 0, p0, r + 1, (1,))

                pairs(HALF, 0, True, False)
                n_loop = (NCHUNK - HALF) // U4 // 2 - 1
                with dve.Fori(0, n_loop) as g0:
                    for g in (1, 2):
                        pairs(g0 * (2 * U4) + (HALF + g * U4), g0 * 4 + 2 * g, False, False)
                pairs(NCHUNK - U4, NGRP - 2, False, True)
                multiply(L, 0, NGRP - 2, 1)

            def peer_down(L):
                b = L * NCHUNK
                build(L, 1, 0, 0)

                def split_v(c0, u):
                    dve.wait_ge(S("w_hi"), c0 + (b + u + 1))
                    V.tensor_tensor(wsplit[:, u % 2, 1, :], W[:, c0 + u, :],
                                    wsplit[:, u % 2, 0, :].bitcast(f32), ALU.subtract).then_inc(S("w_lo"), 1)
                    for f in range(2):
                        dve.wait_ge(S("v_hi"), 2 * c0 + (2 * (b + u) + 1 + f))
                        V.tensor_tensor(split[:, u % 2, 1, f * 512:(f + 1) * 512], raw[:, u, f * 512:(f + 1) * 512],
                                        split[:, u % 2, 0, f * 512:(f + 1) * 512].bitcast(f32), ALU.subtract
                                        ).then_inc(S("v_lo"), 1)

                split_v(0, 0)
                dve.wait_ge(S("gelu_done"), b + NCHUNK)

                def pairs(c0, p0, last_group):
                    for r in range(2):
                        split_v(c0, 2 * r + 1)
                        if not (last_group and r == 1):
                            build(L, 1, p0, r + 1)
                            split_v(c0 + U4 if r else c0, 0 if r else 2)
                        multiply(L, 1, p0, r)

                with dve.Fori(0, NGRP // 2 - 1) as g0:
                    pairs(g0 * U4, g0 * 2, False)
                pairs(HALF - U4, NGRP - 2, True)
                with dve.Fori(HALF // U4, NCHUNK // U4) as g0:
                    for u in range(U4):
                        split_v(g0 * U4, u)
                dve.wait_ge(S("ff_transposed"), 2 * L + 1)
                for half in range(2):
                    for m in range(NT):
                        if half and m == 0:
                            dve.wait_ge(S("ff_transposed"), 2 * L + 2)
                        hs = h[:, m, half * 512:(half + 1) * 512]
                        V.tensor_tensor(hs, hs, bank(4 + 2 * m + half), ALU.add).then_inc(S("h_updated"), 1)
                dve.wait_ge(S("h_updated"), 4 * (L + 1))

            for L in range(2):
                norm(2 * L)
                if L == 0:
                    dense(L, "in", {(0, 5): gla_ones, (1, 1): gla_z, (2, 1): gla_scan, (2, 3): gla_arguments,
                                    (3, 2): gla_q_k, (3, 5): gla_decayed,
                                    (4, 0): lambda: link(V.memset(ar(A_AT, 1024), 0.0)),
                                    (4, 6): gla_causal, (5, 6): gla_states})
                    gla()
                else:
                    dense(L, "in", {(1, 1): angles, (1, 4): lambda: reduced(0), (1, 7): lambda: reduced(1),
                                    (2, 2): lam_dots, (3, 1): minus_lambda,
                                    (3, 3): lambda: rope(0, 0), (3, 6): lambda: rope(0, 1),
                                    (4, 4): lambda: rope(1, 0), (4, 7): lambda: rope(1, 1)})
                    diff()
                mixer_out(L)
                norm(2 * L + 1)
                dense(L, "query")
                peer_search(L)
                peer_up_second(L)
                peer_down(L)
            norm(4)
            dve.wait_ge(S("gfinal_loaded"), 16)
            for m in range(NT):
                V.scalar_tensor_tensor(out=ar(A_HX + m * D, D), in0=h[:, m, :],
                                       scalar=stat[:, ST_Y + m:ST_Y + m + 1], in1=raw[:, 0, :],
                                       op0=ALU.mult, op1=ALU.mult).then_inc(S("out_ready"), 1)


_INS = ["x", "positions", "norm_mix", "norm_ffn", "norm_final",
        "gla_w_in", "gla_w_gate_up", "gla_b_gate", "gla_norm", "gla_w_out",
        "diff_w_in", "diff_lambda_q1", "diff_lambda_k1", "diff_lambda_q2", "diff_lambda_k2",
        "diff_norm", "diff_w_out", "peer_w_query", "peer_sub_keys", "peer_u", "peer_v"]
_OUTS = [((1, SEQ, D), "float32")]


def kernel(**inputs):
    import numpy as _np
    import concourse.bacc as _bacc
    from concourse import mybir as _mybir
    from concourse.bass_utils import run_bass_kernel_spmd as _run

    nc = _bacc.Bacc("TRN2", target_bir_lowering=False, num_devices=1)
    arrays, args = {}, []
    for name in _INS:
        a = _np.ascontiguousarray(inputs[name])
        arrays[f"in_{name}_dram"] = a
        args.append(nc.dram_tensor(f"in_{name}_dram", a.shape, _mybir.dt.from_np(a.dtype), kind="ExternalInput").ap())
    for i, (shape, dtype) in enumerate(_OUTS):
        dt = _mybir.dt.from_np(_np.dtype(dtype))
        args.append(nc.dram_tensor(f"out_{i}_dram", shape, dt, kind="ExternalOutput").ap())
    trunk_kernel(nc, *args)
    r = _run(nc, [arrays], core_ids=[0])
    return r.results[0]["out_0_dram"]
```
